# Optimizing a Trainium2 kernel written in Bass

```python
import math
import jax, jax.numpy as jnp
from jax import lax
import numpy as np
import jax
import jax.numpy as jnp

D_MODEL = 1024
BATCH = 1
SEQ = 256
DEPTH = 2

GRID_W = 64
N_EVEN = (DEPTH + 1) // 2
N_ODD = DEPTH // 2
D_FF = 4 * D_MODEL
NORM_EPS = 1e-6

SSD_HEAD_DIM = 64
SSD_WIDTH = D_MODEL
SSD_HEADS = SSD_WIDTH // SSD_HEAD_DIM
SSD_GROUPS = 2
SSD_STATE = 128
SSD_CONV = 5
SSD_CHUNK = 128
SSD_CONV_CH = SSD_WIDTH + 2 * SSD_GROUPS * SSD_STATE

NA_HEAD_DIM = 64
NA_WIDTH = D_MODEL
NA_HEADS = NA_WIDTH // NA_HEAD_DIM
NA_KH_MAX = 8
NA_KW = 16

AB_IN = SSD_WIDTH + SSD_CONV_CH + 2 * SSD_HEADS + 3 * NA_WIDTH
AB_MIX = SSD_WIDTH + NA_WIDTH

ML_HEADS = 8
ML_DV = 2 * D_MODEL // ML_HEADS
ML_DK = ML_DV // 2
ML_CHUNK = 128
ML_WIDTH = ML_HEADS * ML_DV
ML_QK = ML_HEADS * ML_DK
ML_IN = 2 * ML_QK + 2 * ML_WIDTH + 4 * ML_HEADS


def rmsnorm(x, g):
    xf = x.astype(jnp.float32)
    y = xf * lax.rsqrt(jnp.mean(xf * xf, axis=-1, keepdims=True) + NORM_EPS)
    return (y * g.astype(jnp.float32)).astype(x.dtype)

def modulate(h, shift, scale):
    return h * (1 + scale[:, None, :]) + shift[:, None, :]

def centred_dwconv(u, w, b):
    pad = w.shape[0] // 2
    out = lax.conv_general_dilated(u, w[:, None, :].astype(u.dtype), window_strides=(1,),
                                   padding=[(pad, pad)], dimension_numbers=('NWC', 'WIO', 'NWC'),
                                   feature_group_count=u.shape[-1])
    return out + b

def segsum(a):
    T = a.shape[-1]
    cs = jnp.cumsum(a, axis=-1)
    diff = cs[..., :, None] - cs[..., None, :]
    mask = jnp.tril(jnp.ones((T, T), dtype=bool))
    return jnp.where(mask, diff, -jnp.inf)

def ssd_scan(xh, dt, a, bm, cm):
    Bsz, L, H, P = xh.shape
    G, N = bm.shape[-2:]
    R = H // G
    T = SSD_CHUNK
    nc = L // T
    X = (xh * dt[..., None]).reshape(Bsz, nc, T, G, R, P)
    adt = (dt * a).reshape(Bsz, nc, T, G, R).transpose(0, 3, 4, 1, 2)
    Bc = bm.reshape(Bsz, nc, T, G, N)
    Cc = cm.reshape(Bsz, nc, T, G, N)
    a_cs = jnp.cumsum(adt, axis=-1)
    Lmat = jnp.exp(segsum(adt))
    cb = jnp.einsum('bctgn,bcsgn->bgcts', Cc, Bc)
    y_diag = jnp.einsum('bgrcts,bcsgrp->bctgrp', cb[:, :, None] * Lmat, X)
    decay_states = jnp.exp(a_cs[..., -1:] - a_cs)
    states = jnp.einsum('bctgn,bgrct,bctgrp->bcgrpn', Bc, decay_states, X)
    states = jnp.concatenate([jnp.zeros_like(states[:, :1]), states], axis=1)
    chunk_decay = jnp.exp(segsum(jnp.pad(a_cs[..., -1], ((0, 0), (0, 0), (0, 0), (1, 0)))))
    new_states = jnp.einsum('bgrzc,bcgrpn->bzgrpn', chunk_decay, states)
    states = new_states[:, :-1]
    y_off = jnp.einsum('bctgn,bcgrpn,bgrct->bctgrp', Cc, states, jnp.exp(a_cs))
    return (y_diag + y_off).reshape(Bsz, L, H, P)

def ssd_branch(z, xbc, dt_raw, conv_w, conv_b, dt_bias, a_log, d_skip, norm_g):
    f32 = jnp.float32
    xbc = jax.nn.silu(centred_dwconv(xbc, conv_w, conv_b)).astype(f32)
    xs, bm, cm = jnp.split(xbc, [SSD_WIDTH, SSD_WIDTH + SSD_GROUPS * SSD_STATE], axis=-1)
    Bsz, L, _ = xs.shape
    xh = xs.reshape(Bsz, L, SSD_HEADS, SSD_HEAD_DIM)
    bm = bm.reshape(Bsz, L, SSD_GROUPS, SSD_STATE)
    cm = cm.reshape(Bsz, L, SSD_GROUPS, SSD_STATE)
    dt = jax.nn.softplus(dt_raw.astype(f32).reshape(Bsz, L, 2, SSD_HEADS) + dt_bias.astype(f32))
    a = -jnp.exp(a_log.astype(f32))
    y_f = ssd_scan(xh, dt[:, :, 0], a[0], bm, cm)
    fl = lambda t: jnp.flip(t, axis=1)
    y_b = fl(ssd_scan(fl(xh), fl(dt[:, :, 1]), a[1], fl(bm), fl(cm)))
    y = y_f + y_b + d_skip.astype(f32)[:, None] * xh
    y = y.reshape(Bsz, L, SSD_WIDTH)
    return rmsnorm(y * jax.nn.silu(z.astype(f32)), norm_g)

def na_branch(qkv, rpb):
    Bsz, L, _ = qkv.shape
    rows = L // GRID_W
    kh = min(NA_KH_MAX, rows)
    q, k, v = jnp.split(qkv.astype(jnp.float32), 3, axis=-1)
    grid = lambda t: t.reshape(Bsz, rows, GRID_W, NA_HEADS, NA_HEAD_DIM)
    q = grid(q) * (NA_HEAD_DIM ** -0.5)
    k = grid(k)
    v = grid(v)
    r_idx = np.arange(rows)
    row_start = np.clip(r_idx - kh // 2, 0, rows - kh)
    c_idx = np.arange(GRID_W)
    col_start = np.clip(c_idx - NA_KW // 2, 0, GRID_W - NA_KW)
    col_keys = col_start[:, None] + np.arange(NA_KW)[None, :]
    row_off = row_start[:, None] + np.arange(kh)[None, :] - r_idx[:, None] + NA_KH_MAX - 1
    col_off = col_keys - c_idx[:, None] + NA_KW - 1
    rpb = rpb.astype(jnp.float32)

    def one_row(args):
        q_r, rs, ro = args
        k_band = lax.dynamic_slice_in_dim(k, rs, kh, axis=1)
        v_band = lax.dynamic_slice_in_dim(v, rs, kh, axis=1)
        k_win = jnp.take(k_band, col_keys, axis=2)
        v_win = jnp.take(v_band, col_keys, axis=2)
        bias = rpb[:, ro[:, None, None], col_off[None, :, :]]
        s = jnp.einsum('bwhd,biwjhd->bhwij', q_r, k_win) + bias.transpose(0, 2, 1, 3)[None]
        p = jax.nn.softmax(s.reshape(Bsz, NA_HEADS, GRID_W, kh * NA_KW), axis=-1).reshape(s.shape)
        return jnp.einsum('bhwij,biwjhd->bwhd', p, v_win)

    out = lax.map(one_row, (q.transpose(1, 0, 2, 3, 4),
                            jnp.asarray(row_start, jnp.int32), jnp.asarray(row_off, jnp.int32)))
    return out.transpose(1, 0, 2, 3, 4).reshape(Bsz, L, NA_WIDTH)

def mlstm_chunkwise(q, k, v, i_pre, f_pre):
    Bsz, H, L, DK = q.shape
    DV = v.shape[-1]
    T = ML_CHUNK
    nc = L // T
    q = q.reshape(Bsz, H, nc, T, DK)
    k = k.reshape(Bsz, H, nc, T, DK)
    v = v.reshape(Bsz, H, nc, T, DV)
    ig = i_pre.reshape(Bsz, H, nc, T)
    b = jnp.cumsum(jax.nn.log_sigmoid(f_pre).reshape(Bsz, H, nc, T), axis=-1)
    g = b[..., -1]
    a = g[..., None] - b + ig
    m_loc = jnp.max(a, axis=-1)
    w = jnp.exp(a - m_loc[..., None])
    S_loc = jnp.einsum('bhct,bhctk,bhctv->bhckv', w, k, v)
    n_loc = jnp.einsum('bhct,bhctk->bhck', w, k)

    def step(carry, inp):
        C, n, m = carry
        S_c, n_c, m_c, g_c = inp
        m_new = jnp.maximum(g_c + m, m_c)
        s_old = jnp.exp(g_c + m - m_new)
        s_new = jnp.exp(m_c - m_new)
        C_new = s_old[..., None, None] * C + s_new[..., None, None] * S_c
        n_new = s_old[..., None] * n + s_new[..., None] * n_c
        return (C_new, n_new, m_new), (C, n, m)

    init = (jnp.zeros((Bsz, H, DK, DV), jnp.float32), jnp.zeros((Bsz, H, DK), jnp.float32),
            jnp.zeros((Bsz, H), jnp.float32))
    mv = lambda t: jnp.moveaxis(t, 2, 0)
    _, (C_prev, n_prev, m_prev) = lax.scan(step, init, (mv(S_loc), mv(n_loc), mv(m_loc), mv(g)))
    C_prev = jnp.moveaxis(C_prev, 0, 2)
    n_prev = jnp.moveaxis(n_prev, 0, 2)
    m_prev = jnp.moveaxis(m_prev, 0, 2)
    mask = jnp.tril(jnp.ones((T, T), dtype=bool))
    Dm = jnp.where(mask, b[..., :, None] - b[..., None, :] + ig[..., None, :], -jnp.inf)
    m_inter = b + m_prev[..., None]
    m_t = jnp.maximum(m_inter, jnp.max(Dm, axis=-1))
    sc = jnp.einsum('bhctk,bhcsk->bhcts', q, k) * jnp.exp(Dm - m_t[..., None])
    inter_scale = jnp.exp(m_inter - m_t)
    num = jnp.einsum('bhcts,bhcsv->bhctv', sc, v) + inter_scale[..., None] * jnp.einsum('bhctk,bhckv->bhctv', q, C_prev)
    den = jnp.sum(sc, axis=-1) + inter_scale * jnp.einsum('bhctk,bhck->bhct', q, n_prev)
    h = num / jnp.maximum(jnp.abs(den), jnp.exp(-m_t))[..., None]
    return h.reshape(Bsz, H, L, DV)

def mlstm_branch(proj, gate_b, head_g):
    Bsz, L, _ = proj.shape
    q, k, v, o, gates = jnp.split(proj.astype(jnp.float32),
                                  [ML_QK, 2 * ML_QK, 2 * ML_QK + ML_WIDTH, 2 * ML_QK + 2 * ML_WIDTH], axis=-1)
    heads = lambda t, d: t.reshape(Bsz, L, ML_HEADS, d).transpose(0, 2, 1, 3)
    q = heads(q, ML_DK) * (ML_DK ** -0.5)
    k = heads(k, ML_DK)
    v = heads(v, ML_DV)
    gates = (gates.reshape(Bsz, L, 4, ML_HEADS) + gate_b.astype(jnp.float32)).transpose(0, 2, 3, 1)
    h_f = mlstm_chunkwise(q, k, v, gates[:, 0], gates[:, 1])
    fl = lambda t: jnp.flip(t, axis=2)
    h_b = fl(mlstm_chunkwise(fl(q), fl(k), fl(v), fl(gates[:, 2]), fl(gates[:, 3])))
    h = (h_f + h_b).transpose(0, 2, 1, 3)
    h = rmsnorm(h, head_g.reshape(ML_HEADS, ML_DV))
    return jax.nn.sigmoid(o) * h.reshape(Bsz, L, ML_WIDTH)

def ssd_na_mixer(h, w_in, conv_w, conv_b, dt_bias, a_log, d_skip, ssd_norm, rpb, w_out):
    proj = h @ w_in
    s1 = SSD_WIDTH
    s2 = s1 + SSD_CONV_CH
    s3 = s2 + 2 * SSD_HEADS
    z, xbc, dt_raw, qkv = jnp.split(proj, [s1, s2, s3], axis=-1)
    y_ssd = ssd_branch(z, xbc, dt_raw, conv_w, conv_b, dt_bias, a_log, d_skip, ssd_norm)
    y_na = na_branch(qkv, rpb)
    y = jnp.concatenate([y_ssd.astype(jnp.float32), y_na], axis=-1)
    return y.astype(h.dtype) @ w_out

def mlstm_mixer(h, w_in, gate_b, head_g, w_out):
    y = mlstm_branch(h @ w_in, gate_b, head_g)
    return y.astype(h.dtype) @ w_out

def first_inputs(seed: int = 0) -> dict:
    key = jax.random.key(seed)
    ks = jax.random.split(key, 20)
    nrm = lambda k, shape, s: jax.random.normal(k, shape, jnp.float32) * s
    x = nrm(ks[0], (BATCH, SEQ, D_MODEL), 1.0)
    c = nrm(ks[1], (BATCH, D_MODEL), 1.0)
    ada_w = nrm(ks[2], (DEPTH, D_MODEL, 6 * D_MODEL), 0.5 * D_MODEL ** -0.5)
    ada_b = nrm(ks[3], (DEPTH, 6 * D_MODEL), 0.02)
    norm_g = 1.0 + nrm(ks[4], (DEPTH, 4, D_MODEL), 0.02)
    mlp_w1 = nrm(ks[5], (DEPTH, D_MODEL, D_FF), D_MODEL ** -0.5)
    mlp_w2 = nrm(ks[6], (DEPTH, D_FF, D_MODEL), D_FF ** -0.5)
    ab_w_in = nrm(ks[7], (N_EVEN, D_MODEL, AB_IN), D_MODEL ** -0.5)
    ab_conv_w = nrm(ks[8], (N_EVEN, SSD_CONV, SSD_CONV_CH), SSD_CONV ** -0.5)
    ab_conv_b = nrm(ks[9], (N_EVEN, SSD_CONV_CH), 0.02)
    dt0 = jnp.exp(jax.random.uniform(ks[10], (N_EVEN, 2, SSD_HEADS), jnp.float32,
                                     minval=math.log(1e-3), maxval=math.log(1e-1)))
    ab_dt_bias = dt0 + jnp.log(-jnp.expm1(-dt0))
    ab_a_log = jnp.log(jax.random.uniform(ks[11], (N_EVEN, 2, SSD_HEADS), jnp.float32, minval=1.0, maxval=16.0))
    ab_d_skip = 1.0 + nrm(ks[12], (N_EVEN, SSD_HEADS), 0.02)
    ab_ssd_norm = 1.0 + nrm(ks[13], (N_EVEN, SSD_WIDTH), 0.02)
    ab_rpb = nrm(ks[14], (N_EVEN, NA_HEADS, 2 * NA_KH_MAX - 1, 2 * NA_KW - 1), 0.1)
    ab_w_out = nrm(ks[15], (N_EVEN, AB_MIX, D_MODEL), AB_MIX ** -0.5)
    ml_w_in = nrm(ks[16], (N_ODD, D_MODEL, ML_IN), D_MODEL ** -0.5)
    gate_base = jnp.array([0.0, 4.0, 0.0, 4.0], jnp.float32)[None, :, None]
    ml_gate_b = gate_base + nrm(ks[17], (N_ODD, 4, ML_HEADS), 0.1)
    ml_head_norm = 1.0 + nrm(ks[18], (N_ODD, ML_WIDTH), 0.02)
    ml_w_out = nrm(ks[19], (N_ODD, ML_WIDTH, D_MODEL), ML_WIDTH ** -0.5)
    return {"x": x, "c": c, "ada_w": ada_w, "ada_b": ada_b, "norm_g": norm_g,
            "mlp_w1": mlp_w1, "mlp_w2": mlp_w2,
            "ab_w_in": ab_w_in, "ab_conv_w": ab_conv_w, "ab_conv_b": ab_conv_b,
            "ab_dt_bias": ab_dt_bias, "ab_a_log": ab_a_log, "ab_d_skip": ab_d_skip,
            "ab_ssd_norm": ab_ssd_norm, "ab_rpb": ab_rpb, "ab_w_out": ab_w_out,
            "ml_w_in": ml_w_in, "ml_gate_b": ml_gate_b, "ml_head_norm": ml_head_norm, "ml_w_out": ml_w_out}

def first_block(x, c, ada_w, ada_b, norm_g, mlp_w1, mlp_w2,
              ab_w_in, ab_conv_w, ab_conv_b, ab_dt_bias, ab_a_log, ab_d_skip, ab_ssd_norm, ab_rpb, ab_w_out,
              ml_w_in, ml_gate_b, ml_head_norm, ml_w_out):
    cond = jax.nn.silu(c)
    for layer in range(DEPTH):
        mod = cond @ ada_w[layer] + ada_b[layer]
        sh1, sc1, g1, sh2, sc2, g2 = jnp.split(mod, 6, axis=-1)
        h = modulate(rmsnorm(x, norm_g[layer, 0]), sh1, sc1)
        if layer % 2 == 0:
            j = layer // 2
            mixed = ssd_na_mixer(h, ab_w_in[j], ab_conv_w[j], ab_conv_b[j], ab_dt_bias[j], ab_a_log[j],
                                 ab_d_skip[j], ab_ssd_norm[j], ab_rpb[j], ab_w_out[j])
        else:
            j = layer // 2
            mixed = mlstm_mixer(h, ml_w_in[j], ml_gate_b[j], ml_head_norm[j], ml_w_out[j])
        x = x + g1[:, None, :] * rmsnorm(mixed, norm_g[layer, 1])
        h = modulate(rmsnorm(x, norm_g[layer, 2]), sh2, sc2)
        u = jnp.square(jax.nn.relu(h @ mlp_w1[layer])) @ mlp_w2[layer]
        x = x + g2[:, None, :] * rmsnorm(u, norm_g[layer, 3])
    return x


_first_inputs = first_inputs


def first_inputs(seed=0):
    import zlib

    import numpy as np

    out = dict(_first_inputs(seed))
    spreads = {}
    factors = {'ab_conv_b': 5.268,
     'ab_d_skip': 8.0,
     'ab_ssd_norm': 7.986,
     'ab_rpb': 8.0,
     'ml_head_norm': 8.0}
    for name, (base, spread) in spreads.items():
        noise = np.random.default_rng([zlib.crc32(name.encode()), seed]).standard_normal(out[name].shape)
        drawn = base * np.exp(spread * noise) if base else spread * noise
        out[name] = __import__('jax').numpy.asarray(drawn.astype(out[name].dtype))
    for name, factor in factors.items():
        out[name] = (out[name] * factor).astype(out[name].dtype)
    return out


_narrow_inputs = first_inputs


def first_inputs(seed=0):

    out = dict(_narrow_inputs(seed))
    wider = {'ab_d_skip': 11.51, 'ab_ssd_norm': 8.58, 'ab_rpb': 7.96, 'ml_head_norm': 11.4}
    for name, times in wider.items():
        mean = out[name].mean()
        out[name] = (mean + times * (out[name] - mean)).astype(out[name].dtype)
    return out


DEPTH_2 = 1

N_MEM = 256
BRANCH_W = D_MODEL // 2
N_BRANCH = 3
MIX_W = N_BRANCH * BRANCH_W

FOX_HD = 64
FOX_HEADS = BRANCH_W // FOX_HD
FOX_W = FOX_HEADS * FOX_HD
Q_BLOCK = 128
FOX_FBIAS_OFFSET = 3.0

S5_W = BRANCH_W
S5_GROUP = 16
S5_GROUPS = S5_W // S5_GROUP
S5_STATE = 64

HG_DK = 128
HG_DV = 128
HG_HEADS = BRANCH_W // HG_DV
HG_W = HG_HEADS * HG_DV
HG_CHUNK = 64

X_HEADS = 4
X_HD = D_MODEL // X_HEADS

D_FF_2 = ((8 * D_MODEL + 3 * 256 - 1) // (3 * 256)) * 256

IN_SIZES = (FOX_W, FOX_W, FOX_W, FOX_HEADS, S5_W, HG_HEADS * HG_DK, HG_HEADS * HG_DK, HG_W, HG_W, N_BRANCH * D_MODEL)
IN_COLS = sum(IN_SIZES)
EPS = 1e-6


def rmsnorm_2(x, g):
    xf = x.astype(jnp.float32)
    y = xf * lax.rsqrt(jnp.mean(xf * xf, axis=-1, keepdims=True) + EPS)
    return (y * g.astype(jnp.float32)).astype(x.dtype)

def _split_points(sizes):
    pts, acc = [], 0
    for s in sizes[:-1]:
        acc += s
        pts.append(acc)
    return pts

def fox_attention(q, k, v, log_f):
    bsz, seq, n_h, hd = q.shape
    n_blk = seq // Q_BLOCK
    c = jnp.cumsum(log_f, axis=1)
    c_keys = c.transpose(0, 2, 1)[:, :, None, :]
    q_blocks = q.reshape(bsz, n_blk, Q_BLOCK, n_h, hd).transpose(1, 0, 2, 3, 4)
    c_blocks = c.reshape(bsz, n_blk, Q_BLOCK, n_h).transpose(1, 0, 3, 2)
    k_pos = jnp.arange(seq)
    scale = hd ** -0.5

    def block(args):
        qi, ci, bi = args
        s = jnp.einsum('bqhd,bkhd->bhqk', qi, k, preferred_element_type=jnp.float32) * scale
        s = s + ci[..., None] - c_keys
        q_pos = bi * Q_BLOCK + jnp.arange(Q_BLOCK)
        s = jnp.where(k_pos[None, :] <= q_pos[:, None], s, -jnp.inf)
        p = jax.nn.softmax(s, axis=-1).astype(v.dtype)
        return jnp.einsum('bhqk,bkhd->bqhd', p, v)

    out = lax.map(block, (q_blocks, c_blocks, jnp.arange(n_blk)))
    return out.transpose(1, 0, 2, 3, 4).reshape(bsz, seq, n_h, hd)

def _complex_linear_combine(e1, e2):
    a1r, a1i, b1r, b1i = e1
    a2r, a2i, b2r, b2i = e2
    return (a1r * a2r - a1i * a2i,
            a1r * a2i + a1i * a2r,
            a2r * b1r - a2i * b1i + b2r,
            a2r * b1i + a2i * b1r + b2i)

def s5_mixer(u, a_re, a_im, b_re, b_im, c_re, c_im, d_skip, log_dt, w_glu, b_glu):
    bsz, seq, _ = u.shape
    f32 = jnp.float32
    uf = u.astype(f32)
    ug = uf.reshape(bsz, seq, S5_GROUPS, S5_GROUP)
    dt = jnp.exp(log_dt.astype(f32))[:, None]
    ar, ai = a_re.astype(f32), a_im.astype(f32)
    mag = jnp.exp(dt * ar)
    abar_r, abar_i = mag * jnp.cos(dt * ai), mag * jnp.sin(dt * ai)
    inv_den = 1.0 / (ar * ar + ai * ai)
    nr, ni = abar_r - 1.0, abar_i
    coef_r = (nr * ar + ni * ai) * inv_den
    coef_i = (ni * ar - nr * ai) * inv_den
    br, bi = b_re.astype(f32), b_im.astype(f32)
    bbar_r = coef_r[..., None] * br - coef_i[..., None] * bi
    bbar_i = coef_r[..., None] * bi + coef_i[..., None] * br
    drive_r = jnp.einsum('bsgh,gph->bsgp', ug, bbar_r)
    drive_i = jnp.einsum('bsgh,gph->bsgp', ug, bbar_i)
    a_shape = (1, seq, S5_GROUPS, S5_STATE)
    elems = (jnp.broadcast_to(abar_r, a_shape), jnp.broadcast_to(abar_i, a_shape), drive_r, drive_i)
    _, _, h_r, h_i = lax.associative_scan(_complex_linear_combine, elems, axis=1)
    y = (jnp.einsum('bsgp,ghp->bsgh', h_r, c_re.astype(f32))
         - jnp.einsum('bsgp,ghp->bsgh', h_i, c_im.astype(f32)))
    y = y.reshape(bsz, seq, S5_W) + d_skip.astype(f32) * uf
    z = jax.nn.gelu(y)
    out = z * jax.nn.sigmoid(z @ w_glu.astype(f32) + b_glu.astype(f32))
    return out.astype(u.dtype)

def hgrn2_mixer(q, f_logit, i_in, g_out, lb, o_gain):
    bsz, seq = q.shape[0], q.shape[1]
    f32 = jnp.float32
    n_chunks = seq // HG_CHUNK
    z = f_logit.astype(f32)
    log_f = jnp.logaddexp(jnp.log(lb), jnp.log1p(-lb) + jax.nn.log_sigmoid(z))
    key = (1.0 - lb) * jax.nn.sigmoid(-z)
    qf = jax.nn.silu(q.astype(f32))
    vf = i_in.astype(f32)

    def chunks(t):
        return t.reshape(bsz, n_chunks, HG_CHUNK, HG_HEADS, t.shape[-1]).transpose(1, 0, 3, 2, 4)

    causal = jnp.tril(jnp.ones((HG_CHUNK, HG_CHUNK), dtype=bool))[None, None, :, :, None]

    def step(state, xs):
        qc, kc, vc, lfc = xs
        b = jnp.cumsum(lfc, axis=2)
        o_inter = jnp.einsum('bhtk,bhkv->bhtv', qc * jnp.exp(b), state)
        rel = jnp.where(causal, b[:, :, :, None, :] - b[:, :, None, :, :], -jnp.inf)
        scores = jnp.einsum('bhtsk,bhsk->bhts', qc[:, :, :, None, :] * jnp.exp(rel), kc)
        o_intra = jnp.einsum('bhts,bhsv->bhtv', scores, vc)
        b_last = b[:, :, -1:, :]
        new_state = (jnp.exp(b_last[:, :, 0, :])[..., None] * state
                     + jnp.einsum('bhsk,bhsv->bhkv', kc * jnp.exp(b_last - b), vc))
        return new_state, o_inter + o_intra

    init = jnp.zeros((bsz, HG_HEADS, HG_DK, HG_DV), f32)
    _, o = lax.scan(step, init, (chunks(qf), chunks(key), chunks(vf), chunks(log_f)))
    o = o.transpose(1, 0, 3, 2, 4).reshape(bsz, seq, HG_HEADS, HG_DV)
    o = rmsnorm_2(o, o_gain) * jax.nn.silu(g_out.astype(f32))
    return o.reshape(bsz, seq, HG_W).astype(q.dtype)

def cross_attention(h, m, wq, wk, wv, wo, gq, gk):
    bsz, seq, _ = h.shape
    n_mem = m.shape[1]
    q = rmsnorm_2((h @ wq).reshape(bsz, seq, X_HEADS, X_HD), gq)
    k = rmsnorm_2((m @ wk).reshape(bsz, n_mem, X_HEADS, X_HD), gk)
    v = (m @ wv).reshape(bsz, n_mem, X_HEADS, X_HD)
    s = jnp.einsum('bshd,bmhd->bhsm', q, k, preferred_element_type=jnp.float32) * (X_HD ** -0.5)
    p = jax.nn.softmax(s, axis=-1).astype(v.dtype)
    o = jnp.einsum('bhsm,bmhd->bshd', p, v).reshape(bsz, seq, X_HEADS * X_HD)
    return o @ wo

def swiglu(h, w_gu, w_d):
    a, b = jnp.split(h @ w_gu, 2, axis=-1)
    return (jax.nn.silu(a) * b) @ w_d

def second_inputs(seed: int = 0) -> dict:
    key = jax.random.key(seed)
    keys = jax.random.split(key, 40)
    counter = [0]
    f32 = jnp.float32

    def nxt():
        k = keys[counter[0]]
        counter[0] += 1
        return k

    def nrm(shape, scale):
        return jax.random.normal(nxt(), shape, f32) * scale

    def gain(shape):
        return 1.0 + nrm(shape, 0.02)

    L, D = DEPTH_2, D_MODEL
    G, P, GS = S5_GROUPS, S5_STATE, S5_GROUP
    return {
        'x': nrm((BATCH, SEQ, D), 1.0),
        'mem': nrm((BATCH, N_MEM, D), 1.0),
        'norm_mix': gain((L, D)),
        'w_in': nrm((L, D, IN_COLS), D ** -0.5),
        'fox_fbias': FOX_FBIAS_OFFSET + nrm((L, FOX_HEADS), 0.5),
        'fox_qnorm': gain((L, FOX_HD)),
        'fox_knorm': gain((L, FOX_HD)),
        's5_a_re': -0.5 + nrm((L, G, P), 0.01),
        's5_a_im': math.pi * jnp.arange(P, dtype=f32)[None, None, :] + nrm((L, G, P), 0.01),
        's5_b_re': nrm((L, G, P, GS), (2 * GS) ** -0.5),
        's5_b_im': nrm((L, G, P, GS), (2 * GS) ** -0.5),
        's5_c_re': nrm((L, G, GS, P), (2 * P) ** -0.5),
        's5_c_im': nrm((L, G, GS, P), (2 * P) ** -0.5),
        's5_d': nrm((L, S5_W), 1.0),
        's5_log_dt': jax.random.uniform(nxt(), (L, G), f32, math.log(1e-3), math.log(1e-1)),
        's5_w_glu': nrm((L, S5_W, S5_W), S5_W ** -0.5),
        's5_b_glu': nrm((L, S5_W), 0.01),
        'hg_lb': nrm((L, HG_HEADS * HG_DK), 0.1),
        'hg_onorm': gain((L, HG_DV)),
        'w_branch': nrm((L, MIX_W, D), BRANCH_W ** -0.5),
        'w_out': nrm((L, D, D), D ** -0.5),
        'norm_x': gain((L, D)),
        'norm_mem': gain((L, D)),
        'xq': nrm((L, D, D), D ** -0.5),
        'xk': nrm((L, D, D), D ** -0.5),
        'xv': nrm((L, D, D), D ** -0.5),
        'xo': nrm((L, D, D), D ** -0.5),
        'x_qnorm': gain((L, X_HD)),
        'x_knorm': gain((L, X_HD)),
        'norm_ffn': gain((L, D)),
        'w_gate_up': nrm((L, D, 2 * D_FF_2), D ** -0.5),
        'w_down': nrm((L, D_FF_2, D), D_FF_2 ** -0.5),
    }

def second_block(x, mem, norm_mix, w_in, fox_fbias, fox_qnorm, fox_knorm, s5_a_re, s5_a_im,
              s5_b_re, s5_b_im, s5_c_re, s5_c_im, s5_d, s5_log_dt, s5_w_glu, s5_b_glu,
              hg_lb, hg_onorm, w_branch, w_out, norm_x, norm_mem, xq, xk, xv, xo,
              x_qnorm, x_knorm, norm_ffn, w_gate_up, w_down):
    bsz, seq, _ = x.shape
    split_pts = _split_points(IN_SIZES)
    lb_all = jnp.cumsum(jax.nn.softmax(hg_lb.astype(jnp.float32), axis=0), axis=0)
    lb_all = lb_all - lb_all[0:1]
    for l in range(DEPTH_2):
        h = rmsnorm_2(x, norm_mix[l])
        proj = h @ w_in[l]
        fq, fk, fv, ff, su, hq, hf, hi, hg, gl = jnp.split(proj, split_pts, axis=-1)
        q = rmsnorm_2(fq.reshape(bsz, seq, FOX_HEADS, FOX_HD), fox_qnorm[l])
        k = rmsnorm_2(fk.reshape(bsz, seq, FOX_HEADS, FOX_HD), fox_knorm[l])
        v = fv.reshape(bsz, seq, FOX_HEADS, FOX_HD)
        log_f = jax.nn.log_sigmoid((ff + fox_fbias[l]).astype(jnp.float32))
        y_fox = fox_attention(q, k, v, log_f).reshape(bsz, seq, FOX_W)
        y_s5 = s5_mixer(su, s5_a_re[l], s5_a_im[l], s5_b_re[l], s5_b_im[l], s5_c_re[l], s5_c_im[l],
                        s5_d[l], s5_log_dt[l], s5_w_glu[l], s5_b_glu[l])
        y_hg = hgrn2_mixer(hq.reshape(bsz, seq, HG_HEADS, HG_DK), hf.reshape(bsz, seq, HG_HEADS, HG_DK),
                           hi.reshape(bsz, seq, HG_HEADS, HG_DV), hg.reshape(bsz, seq, HG_HEADS, HG_DV),
                           lb_all[l].reshape(HG_HEADS, HG_DK), hg_onorm[l])
        gates = jax.nn.sigmoid(gl).reshape(bsz, seq, N_BRANCH, D_MODEL)
        wb = w_branch[l]
        merged = (gates[:, :, 0] * (y_fox @ wb[:BRANCH_W])
                  + gates[:, :, 1] * (y_s5 @ wb[BRANCH_W:2 * BRANCH_W])
                  + gates[:, :, 2] * (y_hg @ wb[2 * BRANCH_W:]))
        x = x + merged @ w_out[l]
        x = x + cross_attention(rmsnorm_2(x, norm_x[l]), rmsnorm_2(mem, norm_mem[l]),
                                xq[l], xk[l], xv[l], xo[l], x_qnorm[l], x_knorm[l])
        x = x + swiglu(rmsnorm_2(x, norm_ffn[l]), w_gate_up[l], w_down[l])
    return x


def setup_inputs(seed=0):
    out = dict(first_inputs(seed))
    for name, value in second_inputs(seed + 1).items():
        if name != "x":
            out[name + "_2"] = value
    return out


def reference(
    x, c, ada_w, ada_b, norm_g, mlp_w1, mlp_w2, ab_w_in, ab_conv_w, ab_conv_b, ab_dt_bias,
    ab_a_log, ab_d_skip, ab_ssd_norm, ab_rpb, ab_w_out, ml_w_in, ml_gate_b, ml_head_norm,
    ml_w_out, mem_2, norm_mix_2, w_in_2, fox_fbias_2, fox_qnorm_2, fox_knorm_2, s5_a_re_2,
    s5_a_im_2, s5_b_re_2, s5_b_im_2, s5_c_re_2, s5_c_im_2, s5_d_2, s5_log_dt_2, s5_w_glu_2,
    s5_b_glu_2, hg_lb_2, hg_onorm_2, w_branch_2, w_out_2, norm_x_2, norm_mem_2, xq_2, xk_2,
    xv_2, xo_2, x_qnorm_2, x_knorm_2, norm_ffn_2, w_gate_up_2, w_down_2,
):
    x = first_block(
        x, c, ada_w, ada_b, norm_g, mlp_w1, mlp_w2, ab_w_in, ab_conv_w, ab_conv_b, ab_dt_bias,
        ab_a_log, ab_d_skip, ab_ssd_norm, ab_rpb, ab_w_out, ml_w_in, ml_gate_b, ml_head_norm,
        ml_w_out,
    )
    return second_block(
        x, mem_2, norm_mix_2, w_in_2, fox_fbias_2, fox_qnorm_2, fox_knorm_2, s5_a_re_2,
        s5_a_im_2, s5_b_re_2, s5_b_im_2, s5_c_re_2, s5_c_im_2, s5_d_2, s5_log_dt_2, s5_w_glu_2,
        s5_b_glu_2, hg_lb_2, hg_onorm_2, w_branch_2, w_out_2, norm_x_2, norm_mem_2, xq_2, xk_2,
        xv_2, xo_2, x_qnorm_2, x_knorm_2, norm_ffn_2, w_gate_up_2, w_down_2,
    )


_drawn_inputs = setup_inputs


def setup_inputs(seed=0):
    import zlib

    import numpy as np

    out = dict(_drawn_inputs(seed))
    spreads = {}
    factors = {'norm_mix_2': 5.436,
     'fox_qnorm_2': 8.0,
     'fox_knorm_2': 8.0,
     's5_a_re_2': 64.0,
     's5_a_im_2': 49.024,
     's5_b_re_2': 64.0,
     's5_b_im_2': 64.0,
     's5_c_re_2': 64.0,
     's5_c_im_2': 64.0,
     's5_log_dt_2': 52.608,
     's5_b_glu_2': 64.0,
     'hg_onorm_2': 8.0,
     'norm_x_2': 8.0,
     'norm_mem_2': 8.0,
     'x_qnorm_2': 8.0,
     'x_knorm_2': 8.0,
     'norm_ffn_2': 16.251}
    for name, (base, spread) in spreads.items():
        noise = np.random.default_rng([zlib.crc32(name.encode()), seed]).standard_normal(out[name].shape)
        drawn = base * np.exp(spread * noise) if base else spread * noise
        out[name] = jnp.asarray(drawn.astype(out[name].dtype))
    for name, factor in factors.items():
        out[name] = (out[name] * factor).astype(out[name].dtype)
    return out
```

```python
from contextlib import ExitStack

import numpy as np

import concourse.bass as bass
from concourse import mybir

F32 = mybir.dt.float32
BF16 = mybir.dt.bfloat16
I32 = mybir.dt.int32
ALU = mybir.AluOpType
ACT = mybir.ActivationFunctionType
AX = mybir.AxisListType.X

P = 128
TOK = 256
TT = TOK // P
D = 1024
KD = D // P
CK = 4
CN = 512
RING = 8
EPS = 1e-6
NEG = -1e30
NH = 16
HP = 64
FF1 = 4096
MH, MDK, MDV = 8, 128, 256
FOXH = 8
HGH = 4
S5T = 16
FF2T = 22
GRID = 64


def tiles_of(c0, n=CN):
    return [c0 + P * i for i in range(n // P)]


def groups(kind, c0, c1):
    return [(kind, tiles_of(c)) for c in range(c0, c1, CN)]


def ada_groups():
    out = []
    for part, kind in enumerate(("col", "col", "row", "col", "col", "row")):
        out += groups(kind, part * D, part * D + D)
    return out


PRODUCTS = [
    ("ada0", "ada_w", 0, KD, ada_groups()),
    ("in0", "ab_w_in", 0, KD, groups("feat", 1024, 2560) + groups("tok", 0, 1024)
     + groups("feat", 2592, 4640) + groups("tok", 4640, 5664)),
    ("out0", "ab_w_out", 0, 16, groups("tok", 0, D)),
    ("up0", "mlp_w1", 0, KD, groups("feat", 0, FF1)),
    ("down0", "mlp_w2", 0, FF1 // P, groups("tok", 0, D)),
    ("ada1", "ada_w", 1, KD, ada_groups()),
    ("in1", "ml_w_in", 0, KD, groups("feat", 0, 2048) + groups("tok", 2048, 6144)),
    ("out1", "ml_w_out", 0, 16, groups("tok", 0, D)),
    ("up1", "mlp_w1", 1, KD, groups("feat", 0, FF1)),
    ("down1", "mlp_w2", 1, FF1 // P, groups("tok", 0, D)),
    ("in2", "w_in_2", 0, KD, groups("tok", 0, 1536) + groups("feat", 1544, 3080)
     + groups("tok", 3080, 7176)),
    ("glu", "s5_w_glu_2", 0, 4, groups("feat", 0, 512)),
    ("fox_out", "w_branch_2", 0, 4, groups("tok", 0, D)),
    ("s5_out", "w_branch_2", 0, 4, groups("tok", 0, D)),
    ("hg_out", "w_branch_2", 0, 4, groups("tok", 0, D)),
    ("mix_out", "w_out_2", 0, KD, groups("tok", 0, D)),
    ("xk", "xk_2", 0, KD, groups("tok", 0, D)),
    ("xv", "xv_2", 0, KD, groups("tok", 0, D)),
    ("xq", "xq_2", 0, KD, groups("tok", 0, D)),
    ("xo", "xo_2", 0, KD, groups("tok", 0, D)),
    ("gate_up", "w_gate_up_2", 0, KD,
     [("feat", [256 * j, 256 * j + P, FF2T * P + 256 * j, FF2T * P + 256 * j + P]) for j in range(FF2T // 2)]),
    ("swi_down", "w_down_2", 0, FF2T, groups("tok", 0, D)),
]
ROW0 = {"s5_out": 512, "hg_out": 1024}


def chunks_of(kt):
    return [(k, min(CK, kt - k)) for k in range(0, kt, CK)]


def pack_stream(inputs):
    out = []
    for name, weight, layer, kt, grps in PRODUCTS:
        w = inputs[weight][layer][ROW0.get(name, 0):]
        for _, cols in grps:
            for k0, nk in chunks_of(kt):
                c = np.zeros((P, CK, CN), np.float32)
                for i, col in enumerate(cols):
                    blk = w[k0 * P:(k0 + nk) * P, col:col + P].reshape(nk, P, P)
                    c[:, :nk, i * P:(i + 1) * P] = blk.transpose(1, 0, 2)
                out.append(c)
    return np.stack(out)


def cols(v):
    return np.ascontiguousarray(np.asarray(v).reshape(-1, P).T)


def pad_rows(v, n=64):
    c = np.zeros((P, 1), np.float32)
    c[0:v.shape[1], 0] = v[0]
    c[32:32 + v.shape[1], 0] = v[1]
    return c


def pack_params(I):
    parts = {"c": cols(I["c"][0])}
    for l in range(2):
        for j in (0, 2):
            parts[f"norm{l}{j}"] = cols(I["norm_g"][l, j])
        for j in (0, 1, 3, 4):
            parts[f"ada_b{l}{j}"] = cols(I["ada_b"][l, j * D:(j + 1) * D])
    parts["conv_w"] = np.concatenate([cols(I["ab_conv_w"][0, i]) for i in range(5)], 1)
    parts["conv_b"] = cols(I["ab_conv_b"][0])
    parts["dt_bias"] = pad_rows(I["ab_dt_bias"][0])
    parts["a_log"] = pad_rows(I["ab_a_log"][0])
    parts["d_skip"] = np.broadcast_to(I["ab_d_skip"][0], (P, NH))
    rpb = np.zeros((P, NH, 7), np.float32)
    rpb[0:31] = I["ab_rpb"][0][:, 4:11, :].transpose(2, 0, 1)
    parts["rpb"] = rpb.reshape(P, NH * 7)
    parts["ssd_norm"] = cols(I["ab_ssd_norm"][0])
    parts["gate_i"] = pad_rows(I["ml_gate_b"][0, 0::2])
    parts["gate_f"] = pad_rows(I["ml_gate_b"][0, 1::2])
    parts["head_norm"] = cols(I["ml_head_norm"][0])
    for n in ("norm_mix", "norm_x", "norm_mem", "norm_ffn"):
        parts[n] = cols(I[n + "_2"][0])
    for n in ("fox_qnorm", "fox_knorm"):
        parts[n] = np.tile(I[n + "_2"][0], 2)[:, None]
    parts["fbias"] = np.pad(I["fox_fbias_2"][0], (0, P - FOXH))[:, None]
    for n in ("x_qnorm", "x_knorm"):
        parts[n] = cols(I[n + "_2"][0])
    parts["hg_onorm"] = I["hg_onorm_2"][0][:, None]
    for n in ("s5_a_re", "s5_a_im"):
        parts[n] = cols(I[n + "_2"][0])
    parts["s5_log_dt"] = cols(np.repeat(I["s5_log_dt_2"][0], 64))
    for n in ("s5_b_re", "s5_b_im"):
        parts[n] = I[n + "_2"][0].reshape(S5T, P, 16).transpose(1, 0, 2).reshape(P, -1)
    for n in ("s5_c_re", "s5_c_im"):
        parts[n] = I[n + "_2"][0].transpose(0, 2, 1).reshape(S5T, P, 16).transpose(1, 0, 2).reshape(P, -1)
    parts["s5_d"] = cols(I["s5_d_2"][0])
    parts["s5_b_glu"] = cols(I["s5_b_glu_2"][0])
    at, where = 0, {}
    for n, a in parts.items():
        where[n] = (at, a.shape[1])
        at += a.shape[1]
    return np.concatenate([np.asarray(a, np.float32) for a in parts.values()], 1), where


def pack_narrow(I):
    dt = np.zeros((D, 64), np.float32)
    w = I["ab_w_in"][0][:, 2560:2592]
    dt[:, 0:NH], dt[:, 32:32 + NH] = w[:, 0:NH], w[:, NH:]
    gates = np.zeros((D, 128), np.float32)
    w = I["ml_w_in"][0][:, 6144:6176]
    for j, at in enumerate((0, 64, 32, 96)):
        gates[:, at:at + MH] = w[:, MH * j:MH * j + MH]
    fox = np.zeros((D, 32), np.float32)
    fox[:, 0:FOXH] = I["w_in_2"][0][:, 1536:1544]
    w = np.concatenate([dt, gates, fox], 1)
    return np.ascontiguousarray(w.reshape(KD, P, 224).transpose(1, 0, 2))


def constants():
    p, f = np.arange(P)[:, None], np.arange(P)[None, :]
    up = np.where(f >= p, 0.0, NEG)
    lo = np.where(f <= p, 0.0, NEG)
    zero, none = np.zeros((P, P)), np.full((P, P), NEG)
    levels = [((p // (2 * m) == f // (2 * m)) & (p % (2 * m) < m) & (f % (2 * m) >= m)) * 1.0
              for m in (64, 32, 16, 8, 4, 2, 1)]
    toe = np.zeros((P, 192))
    for x in range(31):
        toe[x, 78 - x] = toe[x, 142 - x] = 1.0
    c = np.arange(P)[:, None] % GRID
    kc = np.arange(GRID)[None, :]
    start = np.clip(c - 8, 0, GRID - 16)
    window = np.where((kc >= start) & (kc < start + 16), 0.0, NEG)
    parts = {
        "ident": np.eye(P), "levels": np.concatenate(levels + [np.eye(P)], 1), "toeplitz": toe,
        "window": window, "time": np.broadcast_to(np.arange(TOK), (P, TOK)), "ones": np.ones((P, TOK)),
        "mask_f": np.concatenate([up, zero, up], 1), "mask_b": np.concatenate([lo, zero, lo], 1),
        "mask_q": np.concatenate([lo, none, zero, lo], 1),
    }
    at, where = 0, {}
    for n, a in parts.items():
        where[n] = (at, a.shape[1])
        at += a.shape[1]
    return np.concatenate([np.asarray(a, np.float32) for a in parts.values()], 1), where


class Mark:

    def __init__(self, sem, before):
        self.sem, self.before = sem, before

    def at(self, n):
        return self.sem, self.before + n


class Steps:

    def __init__(self, eng, sem):
        self.eng, self.sem, self.n = eng, sem, 0

    def __call__(self, ins):
        ins.then_inc(self.sem, 1)
        self.n += 1

    def wait(self):
        self.eng.wait_ge(self.sem, self.n)


class Arena:

    def __init__(self, tensor):
        self.t, self.at, self.size = tensor, 0, tensor.shape[1]

    def rest(self, n):
        self.at = n

    def take(self, *shape):
        n = int(np.prod(shape))
        a = self.t[:, self.at:self.at + n]
        self.at += n
        assert self.at <= self.size, (self.at, self.size)
        if len(shape) == 2:
            a = a.rearrange("p (a b) -> p a b", b=shape[1])
        elif len(shape) == 3:
            a = a.rearrange("p (a b c) -> p a b c", b=shape[1], c=shape[2])
        return a


def region(k, at):
    a = Arena(k.arena.t)
    a.rest(at)
    return a


class Core:

    def __init__(self, nc, ctx, params, consts, narrow_shape, where_p, where_c):
        self.nc, self.ctx = nc, ctx
        sb = lambda name, shape, dt=F32: ctx.enter_context(nc.sbuf_tensor(name, shape, dt))
        self.ring = sb("ring", [P, RING, CK, CN])
        self.x = sb("x_res", [P, TT, D])
        self.hT = sb("hT", [P, KD, TOK])
        self.par_all = sb("par", [P, params])
        self.con_all = sb("con", [P, consts])
        self.narrow = sb("narrow_w", list(narrow_shape))
        self.mask_bf = sb("mask_bf", [P, 10 * P + P], BF16)
        self.arena = Arena(sb("arena", [P, 25536]))
        self.ps = ctx.enter_context(nc.psum_tensor("ps", [P, 8, 512], F32))
        self.where_p, self.where_c = where_p, where_c
        self.sems, self.raised = {}, {}
        self.groups = 0
        self.chunks = 0
        self.act_groups = [0]
        self.dve_groups = [0]
        self.loaded = [self.sem(f"chunk_loaded{i}") for i in range(RING)]
        self.chunk_used = self.sem("chunk_used")
        self.act_took = self.sem("act_took_group")
        self.dve_took = self.sem("dve_took_group")
        self.stage_done = self.sem("stage_done")
        self.inputs_in = self.sem("inputs_in")

    def sem(self, name):
        return self.ctx.enter_context(self.nc.semaphore(name))

    def mark(self, name, total):
        if name not in self.sems:
            self.sems[name], self.raised[name] = self.sem(name), 0
        m = Mark(self.sems[name], self.raised[name])
        self.raised[name] += total
        return m

    def par(self, name):
        at, n = self.where_p[name]
        return self.par_all[:, at:at + n]

    def con(self, name):
        at, n = self.where_c[name]
        return self.con_all[:, at:at + n]


class Stage:

    def __init__(self, k):
        self.k = k

    def tensor(self, pe):
        pass

    def scalar(self, act, st):
        pass

    def vector(self, dve, st):
        pass

    def gpsimd(self, pool, st):
        pass


def rstd_scalar(act, st, k, var, guess, m, n):
    act.wait_ge(*m["var"].at(n))
    st(act.activation(guess, var, ACT.Ln))
    st.wait()
    act.activation(guess, guess, ACT.Exp, scale=-0.5).then_inc(m["guess"].sem, 1)


def rstd_vector(dve, st, var, guess, tmp, m, n):
    dve.wait_ge(*m["guess"].at(n))
    st(dve.tensor_tensor(tmp, guess, guess, ALU.mult))
    st.wait()
    st(dve.tensor_tensor(tmp, tmp, var, ALU.mult))
    st.wait()
    st(dve.tensor_scalar(tmp, tmp, -0.5, 1.5, ALU.mult, ALU.add))
    st.wait()
    st(dve.tensor_tensor(guess, guess, tmp, ALU.mult))
    st.wait()


class Setup(Stage):

    def __init__(self, k, cond):
        super().__init__(k)
        self.cond = cond

    def scalar(self, act, st):
        act.wait_ge(self.k.inputs_in, 64)
        st(act.activation(self.cond, self.k.par("c"), ACT.Silu))

    def vector(self, dve, st):
        k = self.k
        dve.wait_ge(k.inputs_in, 64)
        at, n = k.where_c["mask_f"]
        st(dve.tensor_copy(k.mask_bf[:, 0:10 * P], k.con_all[:, at:at + 10 * P]))
        st(dve.tensor_copy(k.mask_bf[:, 10 * P:11 * P], k.con("ident")))


class Norm(Stage):

    def __init__(self, k, src, nf, dst, scale, bias, xh, small):
        super().__init__(k)
        self.src, self.nf, self.dst, self.scale, self.bias = src, nf, dst, scale, bias
        self.xh, self.small = xh, small
        self.m = {"sq": k.mark("sums_of_squares", 2), "var": k.mark("variance", 1),
                  "guess": k.mark("rstd_guess", 1), "xh": k.mark("rows_scaled", TT),
                  "turned": k.mark("bank_turned", nf // 2)}

    def scalar(self, act, st):
        m = self.m
        for t in range(TT):
            act.activation(self.xh[:, t, :], self.src[:, t, :], ACT.Square,
                           accum_out=self.small[:, t:t + 1]).then_inc(m["sq"].sem, 1)
        rstd_scalar(act, st, self.k, self.small[:, 2:4], self.small[:, 4:6], m, 1)
        self.take_out(act, 0)

    def take_out(self, eng, parity):
        for j in range(self.nf // 2):
            if j % 2 != parity:
                continue
            eng.wait_ge(*self.m["turned"].at(j + 1))
            for f in (2 * j, 2 * j + 1):
                src = self.k.ps[:, 4 + j, (f % 2) * TOK:(f % 2 + 1) * TOK]
                if parity == 0:
                    eng.activation(self.dst[:, f, :], src, ACT.Identity, scale=self.scale[:, f:f + 1],
                                   bias=self.bias[:, f:f + 1] if self.bias is not None else 0.0)
                elif self.bias is not None:
                    eng.tensor_scalar(self.dst[:, f, :], src, self.scale[:, f:f + 1],
                                      self.bias[:, f:f + 1], ALU.mult, ALU.add)
                else:
                    eng.tensor_scalar(self.dst[:, f, :], src, self.scale[:, f:f + 1], None, ALU.mult)

    def vector(self, dve, st):
        m, s = self.m, self.small
        dve.wait_ge(*m["sq"].at(2))
        dve.tensor_scalar(s[:, 2:4], s[:, 0:2], 1.0 / (self.nf * P), EPS, ALU.mult,
                          ALU.add).then_inc(m["var"].sem, 1)
        rstd_vector(dve, st, s[:, 2:4], s[:, 4:6], s[:, 6:8], m, 1)
        for t in range(TT):
            dve.tensor_scalar(self.xh[:, t, :], self.src[:, t, :], s[:, 4 + t:5 + t], None,
                              ALU.mult).then_inc(m["xh"].sem, 1)
        self.take_out(dve, 1)

    def tensor(self, pe):
        k, m = self.k, self.m
        pe.wait_ge(*m["xh"].at(TT))
        for f in range(self.nf):
            for t in range(TT):
                at = (f % 2) * TOK + t * P
                last = pe.transpose(k.ps[:, 4 + f // 2, at:at + P], self.xh[:, t, f * P:(f + 1) * P],
                                    k.con("ident"))
            if f % 2:
                last.then_inc(m["turned"].sem, 1)


class Product(Stage):

    def __init__(self, k, name, src, act_out, dve_out, act_after=None, dve_after=None):
        super().__init__(k)
        self.act_after, self.dve_after = act_after, dve_after
        self.src, self.act_out, self.dve_out = src, act_out, dve_out
        _, _, _, self.kt, self.groups = next(p for p in PRODUCTS if p[0] == name)
        self.first_group, self.first_chunk = k.groups, k.chunks
        self.nchunks = len(chunks_of(self.kt))
        k.groups += len(self.groups)
        k.chunks += len(self.groups) * self.nchunks
        for _ in self.groups:
            k.act_groups.append(k.act_groups[-1] + (act_out is not None))
            k.dve_groups.append(k.dve_groups[-1] + 1)

    def chunk_end(self, i):
        return self.first_chunk + (i + 1) * self.nchunks

    def tensor(self, pe):
        k = self.k
        for i, (kind, _) in enumerate(self.groups):
            g = self.first_group + i
            if g >= 2:
                if k.act_groups[g - 1]:
                    pe.wait_ge(k.act_took, k.act_groups[g - 1])
                pe.wait_ge(k.dve_took, k.dve_groups[g - 1])
            bank = 2 * (g % 2)
            parts = [(self.first_chunk + i * self.nchunks + j, k0, nk)
                     for j, (k0, nk) in enumerate(chunks_of(self.kt))]

            def arrived(c):
                pe.wait_ge(k.loaded[c % RING], 16 * (c // RING + 1))

            if kind in ("tok", "row"):
                for c, k0, nk in parts:
                    arrived(c)
                    for kk in range(nk):
                        first, last = k0 + kk == 0, k0 + kk == self.kt - 1
                        w = k.ring[:, c % RING, kk, :]
                        if kind == "row":
                            mm = pe.matmul(k.ps[:, bank, :], self.src[:, k0 + kk:k0 + kk + 1].broadcast_to([P, P]),
                                           w, start=first, stop=last)
                        else:
                            for t in range(TT):
                                mm = pe.matmul(k.ps[:, bank + t, :], self.src[:, k0 + kk, t * P:(t + 1) * P],
                                               w, start=first, stop=last)
                    mm.then_inc(k.chunk_used, 1)
            else:
                for c, _, _ in parts:
                    arrived(c)
                for f in range(4):
                    for c, k0, nk in parts:
                        for kk in range(nk):
                            first, last = k0 + kk == 0, k0 + kk == self.kt - 1
                            w = k.ring[:, c % RING, kk, f * P:(f + 1) * P]
                            if kind == "col":
                                mm = pe.matmul(k.ps[:, bank, f:f + 1], w, self.src[:, k0 + kk:k0 + kk + 1],
                                               start=first, stop=last)
                            else:
                                mm = pe.matmul(k.ps[:, bank + f // 2, (f % 2) * TOK:(f % 2 + 1) * TOK], w,
                                               self.src[:, k0 + kk, :], start=first, stop=last)
                        if f == 3:
                            mm.then_inc(k.chunk_used, 1)

    def scalar(self, act, st):
        if self.act_out is None:
            return
        for i in range(len(self.groups)):
            act.wait_ge(self.k.chunk_used, self.chunk_end(i))
            self.act_out(act, st, i, self.k.ps[:, 2 * ((self.first_group + i) % 2), :]) \
                .then_inc(self.k.act_took, 1)
            if self.act_after is not None:
                self.act_after(act, st, i)

    def vector(self, dve, st):
        for i in range(len(self.groups)):
            dve.wait_ge(self.k.chunk_used, self.chunk_end(i))
            bank = 2 * ((self.first_group + i) % 2) + (self.act_out is not None)
            self.dve_out(dve, st, i, self.k.ps[:, bank, :]).then_inc(self.k.dve_took, 1)
            if self.dve_after is not None:
                self.dve_after(dve, st, i)


class Post(Stage):

    def __init__(self, k, y, gain, junk, small):
        super().__init__(k)
        self.y, self.gain, self.junk, self.small = y, gain, junk, small
        self.m = {"sq": k.mark("sums_of_squares", 2), "var": k.mark("variance", 1),
                  "guess": k.mark("rstd_guess", 1)}

    def scalar(self, act, st):
        for t in range(TT):
            act.activation(self.junk[:, t, :], self.y[:, t, :], ACT.Square,
                           accum_out=self.small[:, t:t + 1]).then_inc(self.m["sq"].sem, 1)
        rstd_scalar(act, st, self.k, self.small[:, 2:4], self.small[:, 4:6], self.m, 1)

    def vector(self, dve, st):
        m, s = self.m, self.small
        dve.wait_ge(*m["sq"].at(2))
        dve.tensor_scalar(s[:, 2:4], s[:, 0:2], 1.0 / D, EPS, ALU.mult, ALU.add).then_inc(m["var"].sem, 1)
        rstd_vector(dve, st, s[:, 2:4], s[:, 4:6], s[:, 6:8], m, 1)
        for t in range(TT):
            st(dve.scalar_tensor_tensor(self.y[:, t, :], self.y[:, t, :], s[:, 4 + t:5 + t], self.gain,
                                        ALU.mult, ALU.mult))
        st.wait()
        for t in range(TT):
            st(dve.tensor_tensor(self.k.x[:, t, :], self.k.x[:, t, :], self.y[:, t, :], ALU.add))


def to_rows(dst):
    def act_out(act, st, i, bank):
        return act.activation(dst[:, 0, i * CN:(i + 1) * CN], bank, ACT.Identity)

    def dve_out(dve, st, i, bank):
        return dve.tensor_copy(dst[:, 1, i * CN:(i + 1) * CN], bank)
    return act_out, dve_out


def to_features(dst):
    def act_out(act, st, i, bank):
        return act.activation(dst[:, 4 * i:4 * i + 2, :], bank.rearrange("p (a b) -> p a b", a=2), ACT.Identity)

    def dve_out(dve, st, i, bank):
        return dve.tensor_copy(dst[:, 4 * i + 2:4 * i + 4, :], bank.rearrange("p (a b) -> p a b", a=2))
    return act_out, dve_out


def by_ranges(*ranges):
    def pick(which):
        def out(eng, st, i, bank):
            for n, pair in ranges:
                if i < n:
                    return pair[which](eng, st, i, bank)
                i -= n
        return out
    return pick(0), pick(1)


class Ada(Product):

    def __init__(self, k, layer, cond, mod, gains, bias, norm_g, ada_b):
        super().__init__(k, f"ada{layer}", cond, None, self.take)
        self.layer, self.mod, self.gains, self.bias = layer, mod, gains, bias
        self.norm_g, self.ada_b = norm_g, ada_b
        self.rows = k.mark("gate_rows_loaded", 64)

    def gpsimd(self, pool, st):
        for j, part in ((0, 2), (1, 5)):
            pool.dma_start(self.gains[:, j, :], self.norm_g[self.layer, 2 * j + 1].partition_broadcast(P)) \
                .then_inc(self.rows.sem, 16)
            pool.dma_start(self.bias[:, j, :], self.ada_b[self.layer, part * D:(part + 1) * D]
                           .partition_broadcast(P)).then_inc(self.rows.sem, 16)

    def take(self, dve, st, i, bank):
        k, part, half = self.k, i // 2, i % 2
        if part in (2, 5):
            j, at = part // 3, slice(half * CN, (half + 1) * CN)
            if i == 4:
                dve.wait_ge(*self.rows.at(64))
            st(dve.tensor_tensor(self.bias[:, j, at], bank, self.bias[:, j, at], ALU.add))
            st.wait()
            return dve.tensor_tensor(self.gains[:, j, at], self.gains[:, j, at], self.bias[:, j, at], ALU.mult)
        c = {0: 0, 1: 1, 3: 2, 4: 3}[part]
        at = slice(4 * half, 4 * half + 4)
        dst = self.mod[:, c, at]
        b = k.par(f"ada_b{self.layer}{part}")[:, at]
        if c in (0, 2):
            return dve.tensor_tensor(dst, bank[:, 0:4], b, ALU.add)
        st(dve.tensor_tensor(dst, bank[:, 0:4], b, ALU.add))
        st.wait()
        return dve.scalar_tensor_tensor(dst, dst, 1.0, k.par(f"norm{self.layer}{0 if c == 1 else 2}")[:, at],
                                        ALU.add, ALU.mult)


def mlp_stages(k, layer, u, y):
    def act_out(act, st, i, bank):
        dst = u[:, 4 * i:4 * i + 2, :]
        st(act.activation(dst, bank.rearrange("p (a b) -> p a b", a=2), ACT.Relu))
        st.wait()
        return act.activation(dst, dst, ACT.Square)

    def dve_out(dve, st, i, bank):
        dst = u[:, 4 * i + 2:4 * i + 4, :]
        b = bank.rearrange("p (a b) -> p a b", a=2)
        st(dve.tensor_scalar(dst, b, 0.0, None, ALU.max))
        st.wait()
        return dve.tensor_tensor(dst, dst, dst, ALU.mult)

    return [Product(k, f"up{layer}", k.hT, act_out, dve_out),
            Product(k, f"down{layer}", u, *to_rows(y))]


class Turn(Stage):

    def __init__(self, k, src, nf, dst, scale=None):
        super().__init__(k)
        self.src, self.nf, self.dst, self.scale = src, nf, dst, scale
        self.turned = k.mark("bank_turned", nf // 2)

    def tensor(self, pe):
        for f in range(self.nf):
            for t in range(TT):
                at = (f % 2) * TOK + t * P
                last = pe.transpose(self.k.ps[:, f // 2, at:at + P], self.src[:, t, f * P:(f + 1) * P],
                                    self.k.con("ident"))
            if f % 2:
                last.then_inc(self.turned.sem, 1)

    def take_out(self, eng, parity):
        for j in range(self.nf // 2):
            if j % 2 != parity:
                continue
            eng.wait_ge(*self.turned.at(j + 1))
            if self.scale is None:
                src = self.k.ps[:, j, :].rearrange("p (a b) -> p a b", a=2)
                if parity:
                    eng.tensor_copy(self.dst[:, 2 * j:2 * j + 2, :], src)
                else:
                    eng.activation(self.dst[:, 2 * j:2 * j + 2, :], src, ACT.Identity)
                continue
            for f in (2 * j, 2 * j + 1):
                src = self.k.ps[:, j, (f % 2) * TOK:(f % 2 + 1) * TOK]
                if parity:
                    eng.tensor_scalar(self.dst[:, f, :], src, self.scale(f), None, ALU.mult)
                else:
                    eng.activation(self.dst[:, f, :], src, ACT.Identity, scale=self.scale(f))

    def scalar(self, act, st):
        self.take_out(act, 0)

    def vector(self, dve, st):
        self.take_out(dve, 1)


class Attention(Stage):

    def __init__(self, k, heads, w, q, keys, v, out, buf, table=None, lead=None):
        super().__init__(k)
        self.heads, self.w, self.q, self.keys, self.v, self.out = heads, w, q, keys, v, out
        self.table, self.lead = table, lead
        self.pm = buf.take(2, TT, TOK)
        self.pt = buf.take(2, 2, TOK)
        self.sb = buf.take(2, TT, TOK) if table else None
        self.small = buf.take(3, TT, 16)
        self.m = {n: k.mark(n, heads) for n in ("scores_in", "maxima_in", "probs_in", "probs_turned",
                                                "probs_taken", "values_in")}

    def tensor(self, pe):
        k, m, w = self.k, self.m, self.w

        def scores(h):
            if h >= 2:
                pe.wait_ge(*m["probs_in"].at(h - 1))
            bank = k.ps[:, h % 2, :]
            if self.lead:
                self.lead(pe, h, bank)
            for t in range(TT):
                parts = list(zip(self.q(h, t), self.keys(h)))
                for i, (a, b) in enumerate(parts):
                    mm = pe.matmul(bank[:, t * TOK:(t + 1) * TOK], a, b, start=i == 0 and not self.lead,
                                   stop=i == len(parts) - 1, skip_group_check=bool(self.lead))
            mm.then_inc(m["scores_in"].sem, 1)

        def turn(h):
            pe.wait_ge(*m["probs_in"].at(h + 1))
            if h >= 2:
                pe.wait_ge(*m["probs_taken"].at(h - 1))
            for t in range(TT):
                for s in range(2):
                    last = pe.transpose(k.ps[:, 2 + h % 2, s * TOK + t * P:s * TOK + (t + 1) * P],
                                        self.pm[:, h % 2, t, s * P:(s + 1) * P], k.con("ident"))
            last.then_inc(m["probs_turned"].sem, 1)

        def values(h):
            pe.wait_ge(*m["probs_taken"].at(h + 1))
            for t in range(TT):
                at = (h * w) % 512
                for s in range(2):
                    mm = pe.matmul(k.ps[:, 4 + 2 * t + (h * w) // 512, at:at + w],
                                   self.pt[:, h % 2, s, t * P:(t + 1) * P], self.v(h, s),
                                   start=s == 0, stop=s == 1)
            mm.then_inc(m["values_in"].sem, 1)

        for h in range(self.heads + 2):
            if h < self.heads:
                scores(h)
            if 1 <= h <= self.heads:
                turn(h - 1)
            if h >= 2:
                values(h - 2)

    def scalar(self, act, st):
        m, s = self.m, self.small
        for h in range(self.heads):
            act.wait_ge(*m["maxima_in"].at(h + 1))
            if h >= 2:
                act.wait_ge(*m["probs_turned"].at(h - 1))
            for t in range(TT):
                src = self.sb[:, h % 2, t, :] if self.table else self.k.ps[:, h % 2, t * TOK:(t + 1) * TOK]
                last = act.activation(self.pm[:, h % 2, t, :], src, ACT.Exp, bias=s[:, 0, t, h:h + 1],
                                      accum_out=s[:, 1, t, h:h + 1])
            last.then_inc(m["probs_in"].sem, 1)

    def vector(self, dve, st):
        k, m, s, w = self.k, self.m, self.small, self.w
        for h in range(self.heads + 1):
            if h < self.heads:
                dve.wait_ge(*m["scores_in"].at(h + 1))
                if self.table:
                    if h >= 2:
                        dve.wait_ge(*m["probs_in"].at(h - 1))
                    for t in range(TT):
                        st(dve.tensor_tensor_reduce(self.sb[:, h % 2, t, :], k.ps[:, h % 2, t * TOK:(t + 1) * TOK],
                                                    self.table(h, t), 1.0, -3e38, ALU.add, ALU.max,
                                                    s[:, 0, t, h:h + 1]))
                else:
                    st(dve.tensor_reduce(s[:, 0, :, h], k.ps[:, h % 2, :].rearrange("p (t n) -> p t n", t=TT),
                                         AX, ALU.max))
                st.wait()
                dve.tensor_scalar(s[:, 0, :, h], s[:, 0, :, h], -1.0, None, ALU.mult) \
                    .then_inc(m["maxima_in"].sem, 1)
            if h >= 1:
                dve.wait_ge(*m["probs_turned"].at(h))
                if h >= 3:
                    dve.wait_ge(*m["values_in"].at(h - 2))
                dve.tensor_copy(self.pt[:, (h - 1) % 2, :, :],
                                k.ps[:, 2 + (h - 1) % 2, :].rearrange("p (s n) -> p s n", s=2)) \
                   .then_inc(m["probs_taken"].sem, 1)
        dve.wait_ge(*m["probs_in"].at(self.heads))
        dve.wait_ge(*m["values_in"].at(self.heads))
        n = self.heads
        st(dve.reciprocal(s[:, 2, :, 0:n], s[:, 1, :, 0:n]))
        st.wait()
        per = min(n, 512 // w)
        for t in range(TT):
            for half in range(n // per):
                dst = self.out[:, t, half * per * w:(half + 1) * per * w].rearrange("p (h w) -> p h w", w=w)
                src = k.ps[:, 4 + 2 * t + half, 0:per * w].rearrange("p (h w) -> p h w", w=w)
                r = s[:, 2, t, half * per:(half + 1) * per].unsqueeze(2).broadcast_to([P, per, w])
                st(dve.tensor_tensor(dst, src, r, ALU.mult))


class Pads(Stage):

    def __init__(self, k, xp):
        super().__init__(k)
        self.xp = xp

    def vector(self, dve, st):
        st(dve.memset(self.xp[:, :, 0:2], 0.0))
        st(dve.memset(self.xp[:, :, TOK + 2:TOK + 4], 0.0))


def in0_stage(k, xp, xc, zs, qT, kT, v):
    conv_done = k.mark("convolved", 3)
    first = k.groups

    def xbc_act(act, st, i, bank):
        return act.activation(xp[:, 4 * i:4 * i + 2, 2:2 + TOK], bank.rearrange("p (a b) -> p a b", a=2),
                              ACT.Identity)

    def xbc_dve(dve, st, i, bank):
        return dve.tensor_copy(xp[:, 4 * i + 2:4 * i + 4, 2:2 + TOK], bank.rearrange("p (a b) -> p a b", a=2))

    def z_act(act, st, i, bank):
        return act.activation(zs[:, 0, i * CN:(i + 1) * CN], bank, ACT.Silu)

    def z_dve(dve, st, i, bank):
        return dve.tensor_copy(zs[:, 1, i * CN:(i + 1) * CN], bank)

    def q_act(act, st, i, bank):
        return act.activation(qT[:, 4 * i:4 * i + 2, :], bank.rearrange("p (a b) -> p a b", a=2),
                              ACT.Identity, scale=HP ** -0.5)

    def q_dve(dve, st, i, bank):
        return dve.tensor_scalar(qT[:, 4 * i + 2:4 * i + 4, :], bank.rearrange("p (a b) -> p a b", a=2),
                                 HP ** -0.5, None, ALU.mult)

    act_out, dve_out = by_ranges((3, (xbc_act, xbc_dve)), (2, (z_act, z_dve)), (2, (q_act, q_dve)),
                                 (2, to_features(kT)), (2, to_rows(v)))

    def dve_after(dve, st, i):
        if i >= 3:
            return
        dve.wait_ge(k.act_took, k.act_groups[first + i + 1])
        dve.wait_ge(k.dve_took, k.dve_groups[first + i + 1])
        for tap in range(5):
            for j in range(4 * i, 4 * i + 4):
                src, w = xp[:, j, tap:tap + TOK], k.par("conv_w")[:, 12 * tap + j:12 * tap + j + 1]
                if tap == 0:
                    ins = dve.tensor_scalar(xc[:, j, :], src, w, k.par("conv_b")[:, j:j + 1], ALU.mult, ALU.add)
                else:
                    ins = dve.scalar_tensor_tensor(xc[:, j, :], src, w, xc[:, j, :], ALU.mult, ALU.add)
                if tap == 4 and j == 4 * i + 3:
                    ins.then_inc(conv_done.sem, 1)
                else:
                    st(ins)
            if tap < 4:
                st.wait()

    def act_after(act, st, i):
        if 1 <= i <= 3:
            act.wait_ge(*conv_done.at(i))
            dst = xc[:, 4 * i - 4:4 * i, :]
            st(act.activation(dst, dst, ACT.Silu))
        if i == 5:
            act.wait_ge(k.dve_took, k.dve_groups[first + 5])
            st(act.activation(zs[:, 1, :], zs[:, 1, :], ACT.Silu))

    return Product(k, "in0", k.hT, act_out, dve_out, act_after, dve_after)


def softplus_scalar(act, st, k, u, a, wait, done):
    act.wait_ge(*wait)
    st(act.activation(a, u, ACT.Abs))
    st.wait()
    st(act.activation(a, a, ACT.Exp, scale=-1.0))
    st.wait()
    act.activation(a, a, ACT.Ln, bias=k.con("ones")[0:a.shape[0], 0:1]).then_inc(done.sem, 1)


class SsdPrep(Stage):

    def __init__(self, k, xc, xt, xf, xb, cbf, cbb, cs4, csn, dtc, tmp):
        super().__init__(k)
        self.xc, self.xt, self.xf, self.xb, self.cbf, self.cbb = xc, xt, xf, xb, cbf, cbb
        self.cs4, self.csn, self.dtc, self.tmp = cs4, csn, dtc, tmp
        self.m = {n: k.mark(n, c) for n, c in (("narrow_in", 1), ("cb_in", 2), ("x_turned", 4), ("biased", 1),
                                               ("log_in", 1), ("rates_in", 1), ("sums_in", 1), ("sums_turned", 1), ("x_copied", 2))}

    def tensor(self, pe):
        k, m = self.k, self.m
        for f in range(KD):
            mm = pe.matmul(k.ps[0:64, 4, 0:TOK], k.narrow[:, f, 0:64], k.hT[:, f, :], start=f == 0,
                           stop=f == KD - 1)
        mm.then_inc(m["narrow_in"].sem, 1)
        for g in range(2):
            for s in range(2):
                mm = pe.matmul(k.ps[:, 5 + g, s * TOK:(s + 1) * TOK], self.xc[:, 8 + g, s * P:(s + 1) * P],
                               self.xc[:, 10 + g, :], start=True, stop=True)
            mm.then_inc(m["cb_in"].sem, 1)
        for b in range(4):
            for q in range(4):
                mm = pe.transpose(k.ps[:, b, q * P:(q + 1) * P],
                                  self.xc[:, 4 * (b % 2) + q, (b // 2) * P:(b // 2 + 1) * P], k.con("ident"))
            mm.then_inc(m["x_turned"].sem, 1)
        pe.wait_ge(*m["sums_in"].at(1))
        for t in range(TT):
            pe.transpose(k.ps[:, 7, t * 64:(t + 1) * 64], self.cs4[0:64, P + t * P:P + (t + 1) * P],
                         k.con("ident")[0:64, 0:64])
            mm = pe.transpose(k.ps[:, 7, P + t * 64:P + (t + 1) * 64], self.tmp[0:64, 2, t * P:(t + 1) * P],
                              k.con("ident")[0:64, 0:64])
        mm.then_inc(m["sums_turned"].sem, 1)

    def scalar(self, act, st):
        k, m, tmp = self.k, self.m, self.tmp
        softplus_scalar(act, st, k, tmp[0:64, 0, :], tmp[0:64, 1, :], m["biased"].at(1), m["log_in"])
        act.activation(tmp[0:64, 3, 0:1], k.par("a_log")[0:64, :], ACT.Exp).then_inc(m["rates_in"].sem, 1)
        for b in (0, 1):
            act.wait_ge(*m["x_turned"].at(b + 1))
            act.activation(self.xt[:, b // 2, (b % 2) * 512:(b % 2 + 1) * 512], k.ps[:, b, :], ACT.Identity) \
               .then_inc(m["x_copied"].sem, 1)

    def vector(self, dve, st):
        k, m, tmp = self.k, self.m, self.tmp
        u, a, dt, adt = (tmp[0:64, j, :] for j in (0, 1, 2, 4))
        dve.wait_ge(*m["narrow_in"].at(1))
        dve.tensor_scalar(u, k.ps[0:64, 4, 0:TOK], k.par("dt_bias")[0:64, :], None, ALU.add) \
           .then_inc(m["biased"].sem, 1)
        dve.wait_ge(*m["cb_in"].at(2))
        for g in range(2):
            b = k.ps[:, 5 + g, :]
            st(dve.tensor_copy(self.cbf[:, g, 0:TOK], b[:, 0:TOK]))
            st(dve.tensor_copy(self.cbf[:, g, TOK:TOK + P], b[:, TOK + P:2 * TOK]))
            st(dve.tensor_copy(self.cbb[:, g, 0:P], b[:, 0:P]))
            st(dve.tensor_copy(self.cbb[:, g, P:P + TOK], b[:, TOK:2 * TOK]))
        for b in (2, 3):
            dve.wait_ge(*m["x_turned"].at(b + 1))
            st(dve.tensor_copy(self.xt[:, b // 2, (b % 2) * 512:(b % 2 + 1) * 512], k.ps[:, b, :]))
        dve.wait_ge(*m["log_in"].at(1))
        dve.wait_ge(*m["rates_in"].at(1))
        st(dve.scalar_tensor_tensor(dt, u, 0.0, a, ALU.max, ALU.add))
        st.wait()
        st(dve.tensor_scalar(adt, dt, tmp[0:64, 3, 0:1], -1.0, ALU.mult, ALU.mult))
        st.wait()
        ones, cs = k.con("ones"), self.cs4[:, P:P + TOK]
        st(dve.tensor_tensor_scan(cs[0:32, :], ones[0:32, :], adt[0:32, :], 0.0, ALU.mult, ALU.add))
        st(dve.tensor_tensor_scan(cs[32:64, ::-1], ones[32:64, :], adt[32:64, ::-1], 0.0, ALU.mult, ALU.add))
        st.wait()
        st(dve.tensor_copy(self.cs4[0:64, 0:P], self.cs4[0:64, P:2 * P]))
        dve.tensor_copy(self.cs4[0:64, 3 * P:4 * P], self.cs4[0:64, 2 * P:3 * P]).then_inc(m["sums_in"].sem, 1)
        dve.wait_ge(*m["sums_turned"].at(1))
        turned = k.ps[:, 7, 0:4 * 64].rearrange("p (a t c) -> p a t c", a=2, t=TT)
        st(dve.tensor_scalar(self.csn, turned[:, 0], -1.0, None, ALU.mult))
        st(dve.tensor_copy(self.dtc, turned[:, 1]))
        st.wait()
        dve.wait_ge(*m["x_copied"].at(2))
        for t in range(TT):
            x = self.xt[:, t, :].rearrange("p (h w) -> p h w", w=HP)
            for d, dst in ((0, self.xf), (1, self.xb)):
                st(dve.tensor_tensor(dst[:, t, :].rearrange("p (h w) -> p h w", w=HP), x,
                                     self.dtc[:, t, 32 * d:32 * d + NH].unsqueeze(2).broadcast_to([P, NH, HP]),
                                     ALU.mult))


class Ssd(Stage):

    def __init__(self, k, xt, xf, xb, cbf, cbb, cs4, csn, zs, e):
        super().__init__(k)
        self.xt, self.xf, self.xb, self.cbf, self.cbb = xt, xf, xb, cbf, cbb
        self.cs4, self.csn, self.zs, self.e = cs4, csn, zs, e
        self.m = {"args": k.mark("decay_args", 2 * NH), "exp": k.mark("decays_in", 2 * NH),
                  "g": k.mark("weights_in", 2 * NH), "y": k.mark("head_out", NH)}

    def tensor(self, pe):
        k, m = self.k, self.m

        def args(i):
            h, d = i // 2, i % 2
            if i >= 4:
                pe.wait_ge(*m["exp"].at(i - 3))
            c = 32 * d + h
            bank = k.ps[:, i % 4, 0:3 * P]
            pe.matmul(bank, k.con("ident")[0:64, c:c + 1].broadcast_to([64, P]),
                      self.cs4[0:64, P * (1 - d):P * (4 - d)], start=True, stop=False)
            pe.matmul(bank, k.mask_bf[:, 10 * P:11 * P], k.mask_bf[:, 3 * P * d:3 * P * (d + 1)],
                      start=False, stop=True).then_inc(m["args"].sem, 1)

        def out(h):
            pe.wait_ge(*m["g"].at(2 * h + 2))
            f, b = self.e[:, (2 * h) % 4, :], self.e[:, (2 * h + 1) % 4, :]
            hs = slice(h * HP, (h + 1) * HP)
            for t in range(TT):
                if t == 0:
                    parts = [(f[:, 0:P], self.xf[:, 0, hs]), (b[:, 0:P], self.xb[:, 0, hs]),
                             (b[:, P:2 * P], self.xb[:, 1, hs])]
                else:
                    parts = [(f[:, P:2 * P], self.xf[:, 0, hs]), (f[:, 2 * P:3 * P], self.xf[:, 1, hs]),
                             (b[:, 2 * P:3 * P], self.xb[:, 1, hs])]
                for n, (w, x) in enumerate(parts):
                    mm = pe.matmul(k.ps[:, 4 + 2 * t + h // 8, (h % 8) * HP:(h % 8 + 1) * HP], w, x,
                                   start=n == 0, stop=n == 2)
            mm.then_inc(m["y"].sem, 1)

        for h in range(NH + 1):
            if h < NH:
                args(2 * h)
                args(2 * h + 1)
            if h >= 1:
                out(h - 1)

    def scalar(self, act, st):
        m = self.m
        for i in range(2 * NH):
            h, d = i // 2, i % 2
            act.wait_ge(*m["args"].at(i + 1))
            if i >= 4:
                act.wait_ge(*m["y"].at((i - 4) // 2 + 1))
            cut = TOK if d == 0 else P
            e, ps, c = self.e[:, i % 4, :], self.k.ps[:, i % 4, :], 32 * d + h
            act.activation(e[:, 0:cut], ps[:, 0:cut], ACT.Exp, bias=self.csn[:, 0, c:c + 1])
            act.activation(e[:, cut:3 * P], ps[:, cut:3 * P], ACT.Exp, bias=self.csn[:, 1, c:c + 1]) \
               .then_inc(m["exp"].sem, 1)

    def vector(self, dve, st):
        k, m = self.k, self.m
        for t in range(TT):
            x = self.xt[:, t, :].rearrange("p (h w) -> p h w", w=HP)
            st(dve.tensor_tensor(x, x, k.par("d_skip").unsqueeze(2).broadcast_to([P, NH, HP]), ALU.mult))
        for i in range(2 * NH):
            h, d = i // 2, i % 2
            dve.wait_ge(*m["exp"].at(i + 1))
            cb = (self.cbf, self.cbb)[d][:, h // 8, :]
            dve.tensor_tensor(self.e[:, i % 4, :], self.e[:, i % 4, :], cb, ALU.mult).then_inc(m["g"].sem, 1)
        dve.wait_ge(*m["y"].at(NH))
        for t in range(TT):
            for half in range(2):
                x = self.xt[:, t, half * 512:(half + 1) * 512]
                st(dve.tensor_tensor(x, k.ps[:, 4 + 2 * t + half, :], x, ALU.add))
        st.wait()
        for t in range(TT):
            st(dve.tensor_tensor(self.zs[:, t, :], self.zs[:, t, :], self.xt[:, t, :], ALU.mult))


class BiasTable(Stage):

    def __init__(self, k, table):
        super().__init__(k)
        self.table = table
        self.m = {"picked": k.mark("bias_picked", 16), "taken": k.mark("bias_taken", 16)}

    def tensor(self, pe):
        k, m = self.k, self.m
        toe = k.con("toeplitz")
        for j in range(16):
            if j >= 2:
                pe.wait_ge(*m["taken"].at(j - 1))
            for i in range(4):
                kc = 4 * j + i
                mm = pe.matmul(k.ps[:, j % 2, 112 * i:112 * (i + 1)],
                               toe[0:32, 63 - kc:191 - kc],
                               k.par("rpb")[0:32, :], start=True, stop=True)
            mm.then_inc(m["picked"].sem, 1)

    def vector(self, dve, st):
        k, m = self.k, self.m
        table = self.table.rearrange("p (h u c) -> p h u c", h=NH, u=6)
        for j in range(16):
            dve.wait_ge(*m["picked"].at(j + 1))
            for half in range(2):
                rows = slice(64 * half, 64 * half + 64)
                for i in range(4):
                    kc = 4 * j + i
                    src = k.ps[rows, j % 2, 112 * i:112 * (i + 1)].rearrange("p (h d) -> p h d", d=7)
                    ins = dve.tensor_scalar(table[rows, :, :, kc], src[:, :, 1 - half:7 - half],
                                            k.con("window")[rows, kc:kc + 1], None, ALU.add)
                    if half == 1 and i == 3:
                        ins.then_inc(m["taken"].sem, 1)


class GatePrep(Stage):

    def __init__(self, k, tmp, negm, acol, floor):
        super().__init__(k)
        self.tmp, self.negm, self.acol, self.floor = tmp, negm, acol, floor
        self.m = {n: k.mark(n, c) for n, c in (("narrow_in", 2), ("biased", 1), ("log_in", 1),
                                               ("sums_in", 1), ("sums_turned", 1))}

    def tensor(self, pe):
        k, m = self.k, self.m
        for j in range(2):
            for f in range(KD):
                mm = pe.matmul(k.ps[0:64, 4 + j, 0:TOK], k.narrow[:, f, 64 + 64 * j:128 + 64 * j],
                               k.hT[:, f, :], start=f == 0, stop=f == KD - 1)
            mm.then_inc(m["narrow_in"].sem, 1)
        pe.wait_ge(*m["sums_in"].at(1))
        for t in range(TT):
            pe.transpose(k.ps[:, 7, t * 64:(t + 1) * 64], self.tmp[0:64, 5, t * P:(t + 1) * P],
                         k.con("ident")[0:64, 0:64])
            mm = pe.transpose(k.ps[:, 7, P + t * 64:P + (t + 1) * 64], self.tmp[0:64, 6, t * P:(t + 1) * P],
                              k.con("ident")[0:64, 0:64])
        mm.then_inc(m["sums_turned"].sem, 1)

    def scalar(self, act, st):
        k, m, tmp = self.k, self.m, self.tmp
        softplus_scalar(act, st, k, tmp[0:64, 1, :], tmp[0:64, 2, :], m["biased"].at(1), m["log_in"])
        act.wait_ge(*m["sums_turned"].at(1))
        st(act.activation(self.floor, k.ps[:, 7, P:2 * P].rearrange("p (t c) -> p t c", t=TT), ACT.Exp,
                          scale=-1.0))
        st(act.activation(self.acol, k.ps[:, 7, 0:P].rearrange("p (t c) -> p t c", t=TT), ACT.Identity))

    def vector(self, dve, st):
        k, m, tmp = self.k, self.m, self.tmp
        ig, fg, ln, lf, b, a, mm = (tmp[0:64, j, :] for j in range(7))
        dve.wait_ge(*m["narrow_in"].at(2))
        st(dve.tensor_scalar(ig, k.ps[0:64, 4, 0:TOK], k.par("gate_i")[0:64, :], None, ALU.add))
        dve.tensor_scalar(fg, k.ps[0:64, 5, 0:TOK], k.par("gate_f")[0:64, :], None, ALU.add) \
           .then_inc(m["biased"].sem, 1)
        dve.wait_ge(*m["log_in"].at(1))
        st(dve.scalar_tensor_tensor(lf, fg, 0.0, ln, ALU.min, ALU.subtract))
        st.wait()
        ones = k.con("ones")
        st(dve.tensor_tensor_scan(b[0:32, :], ones[0:32, :], lf[0:32, :], 0.0, ALU.mult, ALU.add))
        st(dve.tensor_tensor_scan(b[32:64, ::-1], ones[32:64, :], lf[32:64, ::-1], 0.0, ALU.mult, ALU.add))
        st.wait()
        st(dve.tensor_tensor(a, ig, b, ALU.subtract))
        st.wait()
        st(dve.tensor_tensor_scan(mm[0:32, :], ones[0:32, :], a[0:32, :], 0.0, ALU.mult, ALU.max))
        st(dve.tensor_tensor_scan(mm[32:64, ::-1], ones[32:64, :], a[32:64, ::-1], 0.0, ALU.mult, ALU.max))
        st.wait()
        st(dve.tensor_scalar(self.negm[0:64, P:P + TOK], mm, -1.0, None, ALU.mult))
        st.wait()
        st(dve.tensor_copy(self.negm[0:64, 0:P], self.negm[0:64, P:2 * P]))
        st(dve.tensor_copy(self.negm[0:64, 3 * P:4 * P], self.negm[0:64, 2 * P:3 * P]))
        dve.tensor_tensor(mm, mm, b, ALU.add).then_inc(m["sums_in"].sem, 1)


class Mlstm(Stage):

    def __init__(self, k, qT, kT, v, negm, acol, floor, h, e, sc, small):
        super().__init__(k)
        self.qT, self.kT, self.v, self.negm, self.acol, self.floor = qT, kT, v, negm, acol, floor
        self.h, self.e, self.sc, self.small = h, e, sc, small
        self.m = {"args": k.mark("decay_args", 2 * MH), "exp": k.mark("decays_in", 2 * MH),
                  "g": k.mark("weights_in", 2 * MH), "s": k.mark("products_in", MH),
                  "sc": k.mark("products_copied", MH),
                  "num": k.mark("numerators_in", 4 * MH), "h": k.mark("numerators_taken", 4 * MH)}

    def tensor(self, pe):
        k, m = self.k, self.m

        def args(i):
            h, d = i // 2, i % 2
            if d == 0:
                if h >= 1:
                    pe.wait_ge(*m["sc"].at(h))
                for s in range(2):
                    mm = pe.matmul(k.ps[:, 2, s * TOK:(s + 1) * TOK], self.kT[:, h, s * P:(s + 1) * P],
                                   self.qT[:, h, :], start=True, stop=True)
                mm.then_inc(m["s"].sem, 1)
            if i >= 2:
                pe.wait_ge(*m["exp"].at(i - 1))
            c = 32 * d + h
            bank = k.ps[:, i % 2, 0:3 * P]
            pe.matmul(bank, k.con("ident")[0:64, c:c + 1].broadcast_to([64, P]),
                      self.negm[0:64, P * (1 - d):P * (4 - d)], start=True, stop=False)
            pe.matmul(bank, k.mask_bf[:, 10 * P:11 * P], k.mask_bf[:, 3 * P * d:3 * P * (d + 1)],
                      start=False, stop=True).then_inc(m["args"].sem, 1)

        def out(i):
            h, d = i // 2, i % 2
            pe.wait_ge(*m["g"].at(i + 1))
            w, v = self.e[:, i % 4, :], lambda s: self.v[:, s, h, :]
            for t in range(TT):
                n = 2 * i + t
                if n >= 4:
                    pe.wait_ge(*m["h"].at(n - 3))
                if d == 0:
                    parts = [(w[:, 0:P], v(0))] if t == 0 else [(w[:, P:2 * P], v(0)), (w[:, 2 * P:3 * P], v(1))]
                else:
                    parts = [(w[:, 0:P], v(0)), (w[:, P:2 * P], v(1))] if t == 0 else [(w[:, 2 * P:3 * P], v(1))]
                for j, (a, b) in enumerate(parts):
                    mm = pe.matmul(k.ps[:, 4 + n % 4, 0:MDV + 2], a, b, start=j == 0, stop=j == len(parts) - 1)
                mm.then_inc(m["num"].sem, 1)

        for i in range(2 * MH + 1):
            if i < 2 * MH:
                args(i)
            if i >= 1:
                out(i - 1)

    def scalar(self, act, st):
        m = self.m
        for i in range(2 * MH):
            h, d = i // 2, i % 2
            act.wait_ge(*m["args"].at(i + 1))
            if i >= 4:
                act.wait_ge(*m["num"].at(2 * (i - 4) + 2))
            cut = TOK if d == 0 else P
            e, ps, c = self.e[:, i % 4, :], self.k.ps[:, i % 2, :], 32 * d + h
            act.activation(e[:, 0:cut], ps[:, 0:cut], ACT.Exp, bias=self.acol[:, 0, c:c + 1])
            act.activation(e[:, cut:3 * P], ps[:, cut:3 * P], ACT.Exp, bias=self.acol[:, 1, c:c + 1]) \
               .then_inc(m["exp"].sem, 1)

    def vector(self, dve, st):
        k, m, sm = self.k, self.m, self.small

        def take(i):
            h, d = i // 2, i % 2
            for t in range(TT):
                n, c = 2 * i + t, 32 * d + h
                ps = k.ps[:, 4 + n % 4, :]
                dve.wait_ge(*m["num"].at(n + 1))
                st(dve.tensor_scalar(sm[:, 0:1], ps[:, MDV:MDV + 1], -1.0, None, ALU.mult))
                st.wait()
                st(dve.scalar_tensor_tensor(sm[:, 1:2], ps[:, MDV:MDV + 1], sm[:, 0:1],
                                            self.floor[:, t, c:c + 1], ALU.max, ALU.max))
                st.wait()
                st(dve.reciprocal(sm[:, 2:3], sm[:, 1:2]))
                st.wait()
                dst = self.h[:, t, h * MDV:(h + 1) * MDV]
                if d == 0:
                    ins = dve.tensor_scalar(dst, ps[:, 0:MDV], sm[:, 2:3], None, ALU.mult)
                else:
                    dve.wait_ge(*m["h"].at(n - 1))
                    ins = dve.scalar_tensor_tensor(dst, ps[:, 0:MDV], sm[:, 2:3], dst, ALU.mult, ALU.add)
                ins.then_inc(m["h"].sem, 1)

        for i in range(2 * MH + 1):
            if i < 2 * MH:
                h, d = i // 2, i % 2
                sc = self.sc[:, h % 2, :]
                if d == 0:
                    dve.wait_ge(*m["s"].at(h + 1))
                    dve.tensor_copy(sc[:, P:P + 2 * TOK], k.ps[:, 2, :]).then_inc(m["sc"].sem, 1)
                    dve.wait_ge(*m["sc"].at(h + 1))
                dve.wait_ge(*m["exp"].at(i + 1))
                e = self.e[:, i % 4, :]
                if d == 0:
                    st(dve.tensor_tensor(e[:, 0:TOK], e[:, 0:TOK], sc[:, P:P + TOK], ALU.mult))
                    ins = dve.tensor_tensor(e[:, TOK:3 * P], e[:, TOK:3 * P], sc[:, 2 * TOK:2 * TOK + P], ALU.mult)
                else:
                    st(dve.tensor_tensor(e[:, 0:P], e[:, 0:P], sc[:, P:2 * P], ALU.mult))
                    ins = dve.tensor_tensor(e[:, P:3 * P], e[:, P:3 * P], sc[:, P + TOK:P + 2 * TOK], ALU.mult)
                ins.then_inc(m["g"].sem, 1)
            if i >= 1:
                take(i - 1)


class HeadNorm(Stage):

    def __init__(self, k, h, o, small, junk):
        super().__init__(k)
        self.h, self.o, self.small, self.junk = h, o, small, junk
        self.m = {"sq": k.mark("sums_of_squares", 2), "var": k.mark("variance", 1),
                  "guess": k.mark("rstd_guess", 1)}

    def scalar(self, act, st):
        s = self.small
        for t in range(TT):
            for h in range(MH):
                ins = act.activation(self.junk[:, t * MH + h, :], self.h[:, t, h * MDV:(h + 1) * MDV],
                                     ACT.Square, accum_out=s[:, 0, t * MH + h:t * MH + h + 1])
            ins.then_inc(self.m["sq"].sem, 1)
        rstd_scalar(act, st, self.k, s[:, 1, :], s[:, 2, :], self.m, 1)

    def vector(self, dve, st):
        s, m = self.small, self.m
        dve.wait_ge(*m["sq"].at(2))
        dve.tensor_scalar(s[:, 1, :], s[:, 0, :], 1.0 / MDV, EPS, ALU.mult, ALU.add).then_inc(m["var"].sem, 1)
        rstd_vector(dve, st, s[:, 1, :], s[:, 2, :], s[:, 3, :], m, 1)
        for t in range(TT):
            for h in range(MH):
                dst = self.h[:, t, h * MDV:(h + 1) * MDV]
                st(dve.scalar_tensor_tensor(dst, dst, s[:, 2, t * MH + h:t * MH + h + 1],
                                            self.o[:, t, h * MDV:(h + 1) * MDV], ALU.mult, ALU.mult))


def layer1_stages(k, cond, mod, gains, base, small, norm_g, ada_b):
    ar = k.arena
    ar.rest(base)
    qT, kT = ar.take(8, TOK), ar.take(8, TOK)
    o, h = ar.take(TT, 2 * D), ar.take(TT, 2 * D)
    v = ar.take(TT, MH, MDV + 2)
    at = ar.at
    tmp = ar.take(7, TOK)
    negm, acol, floor = ar.take(1, 4 * P)[:, 0, :], ar.take(TT, 64), ar.take(TT, 64)
    e = ar.take(4, 3 * P)
    sm = ar.take(4, 16)
    sc = ar.take(2, 5 * P)
    ar.rest(at)
    xh = ar.take(TT, D)
    junk = region(k, base).take(TT * MH, MDV)
    ar.rest(base)
    yT = ar.take(16, TOK)
    y, junk2 = ar.take(TT, D), ar.take(TT, D)

    class OnesColumn(Stage):

        def vector(self, dve, st):
            for t in range(TT):
                st(dve.memset(v[:, t, :, MDV:MDV + 2], 1.0))

    def q_act(act, st, i, bank):
        return act.activation(qT[:, 4 * i:4 * i + 2, :], bank.rearrange("p (a b) -> p a b", a=2),
                              ACT.Identity, scale=MDK ** -0.5)

    def q_dve(dve, st, i, bank):
        return dve.tensor_scalar(qT[:, 4 * i + 2:4 * i + 4, :], bank.rearrange("p (a b) -> p a b", a=2),
                                 MDK ** -0.5, None, ALU.mult)

    def v_act(act, st, i, bank):
        return act.activation(v[:, 0, 2 * i:2 * i + 2, 0:MDV], bank.rearrange("p (a b) -> p a b", a=2), ACT.Identity)

    def v_dve(dve, st, i, bank):
        return dve.tensor_copy(v[:, 1, 2 * i:2 * i + 2, 0:MDV], bank.rearrange("p (a b) -> p a b", a=2))

    def o_act(act, st, i, bank):
        return act.activation(o[:, 0, i * CN:(i + 1) * CN], bank, ACT.Sigmoid)

    def o_dve(dve, st, i, bank):
        return dve.tensor_copy(o[:, 1, i * CN:(i + 1) * CN], bank)

    outs = by_ranges((2, (q_act, q_dve)), (2, to_features(kT)), (4, (v_act, v_dve)), (4, (o_act, o_dve)))
    first = k.groups + 12

    def act_after(act, st, i):
        if i == 11:
            act.wait_ge(k.dve_took, k.dve_groups[first + 12])
            st(act.activation(o[:, 1, :], o[:, 1, :], ACT.Sigmoid))

    return [
        Ada(k, 1, cond, mod, gains, xh, norm_g, ada_b),
        OnesColumn(k),
        Norm(k, k.x, KD, k.hT, mod[:, 1, :], mod[:, 0, :], xh, small),
        Product(k, "in1", k.hT, *outs, act_after, None),
        GatePrep(k, tmp, negm, acol, floor),
        Mlstm(k, qT, kT, v, negm, acol, floor, h, e, sc, small),
        HeadNorm(k, h, o, sm, junk),
        Turn(k, h, 16, yT, scale=lambda f: k.par("head_norm")[:, f:f + 1]),
        Product(k, "out1", yT, *to_rows(y)),
        Post(k, y, gains[:, 0, :], junk2, small),
        *mlp(k, 1, mod, gains, base, small),
    ]


class HeadScale(Stage):

    def __init__(self, k, y, heads, w, factor, sq, small, extra=None):
        super().__init__(k)
        self.y, self.heads, self.w, self.factor, self.extra = y, heads, w, factor, extra
        self.sq, self.small = sq, small
        self.m = {"var": k.mark("variance", 1), "guess": k.mark("rstd_guess", 1)}

    def scalar(self, act, st):
        rstd_scalar(act, st, self.k, self.small[:, 0], self.small[:, 1], self.m, 1)

    def vector(self, dve, st):
        s, w = self.small, self.w
        heads = lambda a: a.rearrange("p (h w) -> p h w", w=w)
        for t in range(TT):
            st(dve.tensor_tensor(self.sq[:, t, :], self.y[:, t, :], self.y[:, t, :], ALU.mult))
        st.wait()
        for t in range(TT):
            st(dve.tensor_reduce(s[:, 3, t, :], heads(self.sq[:, t, :]), AX, ALU.add))
        st.wait()
        dve.tensor_scalar(s[:, 0], s[:, 3], 1.0 / w, EPS, ALU.mult, ALU.add).then_inc(self.m["var"].sem, 1)
        rstd_vector(dve, st, s[:, 0], s[:, 1], s[:, 2], self.m, 1)
        for lo, hi, f in self.factor:
            if f != 1.0:
                st(dve.tensor_scalar(s[:, 1, :, lo:hi], s[:, 1, :, lo:hi], f, None, ALU.mult))
        st.wait()
        for t in range(TT):
            st(dve.tensor_tensor(heads(self.y[:, t, :]), heads(self.y[:, t, :]),
                                 s[:, 1, t, :].unsqueeze(2).broadcast_to([P, self.heads, w]), ALU.mult))
        if self.extra is not None:
            st.wait()
            for t in range(TT):
                st(dve.tensor_tensor(self.y[:, t, :], self.y[:, t, :], self.extra[:, t, :], ALU.mult))


class ForgetGate(Stage):

    def __init__(self, k, tmp, negc):
        super().__init__(k)
        self.tmp, self.negc = tmp, negc
        self.m = {"narrow_in": k.mark("narrow_in", 1), "biased": k.mark("biased", 1), "log_in": k.mark("log_in", 1)}

    def tensor(self, pe):
        k = self.k
        for f in range(KD):
            mm = pe.matmul(k.ps[0:32, 4, 0:TOK], k.narrow[:, f, 192:224], k.hT[:, f, :], start=f == 0,
                           stop=f == KD - 1)
        mm.then_inc(self.m["narrow_in"].sem, 1)

    def scalar(self, act, st):
        softplus_scalar(act, st, self.k, self.tmp[0:32, 0, :], self.tmp[0:32, 1, :], self.m["biased"].at(1),
                        self.m["log_in"])

    def vector(self, dve, st):
        k, m, t = self.k, self.m, self.tmp
        dve.wait_ge(*m["narrow_in"].at(1))
        dve.tensor_scalar(t[0:32, 0, :], k.ps[0:32, 4, 0:TOK], k.par("fbias")[0:32, :], None, ALU.add) \
           .then_inc(m["biased"].sem, 1)
        dve.wait_ge(*m["log_in"].at(1))
        st(dve.scalar_tensor_tensor(t[0:32, 2, :], t[0:32, 0, :], 0.0, t[0:32, 1, :], ALU.min, ALU.subtract))
        st.wait()
        st(dve.tensor_scalar(t[0:32, 2, :], t[0:32, 2, :], -1.0, None, ALU.mult))
        st.wait()
        st(dve.tensor_tensor_scan(self.negc[0:32, :], k.con("ones")[0:32, :], t[0:32, 2, :], 0.0,
                                  ALU.mult, ALU.add))


class S5Prep(Stage):

    def __init__(self, k, v, bb, spread, bT, mag, turns):
        super().__init__(k)
        self.v, self.bb, self.spread, self.bT, self.mag, self.turns = v, bb, spread, bT, mag, turns
        self.m = {"phase": k.mark("s5_phase", 2), "exp": k.mark("s5_exp", 2), "sin": k.mark("s5_sin", 2),
                  "spread": k.mark("s5_spread", 8), "turned": k.mark("s5_turned", 8),
                  "taken": k.mark("s5_taken", 8)}

    def scalar(self, act, st):
        k, m, v = self.k, self.m, self.v
        act.activation(v[:, 0, :], k.par("s5_log_dt"), ACT.Exp).then_inc(m["exp"].sem, 1)
        act.wait_ge(*m["phase"].at(1))
        act.activation(self.mag, v[:, 1, :], ACT.Exp).then_inc(m["exp"].sem, 1)
        act.wait_ge(*m["phase"].at(2))
        act.activation(v[:, 3, :], self.turns, ACT.Sin, scale=SIN_TURN).then_inc(m["sin"].sem, 1)
        act.activation(v[:, 4, :], self.turns, ACT.Sin, scale=SIN_TURN / 2).then_inc(m["sin"].sem, 1)

    def tensor(self, pe):
        k, m = self.k, self.m
        for n in range(8):
            pe.wait_ge(*m["spread"].at(n + 1))
            if n >= 2:
                pe.wait_ge(*m["taken"].at(n - 1))
            for j in range(4):
                last = pe.transpose(k.ps[:, n % 2, j * P:(j + 1) * P], self.spread[:, n % 2, j, :], k.con("ident"))
            last.then_inc(m["turned"].sem, 1)

    def vector(self, dve, st):
        k, m, v = self.k, self.m, self.v
        ar, ai = k.par("s5_a_re"), k.par("s5_a_im")
        dt, x, th, s1, s2, em, cm1, nr, ni, cr, ci, den, t1, t2, cos = (v[:, j, :] for j in range(15))

        def do(ins):
            st(ins)
            st.wait()

        dve.wait_ge(*m["exp"].at(1))
        dve.tensor_tensor(x, dt, ar, ALU.mult).then_inc(m["phase"].sem, 1)
        do(dve.tensor_tensor(th, dt, ai, ALU.mult))
        do(dve.tensor_scalar(t1, th, 1.0 / (2.0 * np.pi), ROUND, ALU.mult, ALU.add))
        do(dve.tensor_scalar(t1, t1, ROUND, None, ALU.subtract))
        dve.scalar_tensor_tensor(self.turns, th, 1.0 / (2.0 * np.pi), t1, ALU.mult, ALU.subtract) \
           .then_inc(m["phase"].sem, 1)
        dve.wait_ge(*m["phase"].at(2))
        do(dve.tensor_scalar(t1, x, 0.5, -0.5, ALU.min, ALU.max))
        do(dve.tensor_scalar(em, t1, 1.0 / 9, 1.0, ALU.mult, ALU.add))
        for n in range(8, 1, -1):
            do(dve.tensor_tensor(em, em, t1, ALU.mult))
            do(dve.tensor_scalar(em, em, 1.0 / n, 1.0, ALU.mult, ALU.add))
        do(dve.tensor_tensor(em, em, t1, ALU.mult))
        do(dve.tensor_tensor(t2, t1, x, ALU.is_equal))
        dve.wait_ge(*m["exp"].at(2))
        do(dve.tensor_scalar(t1, self.mag, 1.0, None, ALU.subtract))
        do(dve.tensor_tensor(em, em, t1, ALU.subtract))
        do(dve.tensor_tensor(em, em, t2, ALU.mult))
        do(dve.tensor_tensor(em, em, t1, ALU.add))
        dve.wait_ge(*m["sin"].at(2))
        do(dve.tensor_tensor(cm1, s2, s2, ALU.mult))
        do(dve.tensor_scalar(cm1, cm1, -2.0, None, ALU.mult))
        do(dve.tensor_scalar(cos, cm1, 1.0, None, ALU.add))
        do(dve.tensor_tensor(nr, em, cos, ALU.mult))
        do(dve.tensor_tensor(nr, nr, cm1, ALU.add))
        do(dve.tensor_tensor(ni, self.mag, s1, ALU.mult))
        do(dve.tensor_tensor(t1, ar, ar, ALU.mult))
        do(dve.tensor_tensor(t2, ai, ai, ALU.mult))
        do(dve.tensor_tensor(den, t1, t2, ALU.add))
        do(dve.reciprocal(den, den))
        do(dve.tensor_tensor(t1, nr, ar, ALU.mult))
        do(dve.tensor_tensor(t2, ni, ai, ALU.mult))
        do(dve.tensor_tensor(cr, t1, t2, ALU.add))
        do(dve.tensor_tensor(cr, cr, den, ALU.mult))
        do(dve.tensor_tensor(t1, ni, ar, ALU.mult))
        do(dve.tensor_tensor(t2, nr, ai, ALU.mult))
        do(dve.tensor_tensor(ci, t1, t2, ALU.subtract))
        do(dve.tensor_tensor(ci, ci, den, ALU.mult))
        tiles = lambda a: a.rearrange("p (i h) -> p i h", h=16)
        br, bi = tiles(k.par("s5_b_re")), tiles(k.par("s5_b_im"))
        wide = lambda a: a.unsqueeze(2).broadcast_to([P, S5T, 16])
        bbr, bbi, t3 = self.bb[:, 0], self.bb[:, 1], self.bb[:, 2]
        do(dve.tensor_tensor(bbr, br, wide(cr), ALU.mult))
        do(dve.tensor_tensor(t3, bi, wide(ci), ALU.mult))
        do(dve.tensor_tensor(bbr, bbr, t3, ALU.subtract))
        do(dve.tensor_tensor(bbi, bi, wide(cr), ALU.mult))
        do(dve.tensor_tensor(t3, br, wide(ci), ALU.mult))
        do(dve.tensor_tensor(bbi, bbi, t3, ALU.add))
        do(dve.memset(self.spread, 0.0))

        def take(n):
            dve.wait_ge(*m["turned"].at(n + 1))
            dve.tensor_copy(self.bT[:, n % 2, 4 * (n // 2):4 * (n // 2) + 4, :],
                            k.ps[:, n % 2, :].rearrange("p (j s) -> p j s", j=4)).then_inc(m["taken"].sem, 1)

        for n in range(8):
            if n >= 2:
                take(n - 2)
            src = self.bb[:, n % 2, 4 * (n // 2):4 * (n // 2) + 4, :]
            for j in range(4):
                for half in range(2):
                    rows = slice(64 * half, 64 * half + 64)
                    at = 32 * j + 16 * half
                    ins = dve.tensor_copy(self.spread[rows, n % 2, j, at:at + 16], src[rows, j, :])
                    if j == 3 and half == 1:
                        ins.then_inc(m["spread"].sem, 1)
                    else:
                        st(ins)
        take(6)
        take(7)


SIN_TURN = 6.283185
ROUND = 1.5 * 2.0 ** 23


class S5(Stage):

    def __init__(self, k, uT, bT, mag, turns, spread, tab, rot, hh, z, zs):
        super().__init__(k)
        self.uT, self.bT, self.mag, self.turns = uT, bT, mag, turns
        self.spread, self.tab, self.rot, self.hh, self.z, self.zs = spread, tab, rot, hh, z, zs
        self.m = {"phase": k.mark("s5_phases", S5T), "sin": k.mark("s5_sines", S5T),
                  "drive": k.mark("s5_drive", S5T), "dused": k.mark("s5_drive_used", S5T),
                  "h": k.mark("s5_states", S5T), "c": k.mark("s5_c_spread", 4),
                  "y": k.mark("s5_tile_used", S5T), "z": k.mark("s5_z", 4)}

    def tensor(self, pe):
        k, m = self.k, self.m

        def drive(i):
            if i >= 2:
                pe.wait_ge(*m["dused"].at(i - 1))
            for c in range(2):
                mm = pe.matmul(k.ps[:, i % 2, c * TOK:(c + 1) * TOK], self.bT[:, c, i, :], self.uT[:, i // 4, :],
                               start=True, stop=True)
            mm.then_inc(m["drive"].sem, 1)

        def out(i):
            q, j = i // 4, i % 4
            if j == 0:
                pe.wait_ge(*m["c"].at(q + 1))
            pe.wait_ge(*m["h"].at(i + 1))
            for c in range(2):
                mm = pe.matmul(k.ps[:, 4 + q, 0:TOK], self.spread[:, q % 2, c, j, :], self.hh[:, i % 2, c, :],
                               start=j == 0 and c == 0, stop=j == 3 and c == 1)
            mm.then_inc(m["y"].sem, 1)

        for i in range(S5T + 1):
            if i < S5T:
                drive(i)
            if i >= 1:
                out(i - 1)

    def scalar(self, act, st):
        k, m = self.k, self.m
        for i in range(S5T):
            act.wait_ge(*m["phase"].at(i + 1))
            if i >= 2:
                act.wait_ge(*m["h"].at(i - 1))
            r = self.tab[:, i % 2, 0, :]
            act.activation(self.tab[:, i % 2, 1, :], r, ACT.Sin, scale=SIN_TURN)
            act.activation(self.tab[:, i % 2, 2, :], r, ACT.Sin, scale=SIN_TURN / 2).then_inc(m["sin"].sem, 1)
        for q in range(4):
            act.wait_ge(*m["z"].at(q + 1))
            st(act.activation(self.z[:, q, :], self.z[:, q, :], ACT.Gelu_apprx_tanh))

    def vector(self, dve, st):
        k, m = self.k, self.m

        def do(ins):
            st(ins)
            st.wait()

        do(dve.memset(self.spread, 0.0))

        def phases(i):
            r, n = self.tab[:, i % 2, 0, :], self.rot[:, 6, :]
            f = self.turns[:, i:i + 1]
            if i >= 1:
                dve.wait_ge(*m["phase"].at(i))
            if i >= 2:
                dve.wait_ge(*m["sin"].at(i - 1))
            do(dve.tensor_scalar(n, k.con("time"), f, ROUND, ALU.mult, ALU.add))
            do(dve.tensor_scalar(n, n, ROUND, None, ALU.subtract))
            dve.scalar_tensor_tensor(r, k.con("time"), f, n, ALU.mult, ALU.subtract).then_inc(m["phase"].sem, 1)

        phases(0)
        for i in range(S5T):
            q, j = i // 4, i % 4
            if j == 0:
                if q >= 2:
                    dve.wait_ge(*m["y"].at(4 * (q - 1)))
                for c, name, sign in ((0, "s5_c_re", 1.0), (1, "s5_c_im", -1.0)):
                    src = k.par(name).rearrange("p (i h) -> p i h", h=16)
                    for jj in range(4):
                        for half in range(2):
                            rows, at = slice(64 * half, 64 * half + 64), 32 * jj + 16 * half
                            ins = dve.tensor_scalar(self.spread[rows, q % 2, c, jj, at:at + 16],
                                                    src[rows, 4 * q + jj, :], sign, None, ALU.mult)
                            if c == 1 and jj == 3 and half == 1:
                                ins.then_inc(m["c"].sem, 1)
                            else:
                                st(ins)
            if i + 1 < S5T:
                phases(i + 1)
            sin, cos = self.tab[:, i % 2, 1, :], self.tab[:, i % 2, 2, :]
            a, b, c_, d, gr, gi = (self.rot[:, n, :] for n in range(6))
            if i >= 1:
                dve.wait_ge(*m["h"].at(i))
            dve.wait_ge(*m["sin"].at(i + 1))
            do(dve.tensor_tensor(cos, cos, cos, ALU.mult))
            do(dve.tensor_scalar(cos, cos, -2.0, 1.0, ALU.mult, ALU.add))
            dve.wait_ge(*m["drive"].at(i + 1))
            dr, di = k.ps[:, i % 2, 0:TOK], k.ps[:, i % 2, TOK:2 * TOK]
            st(dve.tensor_tensor(a, dr, cos, ALU.mult))
            st(dve.tensor_tensor(b, di, sin, ALU.mult))
            st(dve.tensor_tensor(c_, di, cos, ALU.mult))
            dve.tensor_tensor(d, dr, sin, ALU.mult).then_inc(m["dused"].sem, 1)
            dve.wait_ge(*m["dused"].at(i + 1))
            st(dve.tensor_tensor(a, a, b, ALU.add))
            st(dve.tensor_tensor(c_, c_, d, ALU.subtract))
            st.wait()
            mag = self.mag[:, i:i + 1].broadcast_to([P, TOK])
            st(dve.tensor_tensor_scan(gr, mag, a, 0.0, ALU.mult, ALU.add))
            st(dve.tensor_tensor_scan(gi, mag, c_, 0.0, ALU.mult, ALU.add))
            st.wait()
            st(dve.tensor_tensor(a, gr, cos, ALU.mult))
            st(dve.tensor_tensor(b, gi, sin, ALU.mult))
            st(dve.tensor_tensor(c_, gr, sin, ALU.mult))
            st(dve.tensor_tensor(d, gi, cos, ALU.mult))
            st.wait()
            if i >= 2:
                dve.wait_ge(*m["y"].at(i - 1))
            st(dve.tensor_tensor(self.hh[:, i % 2, 0, :], a, b, ALU.subtract))
            dve.tensor_tensor(self.hh[:, i % 2, 1, :], c_, d, ALU.add).then_inc(m["h"].sem, 1)
        for q in range(4):
            dve.wait_ge(*m["y"].at(4 * q + 4))
            dve.scalar_tensor_tensor(self.z[:, q, :], self.uT[:, q, :], k.par("s5_d")[:, q:q + 1],
                                     k.ps[:, 4 + q, 0:TOK], ALU.mult, ALU.add).then_inc(m["z"].sem, 1)


class HgrnPrep(Stage):

    def __init__(self, k, f, b, tmp):
        super().__init__(k)
        self.f, self.b, self.tmp = f, b, tmp
        self.m = {"log_in": k.mark("log_in", 1)}

    def scalar(self, act, st):
        t, f = self.tmp, self.f
        st(act.activation(t, f, ACT.Abs))
        st.wait()
        st(act.activation(t, t, ACT.Exp, scale=-1.0))
        st.wait()
        act.activation(t, t, ACT.Ln, bias=self.k.con("ones")[:, 0:1]).then_inc(self.m["log_in"].sem, 1)

    def vector(self, dve, st):
        dve.wait_ge(*self.m["log_in"].at(1))
        st(dve.scalar_tensor_tensor(self.tmp, self.f, 0.0, self.tmp, ALU.min, ALU.subtract))
        st.wait()
        for c in range(2):
            for h in range(HGH):
                st(dve.tensor_tensor_scan(self.b[:, c, h, :], self.k.con("ones")[:, 0:P],
                                          self.tmp[:, h, c * P:(c + 1) * P], 0.0, ALU.mult, ALU.add))


class Hgrn(Stage):

    def __init__(self, k, qT, key, b, v, o, ar):
        super().__init__(k)
        self.q, self.key, self.b, self.v, self.o = qT, key, b, v, o
        self.arg, self.qs, self.ks = ar.take(2, 512), ar.take(2, 512), ar.take(2, 512)
        self.acc, self.part = ar.take(3, 512), ar.take(2, 512)
        self.LV = 8
        n = 2 * self.LV + 1
        self.n = n
        self.m = {"arg": k.mark("hg_args", n), "exp": k.mark("hg_exp", n), "ops": k.mark("hg_operands", n),
                  "prod": k.mark("hg_products", n), "took": k.mark("hg_taken", n), "o": k.mark("hg_out", 2)}

    def steps(self):
        i = 0
        for c in range(2):
            for m in (64, 32, 16, 8, 4, 2, 1, 0):
                yield i, c, m
                i += 1
        yield i, 1, -1

    def tensor(self, pe):
        k, m = self.k, self.m
        for i, c, half in self.steps():
            if i >= 2:
                pe.wait_ge(*m["took"].at(i - 1))
            pe.wait_ge(*m["ops"].at(i + 1))
            for h in range(HGH):
                at = slice(h * P, (h + 1) * P)
                mm = pe.matmul(k.ps[:, i % 2, at], self.ks[:, i % 2, at], self.qs[:, i % 2, at], start=True,
                               stop=True)
            mm.then_inc(m["prod"].sem, 1)
        pe.wait_ge(*m["took"].at(self.n))
        for t in range(TT):
            parts = [(self.acc[:, 0, :], 0)] if t == 0 else [(self.acc[:, 2, :], 0), (self.acc[:, 1, :], 1)]
            for h in range(HGH):
                at = slice(h * P, (h + 1) * P)
                for n, (w, s) in enumerate(parts):
                    mm = pe.matmul(k.ps[:, 4 + t, at], w[:, at], self.v[:, s, at], start=n == 0,
                                   stop=n == len(parts) - 1)
            mm.then_inc(m["o"].sem, 1)

    def scalar(self, act, st):
        m = self.m
        for i, c, half in self.steps():
            act.wait_ge(*m["arg"].at(i + 1))
            a = self.arg[:, i % 2, :]
            if half == -1:
                st(act.activation(self.b[:, 1], self.b[:, 1], ACT.Exp))
            act.activation(a, a, ACT.Exp).then_inc(m["exp"].sem, 1)
        act.wait_ge(*m["o"].at(1))
        st(act.activation(self.o[:, 0, :], self.k.ps[:, 4, :], ACT.Identity))

    def vector(self, dve, st):
        k, m = self.k, self.m
        tok = lambda a, c: a[:, :, c * P:(c + 1) * P]
        flat = lambda a: a.rearrange("p h t -> p (h t)")

        def blocks(a, half):
            return a.rearrange("p (n u m) -> p n u m", u=2, m=half)

        st(dve.memset(self.qs, 0.0))
        st(dve.memset(self.ks, 0.0))
        st.wait()

        def args(i, c, half):
            a = self.arg[:, i % 2, :]
            if half > 0:
                b, a4 = blocks(flat(self.b[:, c]), half), blocks(a, half)
                mid = b[:, :, 0, half - 1:half].broadcast_to([P, 256 // half, half])
                st(dve.tensor_tensor(a4[:, :, 1, :], b[:, :, 1, :], mid, ALU.subtract))
                dve.tensor_tensor(a4[:, :, 0, :], mid, b[:, :, 0, :], ALU.subtract).then_inc(m["arg"].sem, 1)
            elif half == 0:
                dve.memset(a, 0.0).then_inc(m["arg"].sem, 1)
            else:
                b = self.b[:, 0]
                end = b[:, :, P - 1:P].broadcast_to([P, HGH, P])
                dve.tensor_tensor(a.rearrange("p (h t) -> p h t", h=HGH), end, b, ALU.subtract) \
                   .then_inc(m["arg"].sem, 1)

        def operands(i, c, half):
            a, qs, ks = self.arg[:, i % 2, :], self.qs[:, i % 2, :], self.ks[:, i % 2, :]
            dve.wait_ge(*m["exp"].at(i + 1))
            if i >= 2:
                dve.wait_ge(*m["prod"].at(i - 1))
            heads = lambda x: x.rearrange("p (h t) -> p h t", h=HGH)
            if half > 0:
                bl = lambda x: x.rearrange("p h (n u m) -> p h n u m", u=2, m=half)
                st(dve.tensor_tensor(bl(heads(qs))[:, :, :, 1, :], bl(tok(self.q, c))[:, :, :, 1, :],
                                     bl(heads(a))[:, :, :, 1, :], ALU.mult))
                dve.tensor_tensor(bl(heads(ks))[:, :, :, 0, :], bl(tok(self.key, c))[:, :, :, 0, :],
                                  bl(heads(a))[:, :, :, 0, :], ALU.mult).then_inc(m["ops"].sem, 1)
            elif half == 0:
                st(dve.tensor_copy(heads(qs), tok(self.q, c)))
                dve.tensor_copy(heads(ks), tok(self.key, c)).then_inc(m["ops"].sem, 1)
            else:
                st(dve.tensor_tensor(heads(ks), tok(self.key, 0), heads(a), ALU.mult))
                dve.tensor_tensor(heads(qs), tok(self.q, 1), self.b[:, 1], ALU.mult).then_inc(m["ops"].sem, 1)

        def take(i, c, half):
            dve.wait_ge(*m["prod"].at(i + 1))
            ps = k.ps[:, i % 2, :].rearrange("p (h t) -> p h t", h=HGH)
            lv = i % self.LV
            if half == -1:
                dve.tensor_copy(self.acc[:, 2, :], k.ps[:, i % 2, :]).then_inc(m["took"].sem, 1)
                return
            mask = k.con("levels")[:, lv * P:(lv + 1) * P].unsqueeze(1).broadcast_to([P, HGH, P])
            acc = self.acc[:, c, :]
            dst = acc if lv == 0 else self.part[:, i % 2, :]
            dve.tensor_tensor(dst.rearrange("p (h t) -> p h t", h=HGH), ps, mask, ALU.mult) \
               .then_inc(m["took"].sem, 1)
            if lv:
                dve.wait_ge(*m["took"].at(i + 1))
                st(dve.tensor_tensor(acc, acc, self.part[:, i % 2, :], ALU.add))
                st.wait()

        todo = list(self.steps())
        args(*todo[0])
        for n, step in enumerate(todo):
            if n + 1 < len(todo):
                if n >= 1:
                    dve.wait_ge(*m["ops"].at(n))
                args(*todo[n + 1])
            operands(*step)
            if n >= 1:
                take(*todo[n - 1])
        take(*todo[-1])
        dve.wait_ge(*m["o"].at(2))
        st(dve.tensor_copy(self.o[:, 1, :], k.ps[:, 5, :]))


def in2_stage(k, fqk, fv, suT, hqT, fT, key, hi, hg, gl):
    def silu_pair(dst, rows):
        def act_out(act, st, i, bank):
            if rows:
                return act.activation(dst[:, 0, i * CN:(i + 1) * CN], bank, ACT.Silu)
            return act.activation(dst[:, 0:2, :], bank.rearrange("p (a b) -> p a b", a=2), ACT.Silu)

        def dve_out(dve, st, i, bank):
            if rows:
                return dve.tensor_copy(dst[:, 1, i * CN:(i + 1) * CN], bank)
            return dve.tensor_copy(dst[:, 2:4, :], bank.rearrange("p (a b) -> p a b", a=2))
        return act_out, dve_out

    def gate_act(act, st, i, bank):
        return act.activation(gl[:, 0, i * CN:(i + 1) * CN], bank, ACT.Sigmoid)

    def gate_dve(dve, st, i, bank):
        return dve.tensor_copy(gl[:, 1, i * CN:(i + 1) * CN], bank)

    first = k.groups

    def act_after(act, st, i):
        def copied(g):
            act.wait_ge(k.dve_took, k.dve_groups[first + g + 1])
        if i == 7:
            copied(4)
            st(act.activation(hqT[:, 2:4, :], hqT[:, 2:4, :], ACT.Silu))
            copied(7)
            st(act.activation(hg[:, 1, :], hg[:, 1, :], ACT.Silu))
        if i == 8:
            copied(5)
            st(act.activation(key[:, :, :], fT[:, :, :], ACT.Sigmoid, scale=-1.0))
        if i == 13:
            copied(13)
            st(act.activation(gl[:, 1, :], gl[:, 1, :], ACT.Sigmoid))

    outs = by_ranges((2, to_rows(fqk)), (1, to_rows(fv)), (1, to_features(suT)), (1, silu_pair(hqT, False)),
                     (1, to_features(fT)), (1, to_rows(hi)), (1, silu_pair(hg, True)), (6, (gate_act, gate_dve)))
    return Product(k, "in2", k.hT, *outs, act_after, None)


class DveProduct(Product):

    def __init__(self, k, name, src, take):
        super().__init__(k, name, src, None, None)
        self.take = take

    def vector(self, dve, st):
        for i in range(len(self.groups)):
            dve.wait_ge(self.k.chunk_used, self.chunk_end(i))
            b = 2 * ((self.first_group + i) % 2)
            self.take(dve, st, i, self.k.ps[:, b:b + 2, :]).then_inc(self.k.dve_took, 1)


def add_to_x(k):
    def take(dve, st, i, banks):
        at = slice(i * CN, (i + 1) * CN)
        return dve.tensor_tensor(k.x[:, :, at], k.x[:, :, at], banks, ALU.add)
    return take


def branch(k, name, src, gl, n):
    def take(dve, st, i, banks):
        at = slice(n * D + i * CN, n * D + (i + 1) * CN)
        if n == 0:
            return dve.tensor_tensor(gl[:, :, at], gl[:, :, at], banks, ALU.mult)
        st(dve.tensor_tensor(gl[:, :, at], gl[:, :, at], banks, ALU.mult))
        st.wait()
        to = slice(i * CN, (i + 1) * CN)
        return dve.tensor_tensor(gl[:, :, to], gl[:, :, to], gl[:, :, at], ALU.add)
    return DveProduct(k, name, src, take)


class LoadMem(Stage):
    def __init__(self, k, dst, mem):
        super().__init__(k)
        self.dst, self.mem = dst, mem
        self.m = k.mark("mem_loaded", 16)

    def gpsimd(self, pool, st):
        pool.dma_start(self.dst, self.mem[0].rearrange("(t p) d -> p t d", p=P)).then_inc(self.m.sem, 16)

    def scalar(self, act, st):
        act.wait_ge(*self.m.at(16))


def block2_stages(k, base, small, mem):
    ar = k.arena
    ar.rest(base)
    fqk, fv = ar.take(TT, D), ar.take(TT, 512)
    suT, hqT, fT, key = (ar.take(4, TOK) for _ in range(4))
    hi, hg, gl = ar.take(TT, 512), ar.take(TT, 512), ar.take(TT, 3 * D)
    foxT = ar.take(4, TOK)
    work = ar.at
    xh = ar.take(TT, D)
    ar.rest(work)
    tmp, negc, fo, sm = ar.take(3, TOK), ar.take(1, TOK)[:, 0, :], ar.take(TT, 512), ar.take(8, 16)
    sm4 = sm.rearrange("p a b -> p (a b)").rearrange("p (a t h) -> p a t h", a=4, t=TT)
    stages = [
        Norm(k, k.x, KD, k.hT, k.par("norm_mix"), None, xh, small),
        in2_stage(k, fqk, fv, suT, hqT, fT, key, hi, hg, gl),
    ]
    at_att = ar.at
    sqf = ar.take(TT, D)
    ar.rest(at_att)
    stages += [
        ForgetGate(k, tmp, negc),
        HeadScale(k, fqk, 16, 64, [(0, 8, HP ** -0.5), (8, 16, 1.0)], sqf, sm4),
    ]
    ar.rest(at_att)
    qkT = ar.take(8, TOK)
    stages.append(Turn(k, fqk, 8, qkT, scale=lambda f: k.par("fox_qnorm" if f < 4 else "fox_knorm")))

    def lead(pe, h, bank):
        pe.matmul(bank, k.mask_bf[:, 10 * P:11 * P], k.mask_bf[:, 6 * P:10 * P], start=True, stop=False,
                  skip_group_check=True)
        pe.matmul(bank, k.con("ident")[0:32, h:h + 1].broadcast_to([32, P]),
                  negc[0:32, :].unsqueeze(1).broadcast_to([32, 2, TOK]), start=False, stop=False,
                  skip_group_check=True)

    fox = Attention(k, FOXH, 64,
                    lambda h, t: [qkT[64 * (h % 2):64 * (h % 2) + 64, h // 2, t * P:(t + 1) * P]],
                    lambda h: [qkT[64 * (h % 2):64 * (h % 2) + 64, 4 + h // 2, :]],
                    lambda h, s: fv[:, s, h * 64:(h + 1) * 64], fo, ar,
                    lead=lead)
    stages += [fox, Turn(k, fo, 4, foxT)]

    ar.rest(base)
    turns, mag, z = ar.take(1, 16)[:, 0, :], ar.take(1, 16)[:, 0, :], ar.take(4, TOK)
    rot = region(k, ar.at).take(7, TOK)
    v, bb = ar.take(15, 16), ar.take(3, S5T, 16)
    ar.rest(work)
    bT = ar.take(2, S5T * P).rearrange("p c (i s) -> p c i s", i=S5T)
    spread = ar.take(2, 2 * 4 * P).rearrange("p a (c j s) -> p a c j s", c=2, j=4)
    tab = ar.take(2, 3, TOK)
    hh = ar.take(2, 2, TOK)
    stages += [
        S5Prep(k, v, bb, spread[:, :, 0], bT, mag, turns),
        S5(k, suT, bT, mag, turns, spread, tab, rot, hh, z, None),
    ]
    s5T = suT

    def glu_act(act, st, i, bank):
        for f in range(2):
            ins = act.activation(s5T[:, f, :], bank[:, f * TOK:(f + 1) * TOK], ACT.Sigmoid,
                                 bias=k.par("s5_b_glu")[:, f:f + 1])
            if f == 0:
                st(ins)
        return ins

    def glu_dve(dve, st, i, bank):
        for f in range(2):
            ins = dve.tensor_scalar(s5T[:, 2 + f, :], bank[:, f * TOK:(f + 1) * TOK],
                                    k.par("s5_b_glu")[:, 2 + f:3 + f], None, ALU.add)
            if f == 0:
                st(ins)
        return ins

    first = k.groups

    def glu_act_after(act, st, i):
        act.wait_ge(k.dve_took, k.dve_groups[first + 1])
        st(act.activation(s5T[:, 2:4, :], s5T[:, 2:4, :], ACT.Sigmoid))

    class GluMul(Stage):

        def vector(self, dve, st):
            st(dve.tensor_tensor(s5T, s5T, z, ALU.mult))

    stages += [Product(k, "glu", z, glu_act, glu_dve, glu_act_after, None), GluMul(k)]

    ar.rest(work)
    b = ar.take(2, HGH, P)
    ho, hT4 = ar.take(TT, 512), ar.take(4, TOK)
    dead = ar.at
    htmp = ar.take(4, TOK)
    ar.rest(dead)
    sm2, hsq = ar.take(4, TT, HGH), ar.take(TT, 512)
    ar.rest(dead)
    stages += [
        HgrnPrep(k, fT, b, htmp),
        Hgrn(k, hqT, key, b, hi, ho, ar),
        HeadScale(k, ho, HGH, 128, [(0, 4, 1.0)], hsq, sm2, extra=hg),
        Turn(k, ho, 4, hT4, scale=lambda f: k.par("hg_onorm")),
        branch(k, "fox_out", foxT, gl, 0),
        branch(k, "s5_out", s5T, gl, 1),
        branch(k, "hg_out", hT4, gl, 2),
        Turn(k, gl[:, :, 0:D], 8, k.hT),
        DveProduct(k, "mix_out", k.hT, add_to_x(k)),
    ]

    ar.rest(base)
    mt, mT = ar.take(TT, D), ar.take(8, TOK)
    xk, xv, xq, xo, sq2, xh2 = (ar.take(TT, D) for _ in range(6))
    sm3 = ar.take(4, TT, 4)
    qT, kT = sq2.rearrange("p a b -> p (a b)").rearrange("p (a b) -> p a b", b=TOK), mT
    stages += [
        LoadMem(k, mt, mem),
        Norm(k, mt, KD, mT, k.par("norm_mem"), None, xh2, small),
        Product(k, "xk", mT, *to_rows(xk)),
        Product(k, "xv", mT, *to_rows(xv)),
        Norm(k, k.x, KD, k.hT, k.par("norm_x"), None, xh2, small),
        Product(k, "xq", k.hT, *to_rows(xq)),
        HeadScale(k, xk, 4, 256, [(0, 4, 1.0)], sq2, sm3),
        HeadScale(k, xq, 4, 256, [(0, 4, 256.0 ** -0.5)], sq2, sm3),
        Turn(k, xk, 8, kT, scale=lambda f: k.par("x_knorm")[:, f % 2:f % 2 + 1]),
        Turn(k, xq, 8, qT, scale=lambda f: k.par("x_qnorm")[:, f % 2:f % 2 + 1]),
        Attention(k, 4, 256,
                  lambda h, t: [qT[:, 2 * h + i, t * P:(t + 1) * P] for i in range(2)],
                  lambda h: [kT[:, 2 * h + i, :] for i in range(2)],
                  lambda h, s: xv[:, s, h * 256:(h + 1) * 256], xo, ar),
        Turn(k, xo, 8, k.hT),
        DveProduct(k, "xo", k.hT, add_to_x(k)),
    ]

    ar.rest(base)
    u, xh3 = ar.take(FF2T, TOK), ar.take(TT, D)
    swi = k.groups

    def a_act(act, st, i, bank):
        return act.activation(u[:, 2 * i:2 * i + 2, :], bank.rearrange("p (a b) -> p a b", a=2), ACT.Silu)

    def b_dve(dve, st, i, bank):
        dve.wait_ge(k.act_took, k.act_groups[swi + i + 1])
        dst = u[:, 2 * i:2 * i + 2, :]
        return dve.tensor_tensor(dst, dst, bank.rearrange("p (a b) -> p a b", a=2), ALU.mult)

    stages += [
        Norm(k, k.x, KD, k.hT, k.par("norm_ffn"), None, xh3, small),
        Product(k, "gate_up", k.hT, a_act, b_dve),
        DveProduct(k, "swi_down", u, add_to_x(k)),
    ]
    return stages


def all_stages(k, norm_g, ada_b, mem):
    ar = k.arena
    small, cond, mod, gains = ar.take(1, 64), ar.take(1, KD), ar.take(4, KD), ar.take(2, D)
    small, cond = small[:, 0, :], cond[:, 0, :]
    base = ar.at
    stages = [Setup(k, cond)]

    zs = ar.take(TT, D)
    at_b = ar.at
    xp, xc = ar.take(12, TOK + 4), ar.take(12, TOK)
    at_c = ar.at
    qT, kT, v = ar.take(8, TOK), ar.take(8, TOK), ar.take(TT, D)
    at_d = ar.at
    xf, xb = ar.take(TT, D), ar.take(TT, D)
    at_e = ar.at
    cbf, cbb = ar.take(2, 3 * P), ar.take(2, 3 * P)
    cs4, csn, dtc, tmp = ar.take(1, 512)[:, 0, :], ar.take(TT, 64), ar.take(TT, 64), ar.take(5, TOK)
    ar.rest(at_b)
    xt = ar.take(TT, D)
    ar.rest(at_b + 12 * (TOK + 4))
    e = ar.take(4, 3 * P)
    ar.rest(at_c)
    xh = ar.take(TT, D)
    ar.rest(at_d)
    yT = ar.take(16, TOK)
    ar.rest(at_b)
    table = ar.take(1, NH * 6 * GRID)[:, 0, :]
    ar.rest(at_b)
    y = ar.take(TT, D)
    junk = ar.take(TT, D)
    ar.rest(at_e)
    stages += [
        Ada(k, 0, cond, mod, gains, xf, norm_g, ada_b),
        Pads(k, xp),
        Norm(k, k.x, KD, k.hT, mod[:, 1, :], mod[:, 0, :], xh, small),
        in0_stage(k, xp, xc, zs, qT, kT, v),
        SsdPrep(k, xc, xt, xf, xb, cbf, cbb, cs4, csn, dtc, tmp),
        Ssd(k, xt, xf, xb, cbf, cbb, cs4, csn, zs, e),
        Norm(k, zs, KD, yT[:, 0:8, :], k.par("ssd_norm"), None, xt, small),
        BiasTable(k, table),
        Attention(k, NH, HP,
                  lambda h, t: [qT[64 * (h % 2):64 * (h % 2) + 64, h // 2, t * P:(t + 1) * P]],
                  lambda h: [kT[64 * (h % 2):64 * (h % 2) + 64, h // 2, :]],
                  lambda h, s: v[:, s, h * HP:(h + 1) * HP], zs, ar,
                  table=lambda h, t: table.rearrange("p (h u c) -> p h (u c)", h=NH, u=6)
                  [:, h, GRID * (2 - 2 * t):GRID * (6 - 2 * t)]),
        Turn(k, zs, KD, yT[:, 8:16, :]),
        Product(k, "out0", yT, *to_rows(y)),
        Post(k, y, gains[:, 0, :], junk, small),
    ]
    stages += mlp(k, 0, mod, gains, base, small)
    stages += layer1_stages(k, cond, mod, gains, base, small, norm_g, ada_b)
    stages += block2_stages(k, 64 + KD, small, mem)
    return stages


def mlp(k, layer, mod, gains, base, small):
    ar = k.arena
    ar.rest(base)
    u, y, xh = ar.take(32, TOK), ar.take(TT, D), ar.take(TT, D)
    return [Norm(k, k.x, KD, k.hT, mod[:, 3, :], mod[:, 2, :], xh, small),
            *mlp_stages(k, layer, u, y),
            Post(k, y, gains[:, 1, :], xh, small)]


def program(nc, x, stream, params, consts, narrow, norm_g, ada_b, mem, out, where_p, where_c):
    with ExitStack() as ctx:
        k = Core(nc, ctx, params.shape[1], consts.shape[1], narrow.shape, where_p, where_c)
        stages = all_stages(k, norm_g, ada_b, mem)
        result = k.x[:, :, :]
        steps = {n: k.sem(f"{n}_steps") for n in ("act", "dve", "pool")}
        out_stored = k.sem("out_stored")
        block = ctx.enter_context(nc.Block())

        def meet(eng, n):
            eng.drain().then_inc(k.stage_done, 1)
            eng.wait_ge(k.stage_done, 3 * (n + 1))

        @block.sync
        def _(sp):
            sp.dma_start(k.par_all[:, :], params).then_inc(k.inputs_in, 16)
            sp.dma_start(k.con_all[:, :], consts).then_inc(k.inputs_in, 16)
            sp.dma_start(k.x[:, :, :], x[0].rearrange("(t p) d -> p t d", p=P)).then_inc(k.inputs_in, 16)
            sp.dma_start(k.narrow[:, :, :], narrow).then_inc(k.inputs_in, 16)

            def load(c, slot):
                sp.dma_start(k.ring[:, slot, :, :], stream[c]).then_inc(k.loaded[slot], 16)

            for c in range(min(RING, k.chunks)):
                load(c, c)
            rounds = (k.chunks - RING) // RING
            if rounds > 0:
                with sp.Fori(1, 1 + rounds) as r:
                    for slot in range(RING):
                        sp.wait_ge(k.chunk_used, r * RING + (slot - RING + 1))
                        load(r * RING + slot, slot)
            for c in range(RING * (1 + max(rounds, 0)), k.chunks):
                sp.wait_ge(k.chunk_used, c - RING + 1)
                load(c, c % RING)
            sp.wait_ge(k.stage_done, 3 * len(stages))
            sp.dma_start(out[0].rearrange("(t p) d -> p t d", p=P), result).then_inc(out_stored, 16)
            sp.wait_ge(out_stored, 16)

        @block.tensor
        def _(pe):
            for n, stage in enumerate(stages):
                stage.tensor(pe)
                meet(pe, n)

        @block.scalar
        def _(act):
            st = Steps(act, steps["act"])
            for n, stage in enumerate(stages):
                stage.scalar(act, st)
                meet(act, n)

        @block.vector
        def _(dve):
            st = Steps(dve, steps["dve"])
            for n, stage in enumerate(stages):
                stage.vector(dve, st)
                meet(dve, n)

        @block.gpsimd
        def _(pool):
            st = Steps(pool, steps["pool"])
            for n, stage in enumerate(stages):
                stage.gpsimd(pool, st)
                pool.wait_ge(k.stage_done, 3 * (n + 1))


def kernel(**inputs):
    import concourse.bacc as bacc
    from concourse.bass_utils import run_bass_kernel_spmd as run

    I = {n: np.asarray(a) for n, a in inputs.items()}
    params, where_p = pack_params(I)
    consts, where_c = constants()
    arrays = {"x": I["x"], "stream": pack_stream(I), "params": params, "consts": consts,
              "narrow": pack_narrow(I), "norm_g": I["norm_g"], "ada_b": I["ada_b"], "mem": I["mem_2"]}
    arrays = {n: np.ascontiguousarray(a) for n, a in arrays.items()}
    nc = bacc.Bacc("TRN2", target_bir_lowering=False, num_devices=1)
    args = [nc.dram_tensor(n, a.shape, mybir.dt.from_np(a.dtype), kind="ExternalInput").ap()
            for n, a in arrays.items()]
    out = nc.dram_tensor("out", (1, TOK, D), F32, kind="ExternalOutput").ap()
    program(nc, *args, out, where_p, where_c)
    return run(nc, [arrays], core_ids=[0]).results[0]["out"]
```

```python
from contextlib import ExitStack

import numpy as np

import concourse.bass as bass
from concourse import mybir

F32 = mybir.dt.float32
BF16 = mybir.dt.bfloat16
F32R = mybir.dt.float32r
I32 = mybir.dt.int32
ALU = mybir.AluOpType
ACT = mybir.ActivationFunctionType
AX = mybir.AxisListType.X

P = 128
TOK = 256
TT = TOK // P
D = 1024
KD = D // P
CK = 4
CN = 512
HI = 3
ARENA = 23392
RING = 5
AHEAD = 2 * RING
EPS = 1e-6
NEG = -1e30
NH = 16
HP = 64
FF1 = 4096
MH, MDK, MDV = 8, 128, 256
FOXH = 8
HGH = 4
S5T = 16
FF2T = 22
GRID = 64


def tiles_of(c0, n=CN):
    return [c0 + P * i for i in range(n // P)]


def groups(kind, c0, c1):
    return [(kind, tiles_of(c)) for c in range(c0, c1, CN)]


def ada_groups(layer, part0, part1):
    return [(("ada_w", layer), cols) for _, cols in groups("", part0 * D, part1 * D)]


def woven(own, guests):
    out, places = [], len(own) - 1
    for i, g in enumerate(own):
        out.append(g)
        out += guests[len(guests) * i // places:len(guests) * (i + 1) // places] if i < places else []
    return out


PRODUCTS = [
    ("ada", None, 0, KD, ada_groups(0, 0, 2)),
    ("in0", "ab_w_in", 0, KD,
     woven(groups("feat", 1024, 2560) + groups("tok", 0, 1024) + groups("feat", 2592, 4640)
           + groups("tok", 4640, 5664), ada_groups(0, 2, 6))),
    ("out0", "ab_w_out", 0, 16, groups("tok", 0, D)),
    ("up0", "mlp_w1", 0, KD, woven(groups("feat", 0, FF1), ada_groups(1, 0, 2))),
    ("down0", "mlp_w2", 0, FF1 // P, groups("tok", 0, D)),
    ("in1", "ml_w_in", 0, KD, woven(groups("feat", 0, 2048) + groups("tok", 2048, 6144), ada_groups(1, 2, 6))),
    ("out1", "ml_w_out", 0, 16, groups("tok", 0, D)),
    ("up1", "mlp_w1", 1, KD, groups("feat", 0, FF1)),
    ("down1", "mlp_w2", 1, FF1 // P, groups("tok", 0, D)),
    ("in2", "w_in_2", 0, KD, groups("tok", 0, 1536) + groups("feat", 1544, 3080)
     + groups("tok", 3080, 7176)),
    ("glu", "s5_w_glu_2", 0, 4, groups("feat", 0, 512)),
    ("fox_out", "w_branch_2", 0, 4, groups("tok", 0, D)),
    ("s5_out", "w_branch_2", 0, 4, groups("tok", 0, D)),
    ("hg_out", "w_branch_2", 0, 4, groups("tok", 0, D)),
    ("mix_out", "w_out_2", 0, KD, groups("tok", 0, D)),
    ("xk", "xk_2", 0, KD, groups("tok", 0, D)),
    ("xv", "xv_2", 0, KD, groups("tok", 0, D)),
    ("xq", "xq_2", 0, KD, groups("tok", 0, D)),
    ("xo", "xo_2", 0, KD, groups("tok", 0, D)),
    ("gate_up", "w_gate_up_2", 0, KD,
     [("feat", [256 * j, 256 * j + P, FF2T * P + 256 * j, FF2T * P + 256 * j + P]) for j in range(FF2T // 2)]),
    ("swi_down", "w_down_2", 0, FF2T, groups("tok", 0, D)),
]
ROW0 = {"s5_out": 512, "hg_out": 1024}


def is_guest(kind):
    return isinstance(kind, tuple)


def place(name, n):
    kinds = [kind for p in PRODUCTS if p[0] == name for kind, _ in p[4]]
    return [i for i, kind in enumerate(kinds) if not is_guest(kind)][n]


def chunks_of(kt):
    return [(k, min(CK, kt - k)) for k in range(0, kt, CK)]


def pack_stream(inputs):
    out = []
    for name, weight, layer, kt, grps in PRODUCTS:
        for kind, cols in grps:
            wn, ly = kind if is_guest(kind) else (weight, layer)
            w = inputs[wn][ly][ROW0.get(name, 0):]
            for k0, nk in chunks_of(kt):
                c = np.zeros((P, CK, CN), np.float32)
                for i, col in enumerate(cols):
                    blk = w[k0 * P:(k0 + nk) * P, col:col + P].reshape(nk, P, P)
                    c[:, :nk, i * P:(i + 1) * P] = blk.transpose(1, 0, 2)
                out.append(c)
    return np.stack(out)


def cols(v):
    return np.ascontiguousarray(np.asarray(v).reshape(-1, P).T)


def pad_rows(v, n=64):
    c = np.zeros((P, 1), np.float32)
    c[0:v.shape[1], 0] = v[0]
    c[32:32 + v.shape[1], 0] = v[1]
    return c


def pack_params(I):
    parts = {"c": cols(I["c"][0])}
    for l in range(2):
        for j in range(4):
            parts[f"norm{l}{j}"] = cols(I["norm_g"][l, j])
        for j in range(6):
            parts[f"ada_b{l}{j}"] = cols(I["ada_b"][l, j * D:(j + 1) * D])
    parts["conv_w"] = np.concatenate([cols(I["ab_conv_w"][0, i]) for i in range(5)], 1)
    parts["conv_b"] = cols(I["ab_conv_b"][0])
    parts["dt_bias"] = pad_rows(I["ab_dt_bias"][0])
    parts["a_log"] = pad_rows(I["ab_a_log"][0])
    parts["d_skip"] = np.broadcast_to(I["ab_d_skip"][0], (P, NH))
    rpb = np.zeros((P, NH, 7), np.float32)
    rpb[0:31] = I["ab_rpb"][0][:, 4:11, :].transpose(2, 0, 1)
    parts["rpb"] = rpb.reshape(P, NH * 7)
    parts["ssd_norm"] = cols(I["ab_ssd_norm"][0])
    parts["gate_i"] = pad_rows(I["ml_gate_b"][0, 0::2])
    parts["gate_f"] = pad_rows(I["ml_gate_b"][0, 1::2])
    parts["head_norm"] = cols(I["ml_head_norm"][0])
    for n in ("norm_mix", "norm_x", "norm_mem", "norm_ffn"):
        parts[n] = cols(I[n + "_2"][0])
    for n in ("fox_qnorm", "fox_knorm"):
        parts[n] = np.tile(I[n + "_2"][0], 2)[:, None]
    parts["fbias"] = np.pad(I["fox_fbias_2"][0], (0, P - FOXH))[:, None]
    for n in ("x_qnorm", "x_knorm"):
        parts[n] = cols(I[n + "_2"][0])
    parts["hg_onorm"] = I["hg_onorm_2"][0][:, None]
    for n in ("s5_a_re", "s5_a_im"):
        parts[n] = cols(I[n + "_2"][0])
    parts["s5_log_dt"] = cols(np.repeat(I["s5_log_dt_2"][0], 64))
    for n in ("s5_b_re", "s5_b_im"):
        parts[n] = I[n + "_2"][0].reshape(S5T, P, 16).transpose(1, 0, 2).reshape(P, -1)
    for n in ("s5_c_re", "s5_c_im"):
        parts[n] = I[n + "_2"][0].transpose(0, 2, 1).reshape(S5T, P, 16).transpose(1, 0, 2).reshape(P, -1)
    parts["s5_d"] = cols(I["s5_d_2"][0])
    parts["s5_b_glu"] = cols(I["s5_b_glu_2"][0])
    at, where = 0, {}
    for n, a in parts.items():
        where[n] = (at, a.shape[1])
        at += a.shape[1]
    return np.concatenate([np.asarray(a, np.float32) for a in parts.values()], 1), where


def pack_narrow(I):
    dt = np.zeros((D, 64), np.float32)
    w = I["ab_w_in"][0][:, 2560:2592]
    dt[:, 0:NH], dt[:, 32:32 + NH] = w[:, 0:NH], w[:, NH:]
    gates = np.zeros((D, 128), np.float32)
    w = I["ml_w_in"][0][:, 6144:6176]
    for j, at in enumerate((0, 64, 32, 96)):
        gates[:, at:at + MH] = w[:, MH * j:MH * j + MH]
    fox = np.zeros((D, 32), np.float32)
    fox[:, 0:FOXH] = I["w_in_2"][0][:, 1536:1544]
    w = np.concatenate([dt, gates, fox], 1)
    return np.ascontiguousarray(w.reshape(KD, P, 224).transpose(1, 0, 2))


def constants():
    p, f = np.arange(P)[:, None], np.arange(P)[None, :]
    up = np.where(f >= p, 0.0, NEG)
    lo = np.where(f <= p, 0.0, NEG)
    zero, none = np.zeros((P, P)), np.full((P, P), NEG)
    levels = [((p // (2 * m) == f // (2 * m)) & (p % (2 * m) < m) & (f % (2 * m) >= m)) * 1.0
              for m in (64, 32, 16, 8, 4, 2, 1)]
    toe = np.zeros((P, 192))
    for x in range(31):
        toe[x, 78 - x] = toe[x, 142 - x] = 1.0
    c = np.arange(P)[:, None] % GRID
    kc = np.arange(GRID)[None, :]
    start = np.clip(c - 8, 0, GRID - 16)
    window = np.where((kc >= start) & (kc < start + 16), 0.0, NEG)
    parts = {
        "ident": np.eye(P), "levels": np.concatenate(levels + [np.eye(P)], 1), "toeplitz": toe,
        "window": window, "time": np.broadcast_to(np.arange(TOK), (P, TOK)), "ones": np.ones((P, TOK)),
        "mask_f": np.concatenate([up, zero, up], 1), "mask_b": np.concatenate([lo, zero, lo], 1),
        "mask_q": np.concatenate([lo, none, zero, lo], 1),
    }
    at, where = 0, {}
    for n, a in parts.items():
        where[n] = (at, a.shape[1])
        at += a.shape[1]
    return np.concatenate([np.asarray(a, np.float32) for a in parts.values()], 1), where


class Mark:

    def __init__(self, sem, before):
        self.sem, self.before = sem, before

    def at(self, n):
        return self.sem, self.before + n


class Steps:

    def __init__(self, eng, sem):
        self.eng, self.sem, self.n = eng, sem, 0

    def __call__(self, ins):
        ins.then_inc(self.sem, 1)
        self.n += 1

    def wait(self):
        self.eng.wait_ge(self.sem, self.n)


class Arena:

    def __init__(self, tensor):
        self.t, self.at, self.size = tensor, 0, tensor.shape[1]

    def rest(self, n):
        self.at = n

    def take(self, *shape):
        n = int(np.prod(shape))
        a = self.t[:, self.at:self.at + n]
        self.at += n
        assert self.at <= self.size, (self.at, self.size)
        if len(shape) == 2:
            a = a.rearrange("p (a b) -> p a b", b=shape[1])
        elif len(shape) == 3:
            a = a.rearrange("p (a b c) -> p a b c", b=shape[1], c=shape[2])
        return a


def region(k, at):
    a = Arena(k.arena.t)
    a.rest(at)
    return a


class Operand:

    def __init__(self, f, hi, lo):
        self.f, self.hi, self.lo = f, hi, lo


def operand(k, at, tiles, hi_at):
    view = lambda t, c: t[:, c:c + tiles * TOK].rearrange("p (a b) -> p a b", b=TOK)
    return Operand(view(k.arena.t, at), view(k.arena_lo, hi_at), view(k.arena_lo, at))


class Core:

    def __init__(self, nc, ctx, params, consts, narrow_shape, where_p, where_c):
        self.nc, self.ctx = nc, ctx
        sb = lambda name, shape, dt=F32: ctx.enter_context(nc.sbuf_tensor(name, shape, dt))
        self.x = sb("x_res", [P, TT, D])
        self.par_all = sb("par", [P, params])
        self.con_all = sb("con", [P, consts])
        self.narrow = sb("narrow_w", list(narrow_shape))
        self.mask_bf = sb("mask_bf", [P, 10 * P + P], BF16)
        self.w_hi = sb("w_hi", [P, HI, CK, CN], F32R)
        self.h_hi = sb("h_hi", [P, KD, TOK], F32R)
        self.cond = sb("cond", [P, KD])
        self.ones = sb("ones", [P, 2])
        at = -(-nc.sbuf_base // 32) * 32
        sizes = (("ring", [P, RING, CK, CN]), ("hT", [P, KD, TOK]), ("arena", [P, ARENA]))
        sb("in_place", [P, sum(int(np.prod(s[1:])) for _, s in sizes) + 32])
        views = {}
        for name, shape in sizes:
            for tag, dt in (("", F32), ("_lo", F32R)):
                views[name + tag] = nc.alloc_sbuf_tensor_at(name + "_at" + tag, shape, dt, offset=at)
            at += 4 * int(np.prod(shape[1:]))
        self.ring, self.w_lo = views["ring"], views["ring_lo"]
        self.hT, self.h_lo = views["hT"], views["hT_lo"]
        self.arena, self.arena_lo = Arena(views["arena"]), views["arena_lo"]
        self.guest_acc = self.arena.t[:, ARENA - 2 * CN:ARENA].rearrange("p (a b) -> p a b", a=2)
        self.hT_operand = Operand(self.hT[:, :, :], self.h_hi[:, :, :], self.h_lo[:, :, :])
        self.hi_done, self.lo_done = self.sem("weights_hi"), self.sem("weights_lo")
        self.src_hi, self.src_lo = self.sem("operand_hi"), self.sem("operand_lo")
        self.pieces = 0
        self.split = {"act": 0, "dve": 0}
        self.guests = 0
        self.guest_summed = self.sem("guest_summed")
        self.split_no = []
        self.split_chunk = []
        self.ps = ctx.enter_context(nc.psum_tensor("ps", [P, 8, 512], F32))
        self.where_p, self.where_c = where_p, where_c
        self.sems, self.raised = {}, {}
        self.groups = 0
        self.chunks = 0
        self.act_groups = [0]
        self.dve_groups = [0]
        self.loaded = [self.sem(f"chunk_loaded{i}") for i in range(RING)]
        self.chunk_used = self.sem("chunk_used")
        self.act_took = self.sem("act_took_group")
        self.dve_took = self.sem("dve_took_group")
        self.stage_done = self.sem("stage_done")
        self.params_in, self.inputs_in = self.sem("params_in"), self.sem("inputs_in")

    def sem(self, name):
        return self.ctx.enter_context(self.nc.semaphore(name))

    def mark(self, name, total):
        if name not in self.sems:
            self.sems[name], self.raised[name] = self.sem(name), 0
        m = Mark(self.sems[name], self.raised[name])
        self.raised[name] += total
        return m

    def par(self, name):
        at, n = self.where_p[name]
        return self.par_all[:, at:at + n]

    def con(self, name):
        at, n = self.where_c[name]
        return self.con_all[:, at:at + n]


class Stage:

    def __init__(self, k):
        self.k = k

    def tensor(self, pe):
        pass

    def scalar(self, act, st):
        pass

    def vector(self, dve, st):
        pass

    def gpsimd(self, pool, st):
        pass


def rstd(dve, st, var, y, tmp):
    st.wait()
    st(dve.tensor_scalar(y.bitcast(I32), var.bitcast(I32), -0.5, float(0x5f3759df), ALU.mult, ALU.add))
    for _ in range(3):
        st.wait()
        st(dve.scalar_tensor_tensor(tmp, y, -0.5, y, ALU.mult, ALU.mult))
        st.wait()
        st(dve.tensor_tensor(tmp, tmp, var, ALU.mult))
        st.wait()
        st(dve.scalar_tensor_tensor(y, tmp, 1.5, y, ALU.add, ALU.mult))
    st.wait()


class Setup(Stage):

    def scalar(self, act, st):
        act.wait_ge(self.k.params_in, 16)
        st(act.activation(self.k.cond[:, :], self.k.par("c"), ACT.Silu))

    def vector(self, dve, st):
        st(dve.memset(self.k.ones[:, :], 1.0))


class Inputs(Stage):

    def tensor(self, pe):
        pe.wait_ge(self.k.inputs_in, 48)

    def scalar(self, act, st):
        act.wait_ge(self.k.inputs_in, 48)

    def vector(self, dve, st):
        k = self.k
        dve.wait_ge(k.inputs_in, 48)
        at, n = k.where_c["mask_f"]
        st(dve.tensor_copy(k.mask_bf[:, 0:10 * P], k.con_all[:, at:at + 10 * P]))
        st(dve.tensor_copy(k.mask_bf[:, 10 * P:11 * P], k.con("ident")))


class Norm(Stage):

    def __init__(self, k, src, nf, dst, scale, bias, xh, small):
        super().__init__(k)
        self.src, self.nf, self.dst, self.scale, self.bias = src, nf, dst, scale, bias
        self.xh, self.small = xh, small
        self.m = {"sq": k.mark("sums_of_squares", 2), "xh": k.mark("rows_scaled", TT),
                  "turned": k.mark("bank_turned", nf // 2)}

    def scalar(self, act, st):
        m = self.m
        for t in range(TT):
            act.activation(self.xh[:, t, :], self.src[:, t, :], ACT.Square,
                           accum_out=self.small[:, t:t + 1]).then_inc(m["sq"].sem, 1)
        self.take_out(act, 0)

    def take_out(self, eng, parity):
        for j in range(self.nf // 2):
            if j % 2 != parity:
                continue
            eng.wait_ge(*self.m["turned"].at(j + 1))
            for f in (2 * j, 2 * j + 1):
                src = self.k.ps[:, 4 + j, (f % 2) * TOK:(f % 2 + 1) * TOK]
                if parity == 0:
                    eng.activation(self.dst[:, f, :], src, ACT.Identity, scale=self.scale[:, f:f + 1],
                                   bias=self.bias[:, f:f + 1] if self.bias is not None else 0.0)
                elif self.bias is not None:
                    eng.tensor_scalar(self.dst[:, f, :], src, self.scale[:, f:f + 1],
                                      self.bias[:, f:f + 1], ALU.mult, ALU.add)
                else:
                    eng.tensor_scalar(self.dst[:, f, :], src, self.scale[:, f:f + 1], None, ALU.mult)

    def vector(self, dve, st):
        m, s = self.m, self.small
        dve.wait_ge(*m["sq"].at(2))
        st(dve.tensor_scalar(s[:, 2:4], s[:, 0:2], 1.0 / (self.nf * P), EPS, ALU.mult, ALU.add))
        rstd(dve, st, s[:, 2:4], s[:, 4:6], s[:, 6:8])
        for t in range(TT):
            dve.tensor_scalar(self.xh[:, t, :], self.src[:, t, :], s[:, 4 + t:5 + t], None,
                              ALU.mult).then_inc(m["xh"].sem, 1)
        self.take_out(dve, 1)

    def tensor(self, pe):
        k, m = self.k, self.m
        pe.wait_ge(*m["xh"].at(TT))
        for f in range(self.nf):
            for t in range(TT):
                at = (f % 2) * TOK + t * P
                last = pe.transpose(k.ps[:, 4 + f // 2, at:at + P], self.xh[:, t, f * P:(f + 1) * P],
                                    k.con("ident"))
            if f % 2:
                last.then_inc(m["turned"].sem, 1)


class Product(Stage):

    def __init__(self, k, name, src, act_out, dve_out, act_after=None, dve_after=None, is_split=False,
                 guest=None):
        super().__init__(k)
        self.name = name
        self.is_split = is_split
        self.act_after, self.dve_after = act_after, dve_after
        self.src, self.act_out, self.dve_out, self.guest = src, act_out, dve_out, guest
        _, _, _, self.kt, groups = next(p for p in PRODUCTS if p[0] == name)
        self.groups, count = [], {False: 0, True: 0}
        for kind, _ in groups:
            self.groups.append((kind, count[is_guest(kind)]))
            count[is_guest(kind)] += 1
        self.first_group, self.first_chunk = k.groups, k.chunks
        self.first_guest = k.guests
        k.guests += count[True]
        self.nchunks = len(chunks_of(self.kt))
        self.first_piece = k.pieces
        k.groups += len(self.groups)
        k.chunks += len(self.groups) * self.nchunks
        k.pieces += 0 if is_split or count[False] == 0 else self.kt // 2
        for kind, _ in self.groups:
            k.act_groups.append(k.act_groups[-1] + (act_out is not None and not is_guest(kind)))
            k.dve_groups.append(k.dve_groups[-1] + 1)
            for _ in range(self.nchunks):
                k.split_no.append(None if is_guest(kind) else len(k.split_chunk))
                if not is_guest(kind):
                    k.split_chunk.append(len(k.split_no) - 1)

    def chunk_end(self, i):
        return self.first_chunk + (i + 1) * self.nchunks

    def tensor(self, pe):
        k, src = self.k, self.src
        for i, (kind, n) in enumerate(self.groups):
            g = self.first_group + i
            if g >= 2:
                if k.act_groups[g - 1]:
                    pe.wait_ge(k.act_took, k.act_groups[g - 1])
                pe.wait_ge(k.dve_took, k.dve_groups[g - 1])
            bank = 2 * (g % 2)
            if is_guest(kind):
                n += self.first_guest
                pe.wait_ge(k.guest_summed, n + 1)
                for q in range(4):
                    mm = pe.matmul(k.ps[:, bank, 2 * q:2 * q + 2], k.guest_acc[:, n % 2, q * P:(q + 1) * P],
                                   k.ones[:, :], start=True, stop=True)
                    if q >= 4 - self.nchunks:
                        mm.then_inc(k.chunk_used, 1)
                continue
            for j, (k0, nk) in enumerate(chunks_of(self.kt)):
                c = self.first_chunk + i * self.nchunks + j
                s = k.split_no[c]
                pe.wait_ge(k.hi_done, s + 1)
                pe.wait_ge(k.lo_done, s + 1)
                for kk in range(nk):
                    f = k0 + kk
                    if i == 0 and f % 2 == 0 and not self.is_split:
                        pe.wait_ge(k.src_hi, self.first_piece + f // 2 + 1)
                        pe.wait_ge(k.src_lo, self.first_piece + f // 2 + 1)
                    first, last = f == 0, f == self.kt - 1
                    w_hi, w_lo = k.w_hi[:, s % HI, kk, :], k.w_lo[:, c % RING, kk, :]
                    passes = [(src.hi, w_hi), (src.lo, w_hi), (src.hi, w_lo)]
                    if kind == "tok":
                        for t in range(TT):
                            for n, (x, w) in enumerate(passes):
                                mm = pe.matmul(k.ps[:, bank + t, :], x[:, f, t * P:(t + 1) * P], w,
                                               start=first and n == 0, stop=last and n == 2)
                    else:
                        for q in range(4):
                            for n, (x, w) in enumerate(passes):
                                mm = pe.matmul(k.ps[:, bank + q // 2, (q % 2) * TOK:(q % 2 + 1) * TOK],
                                               w[:, q * P:(q + 1) * P], x[:, f, :],
                                               start=first and n == 0 and q % 2 == 0, stop=last and n == 2,
                                               skip_group_check=True)
                mm.then_inc(k.chunk_used, 1)

    def split_source(self, eng, j, hi):
        k, (k0, nk) = self.k, chunks_of(self.kt)[j]
        if self.is_split:
            return
        for p in range(k0 // 2, (k0 + nk) // 2):
            at = slice(2 * p, 2 * p + 2)
            if hi:
                eng.activation(self.src.hi[:, at, :], self.src.f[:, at, :], ACT.Identity).then_inc(k.src_hi, 1)
            else:
                eng.wait_ge(k.src_hi, self.first_piece + p + 1)
                eng.tensor_tensor(self.src.lo[:, at, :], self.src.f[:, at, :], self.src.hi[:, at, :].bitcast(F32),
                                  ALU.subtract).then_inc(k.src_lo, 1)

    def begin(self, eng, hi):
        if not is_guest(self.groups[0][0]):
            for j in range(self.nchunks):
                self.split_source(eng, j, hi)
                split_weights(self.k, eng, self.first_chunk + j + 1, hi)

    def ahead(self, i):
        n = len(self.groups)
        if i + 1 == n:
            return self.chunk_end(i) + 2
        if not is_guest(self.groups[i + 1][0]):
            return self.chunk_end(i + 1)
        return self.chunk_end(i + 1) + 1 if i + 2 < n and not is_guest(self.groups[i + 2][0]) else self.chunk_end(i)

    def scalar(self, act, st):
        self.begin(act, True)
        for i, (kind, n) in enumerate(self.groups):
            split_weights(self.k, act, self.ahead(i), True)
            if self.act_out is None or is_guest(kind):
                continue
            act.wait_ge(self.k.chunk_used, self.chunk_end(i))
            self.act_out(act, st, n, self.k.ps[:, 2 * ((self.first_group + i) % 2), :]) \
                .then_inc(self.k.act_took, 1)
            if self.act_after is not None:
                self.act_after(act, st, n)

    def sum_guest(self, dve, st, i):
        if i == len(self.groups) or not is_guest(self.groups[i][0]):
            return
        k, n = self.k, self.first_guest + self.groups[i][1]
        acc = k.guest_acc[:, n % 2, :]
        for j, (k0, nk) in enumerate(chunks_of(self.kt)):
            c = self.first_chunk + i * self.nchunks + j
            dve.wait_ge(k.loaded[c % RING], 16 * (c // RING + 1))
            for f in range(k0, k0 + nk):
                w, cond = k.ring[:, c % RING, f - k0, :], k.cond[:, f:f + 1]
                if f == 0:
                    ins = dve.tensor_scalar(acc, w, cond, None, ALU.mult)
                else:
                    ins = dve.scalar_tensor_tensor(acc, w, cond, acc, ALU.mult, ALU.add)
                if f == self.kt - 1:
                    ins.then_inc(k.guest_summed, 1)
                else:
                    st(ins)
                    st.wait()

    def vector(self, dve, st):
        self.begin(dve, False)
        self.sum_guest(dve, st, 0)
        for i, (kind, n) in enumerate(self.groups):
            self.sum_guest(dve, st, i + 1)
            split_weights(self.k, dve, self.ahead(i), False)
            dve.wait_ge(self.k.chunk_used, self.chunk_end(i))
            bank = 2 * ((self.first_group + i) % 2)
            if is_guest(kind):
                self.guest(dve, st, n, self.k.ps[:, bank, :]).then_inc(self.k.dve_took, 1)
                continue
            self.take_group(dve, st, i, n).then_inc(self.k.dve_took, 1)
            if self.dve_after is not None:
                self.dve_after(dve, st, n)

    def take_group(self, dve, st, i, n):
        bank = 2 * ((self.first_group + i) % 2) + (self.act_out is not None)
        return self.dve_out(dve, st, n, self.k.ps[:, bank, :])


def split_weights(k, eng, upto, hi):
    who = "act" if hi else "dve"
    while k.split[who] < min(upto, k.chunks):
        c = k.split[who]
        k.split[who] += 1
        s = k.split_no[c]
        if s is None:
            continue
        w = k.ring[:, c % RING, :, :]
        if hi:
            eng.wait_ge(k.loaded[c % RING], 16 * (c // RING + 1))
            if s >= HI:
                eng.wait_ge(k.chunk_used, k.split_chunk[s - HI] + 1)
            eng.activation(k.w_hi[:, s % HI, :, :], w, ACT.Identity).then_inc(k.hi_done, 1)
        else:
            eng.wait_ge(k.hi_done, s + 1)
            eng.tensor_tensor(k.w_lo[:, c % RING, :, :], w, k.w_hi[:, s % HI, :, :].bitcast(F32),
                              ALU.subtract).then_inc(k.lo_done, 1)


class Narrow(Stage):

    def __init__(self, k, parts):
        super().__init__(k)
        self.parts = parts

    def tensor(self, pe):
        k = self.k
        for bank, rows, c in self.parts:
            for f in range(KD):
                pe.matmul(k.ps[0:rows, bank, 0:TOK], k.narrow[:, f, c:c + rows], k.hT[:, f, :], start=f == 0,
                          stop=f == KD - 1)


class Post(Stage):

    def __init__(self, k, y, gain, junk, small):
        super().__init__(k)
        self.y, self.gain, self.junk, self.small = y, gain, junk, small
        self.m = {"sq": k.mark("sums_of_squares", 2), "gain": k.mark("gain_laid_out", 1)}

    def tensor(self, pe):
        for f in range(KD):
            mm = pe.matmul(self.k.ps[:, 4 + f // 4, (f % 4) * P:(f % 4 + 1) * P],
                           self.gain[:, f:f + 1].broadcast_to([P, P]), self.k.con("ident"), start=True, stop=True)
        mm.then_inc(self.m["gain"].sem, 1)

    def scalar(self, act, st):
        for t in range(TT):
            act.activation(self.junk[:, t, :], self.y[:, t, :], ACT.Square,
                           accum_out=self.small[:, t:t + 1]).then_inc(self.m["sq"].sem, 1)

    def vector(self, dve, st):
        m, s = self.m, self.small
        dve.wait_ge(*m["sq"].at(2))
        st(dve.tensor_scalar(s[:, 2:4], s[:, 0:2], 1.0 / D, EPS, ALU.mult, ALU.add))
        rstd(dve, st, s[:, 2:4], s[:, 4:6], s[:, 6:8])
        dve.wait_ge(*m["gain"].at(1))
        for t in range(TT):
            y = self.y[:, t, :].rearrange("p (a b) -> p a b", a=2)
            st(dve.scalar_tensor_tensor(y, y, s[:, 4 + t:5 + t], self.k.ps[:, 4:6, :], ALU.mult, ALU.mult))
        st.wait()
        for t in range(TT):
            st(dve.tensor_tensor(self.k.x[:, t, :], self.k.x[:, t, :], self.y[:, t, :], ALU.add))


def to_rows(dst):
    def act_out(act, st, i, bank):
        return act.activation(dst[:, 0, i * CN:(i + 1) * CN], bank, ACT.Identity)

    def dve_out(dve, st, i, bank):
        return dve.tensor_copy(dst[:, 1, i * CN:(i + 1) * CN], bank)
    return act_out, dve_out


def to_features(dst):
    def act_out(act, st, i, bank):
        return act.activation(dst[:, 4 * i:4 * i + 2, :], bank.rearrange("p (a b) -> p a b", a=2), ACT.Identity)

    def dve_out(dve, st, i, bank):
        return dve.tensor_copy(dst[:, 4 * i + 2:4 * i + 4, :], bank.rearrange("p (a b) -> p a b", a=2))
    return act_out, dve_out


def by_ranges(*ranges):
    def pick(which):
        def out(eng, st, i, bank):
            for n, pair in ranges:
                if i < n:
                    return pair[which](eng, st, i, bank)
                i -= n
        return out
    return pick(0), pick(1)


def ada_take(k, mods, first):
    def take(dve, st, n, bank):
        layer, part, half = (first + n) // 12, (first + n) % 12 // 2, n % 2
        at = slice(4 * half, 4 * half + 4)
        dst, b = mods[layer][:, part, at], k.par(f"ada_b{layer}{part}")[:, at]
        if part % 3 == 0:
            return dve.tensor_tensor(dst, bank[:, 0:8:2], b, ALU.add)
        st(dve.tensor_tensor(dst, bank[:, 0:8:2], b, ALU.add))
        st.wait()
        norm = k.par(f"norm{layer}{2 * (part // 3) + (part % 3 == 2)}")[:, at]
        return dve.scalar_tensor_tensor(dst, dst, 1.0 if part % 3 == 1 else 0.0, norm, ALU.add, ALU.mult)
    return take


def mlp_stages(k, layer, uo, y, guest):
    u = uo.f

    def act_out(act, st, i, bank):
        dst = u[:, 4 * i:4 * i + 2, :]
        st(act.activation(dst, bank.rearrange("p (a b) -> p a b", a=2), ACT.Relu))
        st.wait()
        return act.activation(dst, dst, ACT.Square)

    def dve_out(dve, st, i, bank):
        dst = u[:, 4 * i + 2:4 * i + 4, :]
        b = bank.rearrange("p (a b) -> p a b", a=2)
        st(dve.tensor_scalar(dst, b, 0.0, None, ALU.max))
        st.wait()
        return dve.tensor_tensor(dst, dst, dst, ALU.mult)

    return [Product(k, f"up{layer}", k.hT_operand, act_out, dve_out, guest=guest),
            Product(k, f"down{layer}", uo, *to_rows(y))]


class Turn(Stage):

    def __init__(self, k, src, nf, dst, scale=None):
        super().__init__(k)
        self.src, self.nf, self.dst, self.scale = src, nf, dst, scale
        self.turned = k.mark("bank_turned", nf // 2)

    def tensor(self, pe):
        for f in range(self.nf):
            for t in range(TT):
                at = (f % 2) * TOK + t * P
                last = pe.transpose(self.k.ps[:, f // 2, at:at + P], self.src[:, t, f * P:(f + 1) * P],
                                    self.k.con("ident"))
            if f % 2:
                last.then_inc(self.turned.sem, 1)

    def take_out(self, eng, parity):
        for j in range(self.nf // 2):
            if j % 2 != parity:
                continue
            eng.wait_ge(*self.turned.at(j + 1))
            if self.scale is None:
                src = self.k.ps[:, j, :].rearrange("p (a b) -> p a b", a=2)
                if parity:
                    eng.tensor_copy(self.dst[:, 2 * j:2 * j + 2, :], src)
                else:
                    eng.activation(self.dst[:, 2 * j:2 * j + 2, :], src, ACT.Identity)
                continue
            for f in (2 * j, 2 * j + 1):
                src = self.k.ps[:, j, (f % 2) * TOK:(f % 2 + 1) * TOK]
                if parity:
                    eng.tensor_scalar(self.dst[:, f, :], src, self.scale(f), None, ALU.mult)
                else:
                    eng.activation(self.dst[:, f, :], src, ACT.Identity, scale=self.scale(f))

    def scalar(self, act, st):
        self.take_out(act, 0)

    def vector(self, dve, st):
        self.take_out(dve, 1)


class Attention(Stage):

    def __init__(self, k, heads, w, q, keys, v, out, buf, table=None, lead=None):
        super().__init__(k)
        self.heads, self.w, self.q, self.keys, self.v, self.out = heads, w, q, keys, v, out
        self.table, self.lead = table, lead
        self.pm = buf.take(2, TT, TOK)
        self.pt = buf.take(2, 2, TOK)
        self.sb = buf.take(2, TT, TOK) if table else None
        self.small = buf.take(3, TT, 16)
        self.m = {n: k.mark(n, heads) for n in ("scores_in", "maxima_in", "probs_in", "probs_turned",
                                                "probs_taken", "values_in")}

    def tensor(self, pe):
        k, m, w = self.k, self.m, self.w

        def scores(h):
            if h >= 2:
                pe.wait_ge(*m["probs_in"].at(h - 1))
            bank = k.ps[:, h % 2, :]
            if self.lead:
                self.lead(pe, h, bank)
            for t in range(TT):
                parts = list(zip(self.q(h, t), self.keys(h)))
                for i, (a, b) in enumerate(parts):
                    mm = pe.matmul(bank[:, t * TOK:(t + 1) * TOK], a, b, start=i == 0 and not self.lead,
                                   stop=i == len(parts) - 1, skip_group_check=bool(self.lead))
            mm.then_inc(m["scores_in"].sem, 1)

        def turn(h):
            pe.wait_ge(*m["probs_in"].at(h + 1))
            if h >= 2:
                pe.wait_ge(*m["probs_taken"].at(h - 1))
            for t in range(TT):
                for s in range(2):
                    last = pe.transpose(k.ps[:, 2 + h % 2, s * TOK + t * P:s * TOK + (t + 1) * P],
                                        self.pm[:, h % 2, t, s * P:(s + 1) * P], k.con("ident"))
            last.then_inc(m["probs_turned"].sem, 1)

        def values(h):
            pe.wait_ge(*m["probs_taken"].at(h + 1))
            for t in range(TT):
                at = (h * w) % 512
                for s in range(2):
                    mm = pe.matmul(k.ps[:, 4 + 2 * t + (h * w) // 512, at:at + w],
                                   self.pt[:, h % 2, s, t * P:(t + 1) * P], self.v(h, s),
                                   start=s == 0, stop=s == 1)
            mm.then_inc(m["values_in"].sem, 1)

        for h in range(self.heads + 2):
            if h < self.heads:
                scores(h)
            if 1 <= h <= self.heads:
                turn(h - 1)
            if h >= 2:
                values(h - 2)

    def scalar(self, act, st):
        m, s = self.m, self.small
        for h in range(self.heads):
            act.wait_ge(*m["maxima_in"].at(h + 1))
            if h >= 2:
                act.wait_ge(*m["probs_turned"].at(h - 1))
            for t in range(TT):
                src = self.sb[:, h % 2, t, :] if self.table else self.k.ps[:, h % 2, t * TOK:(t + 1) * TOK]
                last = act.activation(self.pm[:, h % 2, t, :], src, ACT.Exp, bias=s[:, 0, t, h:h + 1],
                                      accum_out=s[:, 1, t, h:h + 1])
            last.then_inc(m["probs_in"].sem, 1)

    def vector(self, dve, st):
        k, m, s, w = self.k, self.m, self.small, self.w
        for h in range(self.heads + 1):
            if h < self.heads:
                dve.wait_ge(*m["scores_in"].at(h + 1))
                if self.table:
                    if h >= 2:
                        dve.wait_ge(*m["probs_in"].at(h - 1))
                    for t in range(TT):
                        st(dve.tensor_tensor_reduce(self.sb[:, h % 2, t, :], k.ps[:, h % 2, t * TOK:(t + 1) * TOK],
                                                    self.table(h, t), 1.0, -3e38, ALU.add, ALU.max,
                                                    s[:, 0, t, h:h + 1]))
                else:
                    st(dve.tensor_reduce(s[:, 0, :, h], k.ps[:, h % 2, :].rearrange("p (t n) -> p t n", t=TT),
                                         AX, ALU.max))
                st.wait()
                dve.tensor_scalar(s[:, 0, :, h], s[:, 0, :, h], -1.0, None, ALU.mult) \
                    .then_inc(m["maxima_in"].sem, 1)
            if h >= 1:
                dve.wait_ge(*m["probs_turned"].at(h))
                if h >= 3:
                    dve.wait_ge(*m["values_in"].at(h - 2))
                dve.tensor_copy(self.pt[:, (h - 1) % 2, :, :],
                                k.ps[:, 2 + (h - 1) % 2, :].rearrange("p (s n) -> p s n", s=2)) \
                   .then_inc(m["probs_taken"].sem, 1)
        dve.wait_ge(*m["probs_in"].at(self.heads))
        dve.wait_ge(*m["values_in"].at(self.heads))
        n = self.heads
        st(dve.reciprocal(s[:, 2, :, 0:n], s[:, 1, :, 0:n]))
        st.wait()
        per = min(n, 512 // w)
        for t in range(TT):
            for half in range(n // per):
                dst = self.out[:, t, half * per * w:(half + 1) * per * w].rearrange("p (h w) -> p h w", w=w)
                src = k.ps[:, 4 + 2 * t + half, 0:per * w].rearrange("p (h w) -> p h w", w=w)
                r = s[:, 2, t, half * per:(half + 1) * per].unsqueeze(2).broadcast_to([P, per, w])
                st(dve.tensor_tensor(dst, src, r, ALU.mult))


class Pads(Stage):

    def __init__(self, k, xp):
        super().__init__(k)
        self.xp = xp

    def vector(self, dve, st):
        st(dve.memset(self.xp[:, :, 0:2], 0.0))
        st(dve.memset(self.xp[:, :, TOK + 2:TOK + 4], 0.0))


def in0_stage(k, xp, xc, zs, qT, kT, v, guest):
    conv_done = k.mark("convolved", 3)
    first = k.groups

    def xbc_act(act, st, i, bank):
        return act.activation(xp[:, 4 * i:4 * i + 2, 2:2 + TOK], bank.rearrange("p (a b) -> p a b", a=2),
                              ACT.Identity)

    def xbc_dve(dve, st, i, bank):
        return dve.tensor_copy(xp[:, 4 * i + 2:4 * i + 4, 2:2 + TOK], bank.rearrange("p (a b) -> p a b", a=2))

    def z_act(act, st, i, bank):
        return act.activation(zs[:, 0, i * CN:(i + 1) * CN], bank, ACT.Silu)

    def z_dve(dve, st, i, bank):
        return dve.tensor_copy(zs[:, 1, i * CN:(i + 1) * CN], bank)

    def q_act(act, st, i, bank):
        return act.activation(qT[:, 4 * i:4 * i + 2, :], bank.rearrange("p (a b) -> p a b", a=2),
                              ACT.Identity, scale=HP ** -0.5)

    def q_dve(dve, st, i, bank):
        return dve.tensor_scalar(qT[:, 4 * i + 2:4 * i + 4, :], bank.rearrange("p (a b) -> p a b", a=2),
                                 HP ** -0.5, None, ALU.mult)

    act_out, dve_out = by_ranges((3, (xbc_act, xbc_dve)), (2, (z_act, z_dve)), (2, (q_act, q_dve)),
                                 (2, to_features(kT)), (2, to_rows(v)))

    def dve_after(dve, st, i):
        if i >= 3:
            return
        dve.wait_ge(k.act_took, k.act_groups[first + place("in0", i) + 1])
        dve.wait_ge(k.dve_took, k.dve_groups[first + place("in0", i) + 1])
        for tap in range(5):
            for j in range(4 * i, 4 * i + 4):
                src, w = xp[:, j, tap:tap + TOK], k.par("conv_w")[:, 12 * tap + j:12 * tap + j + 1]
                if tap == 0:
                    ins = dve.tensor_scalar(xc[:, j, :], src, w, k.par("conv_b")[:, j:j + 1], ALU.mult, ALU.add)
                else:
                    ins = dve.scalar_tensor_tensor(xc[:, j, :], src, w, xc[:, j, :], ALU.mult, ALU.add)
                if tap == 4 and j == 4 * i + 3:
                    ins.then_inc(conv_done.sem, 1)
                else:
                    st(ins)
            if tap < 4:
                st.wait()

    def act_after(act, st, i):
        if 1 <= i <= 3:
            act.wait_ge(*conv_done.at(i))
            dst = xc[:, 4 * i - 4:4 * i, :]
            st(act.activation(dst, dst, ACT.Silu))
        if i == 5:
            act.wait_ge(k.dve_took, k.dve_groups[first + place("in0", 4) + 1])
            st(act.activation(zs[:, 1, :], zs[:, 1, :], ACT.Silu))

    return Product(k, "in0", k.hT_operand, act_out, dve_out, act_after, dve_after, guest=guest)


def softplus_scalar(act, st, k, u, a, wait, done):
    act.wait_ge(*wait)
    st(act.activation(a, u, ACT.Abs))
    st.wait()
    st(act.activation(a, a, ACT.Exp, scale=-1.0))
    st.wait()
    act.activation(a, a, ACT.Ln, bias=k.con("ones")[0:a.shape[0], 0:1]).then_inc(done.sem, 1)


class SsdPrep(Stage):

    def __init__(self, k, xc, xt, xf, xb, cbf, cbb, cs4, csn, dtc, tmp):
        super().__init__(k)
        self.xc, self.xt, self.xf, self.xb, self.cbf, self.cbb = xc, xt, xf, xb, cbf, cbb
        self.cs4, self.csn, self.dtc, self.tmp = cs4, csn, dtc, tmp
        self.m = {n: k.mark(n, c) for n, c in (("cb_in", 2), ("x_turned", 4), ("biased", 1),
                                               ("log_in", 1), ("rates_in", 1), ("sums_in", 1), ("sums_turned", 1), ("x_copied", 2))}

    def tensor(self, pe):
        k, m = self.k, self.m
        for g in range(2):
            for s in range(2):
                mm = pe.matmul(k.ps[:, 5 + g, s * TOK:(s + 1) * TOK], self.xc[:, 8 + g, s * P:(s + 1) * P],
                               self.xc[:, 10 + g, :], start=True, stop=True)
            mm.then_inc(m["cb_in"].sem, 1)
        for b in range(4):
            for q in range(4):
                mm = pe.transpose(k.ps[:, b, q * P:(q + 1) * P],
                                  self.xc[:, 4 * (b % 2) + q, (b // 2) * P:(b // 2 + 1) * P], k.con("ident"))
            mm.then_inc(m["x_turned"].sem, 1)
        pe.wait_ge(*m["sums_in"].at(1))
        for t in range(TT):
            pe.transpose(k.ps[:, 7, t * 64:(t + 1) * 64], self.cs4[0:64, P + t * P:P + (t + 1) * P],
                         k.con("ident")[0:64, 0:64])
            mm = pe.transpose(k.ps[:, 7, P + t * 64:P + (t + 1) * 64], self.tmp[0:64, 2, t * P:(t + 1) * P],
                              k.con("ident")[0:64, 0:64])
        mm.then_inc(m["sums_turned"].sem, 1)

    def scalar(self, act, st):
        k, m, tmp = self.k, self.m, self.tmp
        softplus_scalar(act, st, k, tmp[0:64, 0, :], tmp[0:64, 1, :], m["biased"].at(1), m["log_in"])
        act.activation(tmp[0:64, 3, 0:1], k.par("a_log")[0:64, :], ACT.Exp).then_inc(m["rates_in"].sem, 1)
        for b in (0, 1):
            act.wait_ge(*m["x_turned"].at(b + 1))
            act.activation(self.xt[:, b // 2, (b % 2) * 512:(b % 2 + 1) * 512], k.ps[:, b, :], ACT.Identity) \
               .then_inc(m["x_copied"].sem, 1)

    def vector(self, dve, st):
        k, m, tmp = self.k, self.m, self.tmp
        u, a, dt, adt = (tmp[0:64, j, :] for j in (0, 1, 2, 4))
        dve.tensor_scalar(u, k.ps[0:64, 4, 0:TOK], k.par("dt_bias")[0:64, :], None, ALU.add) \
           .then_inc(m["biased"].sem, 1)
        dve.wait_ge(*m["cb_in"].at(2))
        for g in range(2):
            b = k.ps[:, 5 + g, :]
            st(dve.tensor_copy(self.cbf[:, g, 0:TOK], b[:, 0:TOK]))
            st(dve.tensor_copy(self.cbf[:, g, TOK:TOK + P], b[:, TOK + P:2 * TOK]))
            st(dve.tensor_copy(self.cbb[:, g, 0:P], b[:, 0:P]))
            st(dve.tensor_copy(self.cbb[:, g, P:P + TOK], b[:, TOK:2 * TOK]))
        for b in (2, 3):
            dve.wait_ge(*m["x_turned"].at(b + 1))
            st(dve.tensor_copy(self.xt[:, b // 2, (b % 2) * 512:(b % 2 + 1) * 512], k.ps[:, b, :]))
        dve.wait_ge(*m["log_in"].at(1))
        dve.wait_ge(*m["rates_in"].at(1))
        st(dve.scalar_tensor_tensor(dt, u, 0.0, a, ALU.max, ALU.add))
        st.wait()
        st(dve.tensor_scalar(adt, dt, tmp[0:64, 3, 0:1], -1.0, ALU.mult, ALU.mult))
        st.wait()
        ones, cs = k.con("ones"), self.cs4[:, P:P + TOK]
        st(dve.tensor_tensor_scan(cs[0:32, :], ones[0:32, :], adt[0:32, :], 0.0, ALU.mult, ALU.add))
        st(dve.tensor_tensor_scan(cs[32:64, ::-1], ones[32:64, :], adt[32:64, ::-1], 0.0, ALU.mult, ALU.add))
        st.wait()
        st(dve.tensor_copy(self.cs4[0:64, 0:P], self.cs4[0:64, P:2 * P]))
        dve.tensor_copy(self.cs4[0:64, 3 * P:4 * P], self.cs4[0:64, 2 * P:3 * P]).then_inc(m["sums_in"].sem, 1)
        dve.wait_ge(*m["sums_turned"].at(1))
        turned = k.ps[:, 7, 0:4 * 64].rearrange("p (a t c) -> p a t c", a=2, t=TT)
        st(dve.tensor_scalar(self.csn, turned[:, 0], -1.0, None, ALU.mult))
        st(dve.tensor_copy(self.dtc, turned[:, 1]))
        st.wait()
        dve.wait_ge(*m["x_copied"].at(2))
        for t in range(TT):
            x = self.xt[:, t, :].rearrange("p (h w) -> p h w", w=HP)
            for d, dst in ((0, self.xf), (1, self.xb)):
                st(dve.tensor_tensor(dst[:, t, :].rearrange("p (h w) -> p h w", w=HP), x,
                                     self.dtc[:, t, 32 * d:32 * d + NH].unsqueeze(2).broadcast_to([P, NH, HP]),
                                     ALU.mult))


class Ssd(Stage):

    def __init__(self, k, xt, xf, xb, cbf, cbb, cs4, csn, zs, e):
        super().__init__(k)
        self.xt, self.xf, self.xb, self.cbf, self.cbb = xt, xf, xb, cbf, cbb
        self.cs4, self.csn, self.zs, self.e = cs4, csn, zs, e
        self.m = {"args": k.mark("decay_args", 2 * NH), "exp": k.mark("decays_in", 2 * NH),
                  "g": k.mark("weights_in", 2 * NH), "y": k.mark("head_out", NH)}

    def tensor(self, pe):
        k, m = self.k, self.m

        def args(i):
            h, d = i // 2, i % 2
            if i >= 4:
                pe.wait_ge(*m["exp"].at(i - 3))
            c = 32 * d + h
            bank = k.ps[:, i % 4, 0:3 * P]
            pe.matmul(bank, k.con("ident")[0:64, c:c + 1].broadcast_to([64, P]),
                      self.cs4[0:64, P * (1 - d):P * (4 - d)], start=True, stop=False)
            pe.matmul(bank, k.mask_bf[:, 10 * P:11 * P], k.mask_bf[:, 3 * P * d:3 * P * (d + 1)],
                      start=False, stop=True).then_inc(m["args"].sem, 1)

        def out(h):
            pe.wait_ge(*m["g"].at(2 * h + 2))
            f, b = self.e[:, (2 * h) % 4, :], self.e[:, (2 * h + 1) % 4, :]
            hs = slice(h * HP, (h + 1) * HP)
            for t in range(TT):
                if t == 0:
                    parts = [(f[:, 0:P], self.xf[:, 0, hs]), (b[:, 0:P], self.xb[:, 0, hs]),
                             (b[:, P:2 * P], self.xb[:, 1, hs])]
                else:
                    parts = [(f[:, P:2 * P], self.xf[:, 0, hs]), (f[:, 2 * P:3 * P], self.xf[:, 1, hs]),
                             (b[:, 2 * P:3 * P], self.xb[:, 1, hs])]
                for n, (w, x) in enumerate(parts):
                    mm = pe.matmul(k.ps[:, 4 + 2 * t + h // 8, (h % 8) * HP:(h % 8 + 1) * HP], w, x,
                                   start=n == 0, stop=n == 2)
            mm.then_inc(m["y"].sem, 1)

        for h in range(NH + 1):
            if h < NH:
                args(2 * h)
                args(2 * h + 1)
            if h >= 1:
                out(h - 1)

    def scalar(self, act, st):
        m = self.m
        for i in range(2 * NH):
            h, d = i // 2, i % 2
            act.wait_ge(*m["args"].at(i + 1))
            if i >= 4:
                act.wait_ge(*m["y"].at((i - 4) // 2 + 1))
            cut = TOK if d == 0 else P
            e, ps, c = self.e[:, i % 4, :], self.k.ps[:, i % 4, :], 32 * d + h
            act.activation(e[:, 0:cut], ps[:, 0:cut], ACT.Exp, bias=self.csn[:, 0, c:c + 1])
            act.activation(e[:, cut:3 * P], ps[:, cut:3 * P], ACT.Exp, bias=self.csn[:, 1, c:c + 1]) \
               .then_inc(m["exp"].sem, 1)

    def vector(self, dve, st):
        k, m = self.k, self.m
        for t in range(TT):
            x = self.xt[:, t, :].rearrange("p (h w) -> p h w", w=HP)
            st(dve.tensor_tensor(x, x, k.par("d_skip").unsqueeze(2).broadcast_to([P, NH, HP]), ALU.mult))
        for i in range(2 * NH):
            h, d = i // 2, i % 2
            dve.wait_ge(*m["exp"].at(i + 1))
            cb = (self.cbf, self.cbb)[d][:, h // 8, :]
            dve.tensor_tensor(self.e[:, i % 4, :], self.e[:, i % 4, :], cb, ALU.mult).then_inc(m["g"].sem, 1)
        dve.wait_ge(*m["y"].at(NH))
        for t in range(TT):
            for half in range(2):
                x = self.xt[:, t, half * 512:(half + 1) * 512]
                st(dve.tensor_tensor(x, k.ps[:, 4 + 2 * t + half, :], x, ALU.add))
        st.wait()
        for t in range(TT):
            st(dve.tensor_tensor(self.zs[:, t, :], self.zs[:, t, :], self.xt[:, t, :], ALU.mult))


class BiasTable(Stage):

    def __init__(self, k, table):
        super().__init__(k)
        self.table = table
        self.m = {"picked": k.mark("bias_picked", 16), "taken": k.mark("bias_taken", 16)}

    def tensor(self, pe):
        k, m = self.k, self.m
        toe = k.con("toeplitz")
        for j in range(16):
            if j >= 2:
                pe.wait_ge(*m["taken"].at(j - 1))
            for i in range(4):
                kc = 4 * j + i
                mm = pe.matmul(k.ps[:, j % 2, 112 * i:112 * (i + 1)],
                               toe[0:32, 63 - kc:191 - kc],
                               k.par("rpb")[0:32, :], start=True, stop=True)
            mm.then_inc(m["picked"].sem, 1)

    def vector(self, dve, st):
        k, m = self.k, self.m
        table = self.table.rearrange("p (h u c) -> p h u c", h=NH, u=6)
        for j in range(16):
            dve.wait_ge(*m["picked"].at(j + 1))
            for half in range(2):
                rows = slice(64 * half, 64 * half + 64)
                for i in range(4):
                    kc = 4 * j + i
                    src = k.ps[rows, j % 2, 112 * i:112 * (i + 1)].rearrange("p (h d) -> p h d", d=7)
                    ins = dve.tensor_scalar(table[rows, :, :, kc], src[:, :, 1 - half:7 - half],
                                            k.con("window")[rows, kc:kc + 1], None, ALU.add)
                    if half == 1 and i == 3:
                        ins.then_inc(m["taken"].sem, 1)


class GatePrep(Stage):

    def __init__(self, k, tmp, negm, acol, floor):
        super().__init__(k)
        self.tmp, self.negm, self.acol, self.floor = tmp, negm, acol, floor
        self.m = {n: k.mark(n, c) for n, c in (("biased", 1), ("log_in", 1),
                                               ("sums_in", 1), ("sums_turned", 1))}

    def tensor(self, pe):
        k, m = self.k, self.m
        pe.wait_ge(*m["sums_in"].at(1))
        for t in range(TT):
            pe.transpose(k.ps[:, 7, t * 64:(t + 1) * 64], self.tmp[0:64, 5, t * P:(t + 1) * P],
                         k.con("ident")[0:64, 0:64])
            mm = pe.transpose(k.ps[:, 7, P + t * 64:P + (t + 1) * 64], self.tmp[0:64, 6, t * P:(t + 1) * P],
                              k.con("ident")[0:64, 0:64])
        mm.then_inc(m["sums_turned"].sem, 1)

    def scalar(self, act, st):
        k, m, tmp = self.k, self.m, self.tmp
        softplus_scalar(act, st, k, tmp[0:64, 1, :], tmp[0:64, 2, :], m["biased"].at(1), m["log_in"])
        act.wait_ge(*m["sums_turned"].at(1))
        st(act.activation(self.floor, k.ps[:, 7, P:2 * P].rearrange("p (t c) -> p t c", t=TT), ACT.Exp,
                          scale=-1.0))
        st(act.activation(self.acol, k.ps[:, 7, 0:P].rearrange("p (t c) -> p t c", t=TT), ACT.Identity))

    def vector(self, dve, st):
        k, m, tmp = self.k, self.m, self.tmp
        ig, fg, ln, lf, b, a, mm = (tmp[0:64, j, :] for j in range(7))
        st(dve.tensor_scalar(ig, k.ps[0:64, 4, 0:TOK], k.par("gate_i")[0:64, :], None, ALU.add))
        dve.tensor_scalar(fg, k.ps[0:64, 5, 0:TOK], k.par("gate_f")[0:64, :], None, ALU.add) \
           .then_inc(m["biased"].sem, 1)
        dve.wait_ge(*m["log_in"].at(1))
        st(dve.scalar_tensor_tensor(lf, fg, 0.0, ln, ALU.min, ALU.subtract))
        st.wait()
        ones = k.con("ones")
        st(dve.tensor_tensor_scan(b[0:32, :], ones[0:32, :], lf[0:32, :], 0.0, ALU.mult, ALU.add))
        st(dve.tensor_tensor_scan(b[32:64, ::-1], ones[32:64, :], lf[32:64, ::-1], 0.0, ALU.mult, ALU.add))
        st.wait()
        st(dve.tensor_tensor(a, ig, b, ALU.subtract))
        st.wait()
        st(dve.tensor_tensor_scan(mm[0:32, :], ones[0:32, :], a[0:32, :], 0.0, ALU.mult, ALU.max))
        st(dve.tensor_tensor_scan(mm[32:64, ::-1], ones[32:64, :], a[32:64, ::-1], 0.0, ALU.mult, ALU.max))
        st.wait()
        st(dve.tensor_scalar(self.negm[0:64, P:P + TOK], mm, -1.0, None, ALU.mult))
        st.wait()
        st(dve.tensor_copy(self.negm[0:64, 0:P], self.negm[0:64, P:2 * P]))
        st(dve.tensor_copy(self.negm[0:64, 3 * P:4 * P], self.negm[0:64, 2 * P:3 * P]))
        dve.tensor_tensor(mm, mm, b, ALU.add).then_inc(m["sums_in"].sem, 1)


class Mlstm(Stage):

    def __init__(self, k, qT, kT, v, negm, acol, floor, h, e, sc, small):
        super().__init__(k)
        self.qT, self.kT, self.v, self.negm, self.acol, self.floor = qT, kT, v, negm, acol, floor
        self.h, self.e, self.sc, self.small = h, e, sc, small
        self.m = {"args": k.mark("decay_args", 2 * MH), "exp": k.mark("decays_in", 2 * MH),
                  "g": k.mark("weights_in", 2 * MH), "s": k.mark("products_in", MH),
                  "sc": k.mark("products_copied", MH),
                  "num": k.mark("numerators_in", 4 * MH), "h": k.mark("numerators_taken", 4 * MH)}

    def tensor(self, pe):
        k, m = self.k, self.m

        def args(i):
            h, d = i // 2, i % 2
            if d == 0:
                if h >= 1:
                    pe.wait_ge(*m["sc"].at(h))
                for s in range(2):
                    mm = pe.matmul(k.ps[:, 2, s * TOK:(s + 1) * TOK], self.kT[:, h, s * P:(s + 1) * P],
                                   self.qT[:, h, :], start=True, stop=True)
                mm.then_inc(m["s"].sem, 1)
            if i >= 2:
                pe.wait_ge(*m["exp"].at(i - 1))
            c = 32 * d + h
            bank = k.ps[:, i % 2, 0:3 * P]
            pe.matmul(bank, k.con("ident")[0:64, c:c + 1].broadcast_to([64, P]),
                      self.negm[0:64, P * (1 - d):P * (4 - d)], start=True, stop=False)
            pe.matmul(bank, k.mask_bf[:, 10 * P:11 * P], k.mask_bf[:, 3 * P * d:3 * P * (d + 1)],
                      start=False, stop=True).then_inc(m["args"].sem, 1)

        def out(i):
            h, d = i // 2, i % 2
            pe.wait_ge(*m["g"].at(i + 1))
            w, v = self.e[:, i % 4, :], lambda s: self.v[:, s, h, :]
            for t in range(TT):
                n = 2 * i + t
                if n >= 4:
                    pe.wait_ge(*m["h"].at(n - 3))
                if d == 0:
                    parts = [(w[:, 0:P], v(0))] if t == 0 else [(w[:, P:2 * P], v(0)), (w[:, 2 * P:3 * P], v(1))]
                else:
                    parts = [(w[:, 0:P], v(0)), (w[:, P:2 * P], v(1))] if t == 0 else [(w[:, 2 * P:3 * P], v(1))]
                for j, (a, b) in enumerate(parts):
                    mm = pe.matmul(k.ps[:, 4 + n % 4, 0:MDV + 2], a, b, start=j == 0, stop=j == len(parts) - 1)
                mm.then_inc(m["num"].sem, 1)

        for i in range(2 * MH + 1):
            if i < 2 * MH:
                args(i)
            if i >= 1:
                out(i - 1)

    def scalar(self, act, st):
        m = self.m
        for i in range(2 * MH):
            h, d = i // 2, i % 2
            act.wait_ge(*m["args"].at(i + 1))
            if i >= 4:
                act.wait_ge(*m["num"].at(2 * (i - 4) + 2))
            cut = TOK if d == 0 else P
            e, ps, c = self.e[:, i % 4, :], self.k.ps[:, i % 2, :], 32 * d + h
            act.activation(e[:, 0:cut], ps[:, 0:cut], ACT.Exp, bias=self.acol[:, 0, c:c + 1])
            act.activation(e[:, cut:3 * P], ps[:, cut:3 * P], ACT.Exp, bias=self.acol[:, 1, c:c + 1]) \
               .then_inc(m["exp"].sem, 1)

    def vector(self, dve, st):
        k, m, sm = self.k, self.m, self.small

        def take(i):
            h, d = i // 2, i % 2
            for t in range(TT):
                n, c = 2 * i + t, 32 * d + h
                ps = k.ps[:, 4 + n % 4, :]
                dve.wait_ge(*m["num"].at(n + 1))
                st(dve.tensor_scalar(sm[:, 0:1], ps[:, MDV:MDV + 1], -1.0, None, ALU.mult))
                st.wait()
                st(dve.scalar_tensor_tensor(sm[:, 1:2], ps[:, MDV:MDV + 1], sm[:, 0:1],
                                            self.floor[:, t, c:c + 1], ALU.max, ALU.max))
                st.wait()
                st(dve.reciprocal(sm[:, 2:3], sm[:, 1:2]))
                st.wait()
                dst = self.h[:, t, h * MDV:(h + 1) * MDV]
                if d == 0:
                    ins = dve.tensor_scalar(dst, ps[:, 0:MDV], sm[:, 2:3], None, ALU.mult)
                else:
                    dve.wait_ge(*m["h"].at(n - 1))
                    ins = dve.scalar_tensor_tensor(dst, ps[:, 0:MDV], sm[:, 2:3], dst, ALU.mult, ALU.add)
                ins.then_inc(m["h"].sem, 1)

        for i in range(2 * MH + 1):
            if i < 2 * MH:
                h, d = i // 2, i % 2
                sc = self.sc[:, h % 2, :]
                if d == 0:
                    dve.wait_ge(*m["s"].at(h + 1))
                    dve.tensor_copy(sc[:, P:P + 2 * TOK], k.ps[:, 2, :]).then_inc(m["sc"].sem, 1)
                    dve.wait_ge(*m["sc"].at(h + 1))
                dve.wait_ge(*m["exp"].at(i + 1))
                e = self.e[:, i % 4, :]
                if d == 0:
                    st(dve.tensor_tensor(e[:, 0:TOK], e[:, 0:TOK], sc[:, P:P + TOK], ALU.mult))
                    ins = dve.tensor_tensor(e[:, TOK:3 * P], e[:, TOK:3 * P], sc[:, 2 * TOK:2 * TOK + P], ALU.mult)
                else:
                    st(dve.tensor_tensor(e[:, 0:P], e[:, 0:P], sc[:, P:2 * P], ALU.mult))
                    ins = dve.tensor_tensor(e[:, P:3 * P], e[:, P:3 * P], sc[:, P + TOK:P + 2 * TOK], ALU.mult)
                ins.then_inc(m["g"].sem, 1)
            if i >= 1:
                take(i - 1)


class HeadNorm(Stage):

    def __init__(self, k, h, o, small, junk):
        super().__init__(k)
        self.h, self.o, self.small, self.junk = h, o, small, junk
        self.m = {"sq": k.mark("sums_of_squares", 2)}

    def scalar(self, act, st):
        s = self.small
        for t in range(TT):
            for h in range(MH):
                ins = act.activation(self.junk[:, t * MH + h, :], self.h[:, t, h * MDV:(h + 1) * MDV],
                                     ACT.Square, accum_out=s[:, 0, t * MH + h:t * MH + h + 1])
            ins.then_inc(self.m["sq"].sem, 1)

    def vector(self, dve, st):
        s, m = self.small, self.m
        dve.wait_ge(*m["sq"].at(2))
        st(dve.tensor_scalar(s[:, 1, :], s[:, 0, :], 1.0 / MDV, EPS, ALU.mult, ALU.add))
        rstd(dve, st, s[:, 1, :], s[:, 2, :], s[:, 3, :])
        for t in range(TT):
            for h in range(MH):
                dst = self.h[:, t, h * MDV:(h + 1) * MDV]
                st(dve.scalar_tensor_tensor(dst, dst, s[:, 2, t * MH + h:t * MH + h + 1],
                                            self.o[:, t, h * MDV:(h + 1) * MDV], ALU.mult, ALU.mult))


def layer1_stages(k, mods, base, small, guest):
    ar = k.arena
    ar.rest(base)
    qT, kT = ar.take(8, TOK), ar.take(8, TOK)
    o, h = ar.take(TT, 2 * D), ar.take(TT, 2 * D)
    v = ar.take(TT, MH, MDV + 2)
    at = ar.at
    tmp = ar.take(7, TOK)
    negm, acol, floor = ar.take(1, 4 * P)[:, 0, :], ar.take(TT, 64), ar.take(TT, 64)
    e = ar.take(4, 3 * P)
    sm = ar.take(4, 16)
    sc = ar.take(2, 5 * P)
    ar.rest(at)
    xh = ar.take(TT, D)
    junk = region(k, base).take(TT * MH, MDV)
    ar.rest(base)
    yo = operand(k, base, 16, base + 4 * TT * D)
    yT = ar.take(16, TOK)
    y, junk2 = ar.take(TT, D), ar.take(TT, D)

    class OnesColumn(Stage):

        def vector(self, dve, st):
            for t in range(TT):
                st(dve.memset(v[:, t, :, MDV:MDV + 2], 1.0))

    def q_act(act, st, i, bank):
        return act.activation(qT[:, 4 * i:4 * i + 2, :], bank.rearrange("p (a b) -> p a b", a=2),
                              ACT.Identity, scale=MDK ** -0.5)

    def q_dve(dve, st, i, bank):
        return dve.tensor_scalar(qT[:, 4 * i + 2:4 * i + 4, :], bank.rearrange("p (a b) -> p a b", a=2),
                                 MDK ** -0.5, None, ALU.mult)

    def v_act(act, st, i, bank):
        return act.activation(v[:, 0, 2 * i:2 * i + 2, 0:MDV], bank.rearrange("p (a b) -> p a b", a=2), ACT.Identity)

    def v_dve(dve, st, i, bank):
        return dve.tensor_copy(v[:, 1, 2 * i:2 * i + 2, 0:MDV], bank.rearrange("p (a b) -> p a b", a=2))

    def o_act(act, st, i, bank):
        return act.activation(o[:, 0, i * CN:(i + 1) * CN], bank, ACT.Sigmoid)

    def o_dve(dve, st, i, bank):
        return dve.tensor_copy(o[:, 1, i * CN:(i + 1) * CN], bank)

    outs = by_ranges((2, (q_act, q_dve)), (2, to_features(kT)), (4, (v_act, v_dve)), (4, (o_act, o_dve)))
    first = k.groups

    def act_after(act, st, i):
        if i == 11:
            act.wait_ge(k.dve_took, k.dve_groups[first + place("in1", 11) + 1])
            st(act.activation(o[:, 1, :], o[:, 1, :], ACT.Sigmoid))

    return [
        OnesColumn(k),
        Norm(k, k.x, KD, k.hT, mods[1][:, 1, :], mods[1][:, 0, :], xh, small),
        Narrow(k, [(4, 64, 64), (5, 64, 128)]),
        Product(k, "in1", k.hT_operand, *outs, act_after, None, guest=guest),
        GatePrep(k, tmp, negm, acol, floor),
        Mlstm(k, qT, kT, v, negm, acol, floor, h, e, sc, small),
        HeadNorm(k, h, o, sm, junk),
        Turn(k, h, 16, yT, scale=lambda f: k.par("head_norm")[:, f:f + 1]),
        Product(k, "out1", yo, *to_rows(y)),
        Post(k, y, mods[1][:, 2, :], junk2, small),
        *mlp(k, 1, mods[1], base, small, None),
    ]


class HeadScale(Stage):

    def __init__(self, k, y, heads, w, factor, sq, small, extra=None):
        super().__init__(k)
        self.y, self.heads, self.w, self.factor, self.extra = y, heads, w, factor, extra
        self.sq, self.small = sq, small

    def vector(self, dve, st):
        s, w = self.small, self.w
        heads = lambda a: a.rearrange("p (h w) -> p h w", w=w)
        for t in range(TT):
            st(dve.tensor_tensor(self.sq[:, t, :], self.y[:, t, :], self.y[:, t, :], ALU.mult))
        st.wait()
        for t in range(TT):
            st(dve.tensor_reduce(s[:, 3, t, :], heads(self.sq[:, t, :]), AX, ALU.add))
        st.wait()
        st(dve.tensor_scalar(s[:, 0], s[:, 3], 1.0 / w, EPS, ALU.mult, ALU.add))
        rstd(dve, st, s[:, 0], s[:, 1], s[:, 2])
        for lo, hi, f in self.factor:
            if f != 1.0:
                st(dve.tensor_scalar(s[:, 1, :, lo:hi], s[:, 1, :, lo:hi], f, None, ALU.mult))
        st.wait()
        for t in range(TT):
            st(dve.tensor_tensor(heads(self.y[:, t, :]), heads(self.y[:, t, :]),
                                 s[:, 1, t, :].unsqueeze(2).broadcast_to([P, self.heads, w]), ALU.mult))
        if self.extra is not None:
            st.wait()
            for t in range(TT):
                st(dve.tensor_tensor(self.y[:, t, :], self.y[:, t, :], self.extra[:, t, :], ALU.mult))


class ForgetGate(Stage):

    def __init__(self, k, tmp, negc):
        super().__init__(k)
        self.tmp, self.negc = tmp, negc
        self.m = {"biased": k.mark("biased", 1), "log_in": k.mark("log_in", 1)}

    def scalar(self, act, st):
        softplus_scalar(act, st, self.k, self.tmp[0:32, 0, :], self.tmp[0:32, 1, :], self.m["biased"].at(1),
                        self.m["log_in"])

    def vector(self, dve, st):
        k, m, t = self.k, self.m, self.tmp
        dve.tensor_scalar(t[0:32, 0, :], k.ps[0:32, 4, 0:TOK], k.par("fbias")[0:32, :], None, ALU.add) \
           .then_inc(m["biased"].sem, 1)
        dve.wait_ge(*m["log_in"].at(1))
        st(dve.scalar_tensor_tensor(t[0:32, 2, :], t[0:32, 0, :], 0.0, t[0:32, 1, :], ALU.min, ALU.subtract))
        st.wait()
        st(dve.tensor_scalar(t[0:32, 2, :], t[0:32, 2, :], -1.0, None, ALU.mult))
        st.wait()
        st(dve.tensor_tensor_scan(self.negc[0:32, :], k.con("ones")[0:32, :], t[0:32, 2, :], 0.0,
                                  ALU.mult, ALU.add))


class S5Prep(Stage):

    def __init__(self, k, v, bb, spread, bT, mag, turns):
        super().__init__(k)
        self.v, self.bb, self.spread, self.bT, self.mag, self.turns = v, bb, spread, bT, mag, turns
        self.m = {"phase": k.mark("s5_phase", 2), "exp": k.mark("s5_exp", 2), "sin": k.mark("s5_sin", 2),
                  "spread": k.mark("s5_spread", 8), "turned": k.mark("s5_turned", 8),
                  "taken": k.mark("s5_taken", 8)}

    def scalar(self, act, st):
        k, m, v = self.k, self.m, self.v
        act.activation(v[:, 0, :], k.par("s5_log_dt"), ACT.Exp).then_inc(m["exp"].sem, 1)
        act.wait_ge(*m["phase"].at(1))
        act.activation(self.mag, v[:, 1, :], ACT.Exp).then_inc(m["exp"].sem, 1)
        act.wait_ge(*m["phase"].at(2))
        act.activation(v[:, 3, :], self.turns, ACT.Sin, scale=SIN_TURN).then_inc(m["sin"].sem, 1)
        act.activation(v[:, 4, :], self.turns, ACT.Sin, scale=SIN_TURN / 2).then_inc(m["sin"].sem, 1)

    def tensor(self, pe):
        k, m = self.k, self.m
        for n in range(8):
            pe.wait_ge(*m["spread"].at(n + 1))
            if n >= 2:
                pe.wait_ge(*m["taken"].at(n - 1))
            for j in range(4):
                last = pe.transpose(k.ps[:, n % 2, j * P:(j + 1) * P], self.spread[:, n % 2, j, :], k.con("ident"))
            last.then_inc(m["turned"].sem, 1)

    def vector(self, dve, st):
        k, m, v = self.k, self.m, self.v
        ar, ai = k.par("s5_a_re"), k.par("s5_a_im")
        dt, x, th, s1, s2, em, cm1, nr, ni, cr, ci, den, t1, t2, cos = (v[:, j, :] for j in range(15))

        def do(ins):
            st(ins)
            st.wait()

        dve.wait_ge(*m["exp"].at(1))
        dve.tensor_tensor(x, dt, ar, ALU.mult).then_inc(m["phase"].sem, 1)
        do(dve.tensor_tensor(th, dt, ai, ALU.mult))
        do(dve.tensor_scalar(t1, th, 1.0 / (2.0 * np.pi), ROUND, ALU.mult, ALU.add))
        do(dve.tensor_scalar(t1, t1, ROUND, None, ALU.subtract))
        dve.scalar_tensor_tensor(self.turns, th, 1.0 / (2.0 * np.pi), t1, ALU.mult, ALU.subtract) \
           .then_inc(m["phase"].sem, 1)
        dve.wait_ge(*m["phase"].at(2))
        do(dve.tensor_scalar(t1, x, 0.5, -0.5, ALU.min, ALU.max))
        do(dve.tensor_scalar(em, t1, 1.0 / 9, 1.0, ALU.mult, ALU.add))
        for n in range(8, 1, -1):
            do(dve.tensor_tensor(em, em, t1, ALU.mult))
            do(dve.tensor_scalar(em, em, 1.0 / n, 1.0, ALU.mult, ALU.add))
        do(dve.tensor_tensor(em, em, t1, ALU.mult))
        do(dve.tensor_tensor(t2, t1, x, ALU.is_equal))
        dve.wait_ge(*m["exp"].at(2))
        do(dve.tensor_scalar(t1, self.mag, 1.0, None, ALU.subtract))
        do(dve.tensor_tensor(em, em, t1, ALU.subtract))
        do(dve.tensor_tensor(em, em, t2, ALU.mult))
        do(dve.tensor_tensor(em, em, t1, ALU.add))
        dve.wait_ge(*m["sin"].at(2))
        do(dve.tensor_tensor(cm1, s2, s2, ALU.mult))
        do(dve.tensor_scalar(cm1, cm1, -2.0, None, ALU.mult))
        do(dve.tensor_scalar(cos, cm1, 1.0, None, ALU.add))
        do(dve.tensor_tensor(nr, em, cos, ALU.mult))
        do(dve.tensor_tensor(nr, nr, cm1, ALU.add))
        do(dve.tensor_tensor(ni, self.mag, s1, ALU.mult))
        do(dve.tensor_tensor(t1, ar, ar, ALU.mult))
        do(dve.tensor_tensor(t2, ai, ai, ALU.mult))
        do(dve.tensor_tensor(den, t1, t2, ALU.add))
        do(dve.reciprocal(den, den))
        do(dve.tensor_tensor(t1, nr, ar, ALU.mult))
        do(dve.tensor_tensor(t2, ni, ai, ALU.mult))
        do(dve.tensor_tensor(cr, t1, t2, ALU.add))
        do(dve.tensor_tensor(cr, cr, den, ALU.mult))
        do(dve.tensor_tensor(t1, ni, ar, ALU.mult))
        do(dve.tensor_tensor(t2, nr, ai, ALU.mult))
        do(dve.tensor_tensor(ci, t1, t2, ALU.subtract))
        do(dve.tensor_tensor(ci, ci, den, ALU.mult))
        tiles = lambda a: a.rearrange("p (i h) -> p i h", h=16)
        br, bi = tiles(k.par("s5_b_re")), tiles(k.par("s5_b_im"))
        wide = lambda a: a.unsqueeze(2).broadcast_to([P, S5T, 16])
        bbr, bbi, t3 = self.bb[:, 0], self.bb[:, 1], self.bb[:, 2]
        do(dve.tensor_tensor(bbr, br, wide(cr), ALU.mult))
        do(dve.tensor_tensor(t3, bi, wide(ci), ALU.mult))
        do(dve.tensor_tensor(bbr, bbr, t3, ALU.subtract))
        do(dve.tensor_tensor(bbi, bi, wide(cr), ALU.mult))
        do(dve.tensor_tensor(t3, br, wide(ci), ALU.mult))
        do(dve.tensor_tensor(bbi, bbi, t3, ALU.add))
        do(dve.memset(self.spread, 0.0))

        def take(n):
            dve.wait_ge(*m["turned"].at(n + 1))
            dve.tensor_copy(self.bT[:, n % 2, 4 * (n // 2):4 * (n // 2) + 4, :],
                            k.ps[:, n % 2, :].rearrange("p (j s) -> p j s", j=4)).then_inc(m["taken"].sem, 1)

        for n in range(8):
            if n >= 2:
                take(n - 2)
            src = self.bb[:, n % 2, 4 * (n // 2):4 * (n // 2) + 4, :]
            for j in range(4):
                for half in range(2):
                    rows = slice(64 * half, 64 * half + 64)
                    at = 32 * j + 16 * half
                    ins = dve.tensor_copy(self.spread[rows, n % 2, j, at:at + 16], src[rows, j, :])
                    if j == 3 and half == 1:
                        ins.then_inc(m["spread"].sem, 1)
                    else:
                        st(ins)
        take(6)
        take(7)


SIN_TURN = 6.283185
ROUND = 1.5 * 2.0 ** 23


class S5(Stage):

    def __init__(self, k, uT, bT, mag, turns, spread, tab, rot, hh, z, zs):
        super().__init__(k)
        self.uT, self.bT, self.mag, self.turns = uT, bT, mag, turns
        self.spread, self.tab, self.rot, self.hh, self.z, self.zs = spread, tab, rot, hh, z, zs
        self.m = {"phase": k.mark("s5_phases", S5T), "sin": k.mark("s5_sines", S5T),
                  "drive": k.mark("s5_drive", S5T), "dused": k.mark("s5_drive_used", S5T),
                  "h": k.mark("s5_states", S5T), "c": k.mark("s5_c_spread", 4),
                  "y": k.mark("s5_tile_used", S5T), "z": k.mark("s5_z", 4)}

    def tensor(self, pe):
        k, m = self.k, self.m

        def drive(i):
            if i >= 2:
                pe.wait_ge(*m["dused"].at(i - 1))
            for c in range(2):
                mm = pe.matmul(k.ps[:, i % 2, c * TOK:(c + 1) * TOK], self.bT[:, c, i, :], self.uT[:, i // 4, :],
                               start=True, stop=True)
            mm.then_inc(m["drive"].sem, 1)

        def out(i):
            q, j = i // 4, i % 4
            if j == 0:
                pe.wait_ge(*m["c"].at(q + 1))
            pe.wait_ge(*m["h"].at(i + 1))
            for c in range(2):
                mm = pe.matmul(k.ps[:, 4 + q, 0:TOK], self.spread[:, q % 2, c, j, :], self.hh[:, i % 2, c, :],
                               start=j == 0 and c == 0, stop=j == 3 and c == 1)
            mm.then_inc(m["y"].sem, 1)

        for i in range(S5T + 1):
            if i < S5T:
                drive(i)
            if i >= 1:
                out(i - 1)

    def scalar(self, act, st):
        k, m = self.k, self.m
        for i in range(S5T):
            act.wait_ge(*m["phase"].at(i + 1))
            if i >= 2:
                act.wait_ge(*m["h"].at(i - 1))
            r = self.tab[:, i % 2, 0, :]
            act.activation(self.tab[:, i % 2, 1, :], r, ACT.Sin, scale=SIN_TURN)
            act.activation(self.tab[:, i % 2, 2, :], r, ACT.Sin, scale=SIN_TURN / 2).then_inc(m["sin"].sem, 1)
        for q in range(4):
            act.wait_ge(*m["z"].at(q + 1))
            st(act.activation(self.z[:, q, :], self.z[:, q, :], ACT.Gelu_apprx_tanh))

    def vector(self, dve, st):
        k, m = self.k, self.m

        def do(ins):
            st(ins)
            st.wait()

        do(dve.memset(self.spread, 0.0))

        def phases(i):
            r, n = self.tab[:, i % 2, 0, :], self.rot[:, 6, :]
            f = self.turns[:, i:i + 1]
            if i >= 1:
                dve.wait_ge(*m["phase"].at(i))
            if i >= 2:
                dve.wait_ge(*m["sin"].at(i - 1))
            do(dve.tensor_scalar(n, k.con("time"), f, ROUND, ALU.mult, ALU.add))
            do(dve.tensor_scalar(n, n, ROUND, None, ALU.subtract))
            dve.scalar_tensor_tensor(r, k.con("time"), f, n, ALU.mult, ALU.subtract).then_inc(m["phase"].sem, 1)

        phases(0)
        for i in range(S5T):
            q, j = i // 4, i % 4
            if j == 0:
                if q >= 2:
                    dve.wait_ge(*m["y"].at(4 * (q - 1)))
                for c, name, sign in ((0, "s5_c_re", 1.0), (1, "s5_c_im", -1.0)):
                    src = k.par(name).rearrange("p (i h) -> p i h", h=16)
                    for jj in range(4):
                        for half in range(2):
                            rows, at = slice(64 * half, 64 * half + 64), 32 * jj + 16 * half
                            ins = dve.tensor_scalar(self.spread[rows, q % 2, c, jj, at:at + 16],
                                                    src[rows, 4 * q + jj, :], sign, None, ALU.mult)
                            if c == 1 and jj == 3 and half == 1:
                                ins.then_inc(m["c"].sem, 1)
                            else:
                                st(ins)
            if i + 1 < S5T:
                phases(i + 1)
            sin, cos = self.tab[:, i % 2, 1, :], self.tab[:, i % 2, 2, :]
            a, b, c_, d, gr, gi = (self.rot[:, n, :] for n in range(6))
            if i >= 1:
                dve.wait_ge(*m["h"].at(i))
            dve.wait_ge(*m["sin"].at(i + 1))
            do(dve.tensor_tensor(cos, cos, cos, ALU.mult))
            do(dve.tensor_scalar(cos, cos, -2.0, 1.0, ALU.mult, ALU.add))
            dve.wait_ge(*m["drive"].at(i + 1))
            dr, di = k.ps[:, i % 2, 0:TOK], k.ps[:, i % 2, TOK:2 * TOK]
            st(dve.tensor_tensor(a, dr, cos, ALU.mult))
            st(dve.tensor_tensor(b, di, sin, ALU.mult))
            st(dve.tensor_tensor(c_, di, cos, ALU.mult))
            dve.tensor_tensor(d, dr, sin, ALU.mult).then_inc(m["dused"].sem, 1)
            dve.wait_ge(*m["dused"].at(i + 1))
            st(dve.tensor_tensor(a, a, b, ALU.add))
            st(dve.tensor_tensor(c_, c_, d, ALU.subtract))
            st.wait()
            mag = self.mag[:, i:i + 1].broadcast_to([P, TOK])
            st(dve.tensor_tensor_scan(gr, mag, a, 0.0, ALU.mult, ALU.add))
            st(dve.tensor_tensor_scan(gi, mag, c_, 0.0, ALU.mult, ALU.add))
            st.wait()
            st(dve.tensor_tensor(a, gr, cos, ALU.mult))
            st(dve.tensor_tensor(b, gi, sin, ALU.mult))
            st(dve.tensor_tensor(c_, gr, sin, ALU.mult))
            st(dve.tensor_tensor(d, gi, cos, ALU.mult))
            st.wait()
            if i >= 2:
                dve.wait_ge(*m["y"].at(i - 1))
            st(dve.tensor_tensor(self.hh[:, i % 2, 0, :], a, b, ALU.subtract))
            dve.tensor_tensor(self.hh[:, i % 2, 1, :], c_, d, ALU.add).then_inc(m["h"].sem, 1)
        for q in range(4):
            dve.wait_ge(*m["y"].at(4 * q + 4))
            dve.scalar_tensor_tensor(self.z[:, q, :], self.uT[:, q, :], k.par("s5_d")[:, q:q + 1],
                                     k.ps[:, 4 + q, 0:TOK], ALU.mult, ALU.add).then_inc(m["z"].sem, 1)


class HgrnPrep(Stage):

    def __init__(self, k, f, b, tmp):
        super().__init__(k)
        self.f, self.b, self.tmp = f, b, tmp
        self.m = {"log_in": k.mark("log_in", 1)}

    def scalar(self, act, st):
        t, f = self.tmp, self.f
        st(act.activation(t, f, ACT.Abs))
        st.wait()
        st(act.activation(t, t, ACT.Exp, scale=-1.0))
        st.wait()
        act.activation(t, t, ACT.Ln, bias=self.k.con("ones")[:, 0:1]).then_inc(self.m["log_in"].sem, 1)

    def vector(self, dve, st):
        dve.wait_ge(*self.m["log_in"].at(1))
        st(dve.scalar_tensor_tensor(self.tmp, self.f, 0.0, self.tmp, ALU.min, ALU.subtract))
        st.wait()
        for c in range(2):
            for h in range(HGH):
                st(dve.tensor_tensor_scan(self.b[:, c, h, :], self.k.con("ones")[:, 0:P],
                                          self.tmp[:, h, c * P:(c + 1) * P], 0.0, ALU.mult, ALU.add))


class Hgrn(Stage):

    def __init__(self, k, qT, key, b, v, o, ar, ar2):
        super().__init__(k)
        self.q, self.key, self.b, self.v, self.o = qT, key, b, v, o
        self.arg, self.qs, self.ks = ar.take(2, 512), ar.take(2, 512), ar.take(2, 512)
        self.acc, self.part = ar2.take(3, 512), ar2.take(2, 512)
        self.LV = 8
        n = 2 * self.LV + 1
        self.n = n
        self.m = {"arg": k.mark("hg_args", n), "exp": k.mark("hg_exp", n), "ops": k.mark("hg_operands", n),
                  "prod": k.mark("hg_products", n), "took": k.mark("hg_taken", n), "o": k.mark("hg_out", 2)}

    def steps(self):
        i = 0
        for c in range(2):
            for m in (64, 32, 16, 8, 4, 2, 1, 0):
                yield i, c, m
                i += 1
        yield i, 1, -1

    def tensor(self, pe):
        k, m = self.k, self.m
        for i, c, half in self.steps():
            if i >= 2:
                pe.wait_ge(*m["took"].at(i - 1))
            pe.wait_ge(*m["ops"].at(i + 1))
            for h in range(HGH):
                at = slice(h * P, (h + 1) * P)
                mm = pe.matmul(k.ps[:, i % 2, at], self.ks[:, i % 2, at], self.qs[:, i % 2, at], start=True,
                               stop=True)
            mm.then_inc(m["prod"].sem, 1)
        pe.wait_ge(*m["took"].at(self.n))
        for t in range(TT):
            parts = [(self.acc[:, 0, :], 0)] if t == 0 else [(self.acc[:, 2, :], 0), (self.acc[:, 1, :], 1)]
            for h in range(HGH):
                at = slice(h * P, (h + 1) * P)
                for n, (w, s) in enumerate(parts):
                    mm = pe.matmul(k.ps[:, 4 + t, at], w[:, at], self.v[:, s, at], start=n == 0,
                                   stop=n == len(parts) - 1)
            mm.then_inc(m["o"].sem, 1)

    def scalar(self, act, st):
        m = self.m
        for i, c, half in self.steps():
            act.wait_ge(*m["arg"].at(i + 1))
            a = self.arg[:, i % 2, :]
            if half == -1:
                st(act.activation(self.b[:, 1], self.b[:, 1], ACT.Exp))
            act.activation(a, a, ACT.Exp).then_inc(m["exp"].sem, 1)
        act.wait_ge(*m["o"].at(1))
        st(act.activation(self.o[:, 0, :], self.k.ps[:, 4, :], ACT.Identity))

    def vector(self, dve, st):
        k, m = self.k, self.m
        tok = lambda a, c: a[:, :, c * P:(c + 1) * P]
        flat = lambda a: a.rearrange("p h t -> p (h t)")

        def blocks(a, half):
            return a.rearrange("p (n u m) -> p n u m", u=2, m=half)

        st(dve.memset(self.qs, 0.0))
        st(dve.memset(self.ks, 0.0))
        st.wait()

        def args(i, c, half):
            a = self.arg[:, i % 2, :]
            if half > 0:
                b, a4 = blocks(flat(self.b[:, c]), half), blocks(a, half)
                mid = b[:, :, 0, half - 1:half].broadcast_to([P, 256 // half, half])
                st(dve.tensor_tensor(a4[:, :, 1, :], b[:, :, 1, :], mid, ALU.subtract))
                dve.tensor_tensor(a4[:, :, 0, :], mid, b[:, :, 0, :], ALU.subtract).then_inc(m["arg"].sem, 1)
            elif half == 0:
                dve.memset(a, 0.0).then_inc(m["arg"].sem, 1)
            else:
                b = self.b[:, 0]
                end = b[:, :, P - 1:P].broadcast_to([P, HGH, P])
                dve.tensor_tensor(a.rearrange("p (h t) -> p h t", h=HGH), end, b, ALU.subtract) \
                   .then_inc(m["arg"].sem, 1)

        def operands(i, c, half):
            a, qs, ks = self.arg[:, i % 2, :], self.qs[:, i % 2, :], self.ks[:, i % 2, :]
            dve.wait_ge(*m["exp"].at(i + 1))
            if i >= 2:
                dve.wait_ge(*m["prod"].at(i - 1))
            heads = lambda x: x.rearrange("p (h t) -> p h t", h=HGH)
            if half > 0:
                bl = lambda x: x.rearrange("p h (n u m) -> p h n u m", u=2, m=half)
                st(dve.tensor_tensor(bl(heads(qs))[:, :, :, 1, :], bl(tok(self.q, c))[:, :, :, 1, :],
                                     bl(heads(a))[:, :, :, 1, :], ALU.mult))
                dve.tensor_tensor(bl(heads(ks))[:, :, :, 0, :], bl(tok(self.key, c))[:, :, :, 0, :],
                                  bl(heads(a))[:, :, :, 0, :], ALU.mult).then_inc(m["ops"].sem, 1)
            elif half == 0:
                st(dve.tensor_copy(heads(qs), tok(self.q, c)))
                dve.tensor_copy(heads(ks), tok(self.key, c)).then_inc(m["ops"].sem, 1)
            else:
                st(dve.tensor_tensor(heads(ks), tok(self.key, 0), heads(a), ALU.mult))
                dve.tensor_tensor(heads(qs), tok(self.q, 1), self.b[:, 1], ALU.mult).then_inc(m["ops"].sem, 1)

        def take(i, c, half):
            dve.wait_ge(*m["prod"].at(i + 1))
            ps = k.ps[:, i % 2, :].rearrange("p (h t) -> p h t", h=HGH)
            lv = i % self.LV
            if half == -1:
                dve.tensor_copy(self.acc[:, 2, :], k.ps[:, i % 2, :]).then_inc(m["took"].sem, 1)
                return
            mask = k.con("levels")[:, lv * P:(lv + 1) * P].unsqueeze(1).broadcast_to([P, HGH, P])
            acc = self.acc[:, c, :]
            dst = acc if lv == 0 else self.part[:, i % 2, :]
            dve.tensor_tensor(dst.rearrange("p (h t) -> p h t", h=HGH), ps, mask, ALU.mult) \
               .then_inc(m["took"].sem, 1)
            if lv:
                dve.wait_ge(*m["took"].at(i + 1))
                st(dve.tensor_tensor(acc, acc, self.part[:, i % 2, :], ALU.add))
                st.wait()

        todo = list(self.steps())
        args(*todo[0])
        for n, step in enumerate(todo):
            if n + 1 < len(todo):
                if n >= 1:
                    dve.wait_ge(*m["ops"].at(n))
                args(*todo[n + 1])
            operands(*step)
            if n >= 1:
                take(*todo[n - 1])
        take(*todo[-1])
        dve.wait_ge(*m["o"].at(2))
        st(dve.tensor_copy(self.o[:, 1, :], k.ps[:, 5, :]))


def in2_stage(k, fqk, fv, suT, hqT, fT, key, hi, hg, gl):
    def silu_pair(dst, rows):
        def act_out(act, st, i, bank):
            if rows:
                return act.activation(dst[:, 0, i * CN:(i + 1) * CN], bank, ACT.Silu)
            return act.activation(dst[:, 0:2, :], bank.rearrange("p (a b) -> p a b", a=2), ACT.Silu)

        def dve_out(dve, st, i, bank):
            if rows:
                return dve.tensor_copy(dst[:, 1, i * CN:(i + 1) * CN], bank)
            return dve.tensor_copy(dst[:, 2:4, :], bank.rearrange("p (a b) -> p a b", a=2))
        return act_out, dve_out

    def gate_act(act, st, i, bank):
        return act.activation(gl[:, 0, i * CN:(i + 1) * CN], bank, ACT.Sigmoid)

    def gate_dve(dve, st, i, bank):
        return dve.tensor_copy(gl[:, 1, i * CN:(i + 1) * CN], bank)

    first = k.groups

    def act_after(act, st, i):
        def copied(g):
            act.wait_ge(k.dve_took, k.dve_groups[first + g + 1])
        if i == 7:
            copied(4)
            st(act.activation(hqT[:, 2:4, :], hqT[:, 2:4, :], ACT.Silu))
            copied(7)
            st(act.activation(hg[:, 1, :], hg[:, 1, :], ACT.Silu))
        if i == 8:
            copied(5)
            st(act.activation(key[:, :, :], fT[:, :, :], ACT.Sigmoid, scale=-1.0))
        if i == 13:
            copied(13)
            st(act.activation(gl[:, 1, :], gl[:, 1, :], ACT.Sigmoid))

    outs = by_ranges((2, to_rows(fqk)), (1, to_rows(fv)), (1, to_features(suT)), (1, silu_pair(hqT, False)),
                     (1, to_features(fT)), (1, to_rows(hi)), (1, silu_pair(hg, True)), (6, (gate_act, gate_dve)))
    return Product(k, "in2", k.hT_operand, *outs, act_after, None)


class DveProduct(Product):

    def __init__(self, k, name, src, take):
        super().__init__(k, name, src, None, None)
        self.take = take

    def take_group(self, dve, st, i, n):
        b = 2 * ((self.first_group + i) % 2)
        return self.take(dve, st, n, self.k.ps[:, b:b + 2, :])


def add_to_x(k):
    def take(dve, st, i, banks):
        at = slice(i * CN, (i + 1) * CN)
        return dve.tensor_tensor(k.x[:, :, at], k.x[:, :, at], banks, ALU.add)
    return take


def branch(k, name, src, gl, n):
    def take(dve, st, i, banks):
        at = slice(n * D + i * CN, n * D + (i + 1) * CN)
        if n == 0:
            return dve.tensor_tensor(gl[:, :, at], gl[:, :, at], banks, ALU.mult)
        st(dve.tensor_tensor(gl[:, :, at], gl[:, :, at], banks, ALU.mult))
        st.wait()
        to = slice(i * CN, (i + 1) * CN)
        return dve.tensor_tensor(gl[:, :, to], gl[:, :, to], gl[:, :, at], ALU.add)
    return DveProduct(k, name, src, take)


class LoadMem(Stage):
    def __init__(self, k, dst, mem):
        super().__init__(k)
        self.dst, self.mem = dst, mem
        self.m = k.mark("mem_loaded", 16)

    def gpsimd(self, pool, st):
        pool.dma_start(self.dst, self.mem[0].rearrange("(t p) d -> p t d", p=P)).then_inc(self.m.sem, 16)

    def scalar(self, act, st):
        act.wait_ge(*self.m.at(16))


def block2_stages(k, base, small, mem):
    ar = k.arena
    ar.rest(base)
    fqk, fv = ar.take(TT, D), ar.take(TT, 512)
    suT, hqT, fT, key = (ar.take(4, TOK) for _ in range(4))
    hi, hg, gl = ar.take(TT, 512), ar.take(TT, 512), ar.take(TT, 3 * D)
    at_su, at_fox = base + 3 * D, ar.at
    foxT = ar.take(4, TOK)
    work = ar.at
    xh = ar.take(TT, D)
    ar.rest(work)
    tmp, negc, fo, sm = ar.take(3, TOK), ar.take(1, TOK)[:, 0, :], ar.take(TT, 512), ar.take(8, 16)
    sm4 = sm.rearrange("p a b -> p (a b)").rearrange("p (a t h) -> p a t h", a=4, t=TT)
    stages = [
        Norm(k, k.x, KD, k.hT, k.par("norm_mix"), None, xh, small),
        Narrow(k, [(4, 32, 192)]),
        in2_stage(k, fqk, fv, suT, hqT, fT, key, hi, hg, gl),
    ]
    at_att = ar.at
    sqf = ar.take(TT, D)
    ar.rest(at_att)
    stages += [
        ForgetGate(k, tmp, negc),
        HeadScale(k, fqk, 16, 64, [(0, 8, HP ** -0.5), (8, 16, 1.0)], sqf, sm4),
    ]
    ar.rest(at_att)
    qkT = ar.take(8, TOK)
    stages.append(Turn(k, fqk, 8, qkT, scale=lambda f: k.par("fox_qnorm" if f < 4 else "fox_knorm")))

    def lead(pe, h, bank):
        pe.matmul(bank, k.mask_bf[:, 10 * P:11 * P], k.mask_bf[:, 6 * P:10 * P], start=True, stop=False,
                  skip_group_check=True)
        pe.matmul(bank, k.con("ident")[0:32, h:h + 1].broadcast_to([32, P]),
                  negc[0:32, :].unsqueeze(1).broadcast_to([32, 2, TOK]), start=False, stop=False,
                  skip_group_check=True)

    fox = Attention(k, FOXH, 64,
                    lambda h, t: [qkT[64 * (h % 2):64 * (h % 2) + 64, h // 2, t * P:(t + 1) * P]],
                    lambda h: [qkT[64 * (h % 2):64 * (h % 2) + 64, 4 + h // 2, :]],
                    lambda h, s: fv[:, s, h * 64:(h + 1) * 64], fo, ar,
                    lead=lead)
    stages += [fox, Turn(k, fo, 4, foxT)]

    ar.rest(base)
    turns, mag, z = ar.take(1, 16)[:, 0, :], ar.take(1, 16)[:, 0, :], ar.take(4, TOK)
    rot = region(k, ar.at).take(7, TOK)
    v, bb = ar.take(15, 16), ar.take(3, S5T, 16)
    ar.rest(work)
    bT = ar.take(2, S5T * P).rearrange("p c (i s) -> p c i s", i=S5T)
    spread = k.hT[:, :, :].rearrange("p (a x) b -> p a (x b)", a=2).rearrange("p a (c j s) -> p a c j s", c=2, j=4)
    tab = ar.take(2, 3, TOK)
    hh = ar.take(2, 2, TOK)
    stages += [
        S5Prep(k, v, bb, spread[:, :, 0], bT, mag, turns),
        S5(k, suT, bT, mag, turns, spread, tab, rot, hh, z, None),
    ]
    s5T = suT
    zo = operand(k, base + 32, 4, work)
    z2 = region(k, work + 4 * TOK).take(4, TOK)

    def glu_act(act, st, i, bank):
        for f in range(2):
            ins = act.activation(s5T[:, f, :], bank[:, f * TOK:(f + 1) * TOK], ACT.Sigmoid,
                                 bias=k.par("s5_b_glu")[:, f:f + 1])
            if f == 0:
                st(ins)
        return ins

    def glu_dve(dve, st, i, bank):
        for f in range(2):
            ins = dve.tensor_scalar(s5T[:, 2 + f, :], bank[:, f * TOK:(f + 1) * TOK],
                                    k.par("s5_b_glu")[:, 2 + f:3 + f], None, ALU.add)
            if f == 0:
                st(ins)
        return ins

    first = k.groups

    def glu_act_after(act, st, i):
        act.wait_ge(k.dve_took, k.dve_groups[first + 1])
        st(act.activation(s5T[:, 2:4, :], s5T[:, 2:4, :], ACT.Sigmoid))

    class GluMul(Stage):

        def vector(self, dve, st):
            st(dve.tensor_tensor(z2, zo.hi.bitcast(F32), zo.lo.bitcast(F32), ALU.add))
            st.wait()
            st(dve.tensor_tensor(s5T, s5T, z2, ALU.mult))

    stages += [Product(k, "glu", zo, glu_act, glu_dve, glu_act_after, None), GluMul(k)]

    ar.rest(work)
    b = ar.take(2, HGH, P)
    ho = ar.take(TT, 512)
    at_h = ar.at
    hT4 = ar.take(4, TOK)
    dead = ar.at
    htmp = ar.take(4, TOK)
    ar.rest(dead)
    sm2, hsq = ar.take(4, TT, HGH), ar.take(TT, 512)
    ar.rest(dead)
    stages += [
        HgrnPrep(k, fT, b, htmp),
        Hgrn(k, hqT, key, b, hi, ho, ar, region(k, base)),
        HeadScale(k, ho, HGH, 128, [(0, 4, 1.0)], hsq, sm2, extra=hg),
        Turn(k, ho, 4, hT4, scale=lambda f: k.par("hg_onorm")),
        branch(k, "fox_out", operand(k, at_fox, 4, base), gl, 0),
        branch(k, "s5_out", operand(k, at_su, 4, base + D), gl, 1),
        branch(k, "hg_out", operand(k, at_h, 4, base + 2 * D), gl, 2),
        Turn(k, gl[:, :, 0:D], 8, k.hT),
        DveProduct(k, "mix_out", k.hT_operand, add_to_x(k)),
    ]

    ar.rest(base)
    mt, mT = ar.take(TT, D), ar.take(8, TOK)
    xk, xv, xq, xo, sq2, xh2 = (ar.take(TT, D) for _ in range(6))
    sm3 = ar.take(4, TT, 4)
    qT, kT = sq2.rearrange("p a b -> p (a b)").rearrange("p (a b) -> p a b", b=TOK), mT
    mo = operand(k, base + TT * D, 8, base)
    stages += [
        LoadMem(k, mt, mem),
        Norm(k, mt, KD, mT, k.par("norm_mem"), None, xh2, small),
        Product(k, "xk", mo, *to_rows(xk)),
        Product(k, "xv", mo, *to_rows(xv), is_split=True),
        Norm(k, k.x, KD, k.hT, k.par("norm_x"), None, xh2, small),
        Product(k, "xq", k.hT_operand, *to_rows(xq)),
        HeadScale(k, xk, 4, 256, [(0, 4, 1.0)], sq2, sm3),
        HeadScale(k, xq, 4, 256, [(0, 4, 256.0 ** -0.5)], sq2, sm3),
        Turn(k, xk, 8, kT, scale=lambda f: k.par("x_knorm")[:, f % 2:f % 2 + 1]),
        Turn(k, xq, 8, qT, scale=lambda f: k.par("x_qnorm")[:, f % 2:f % 2 + 1]),
        Attention(k, 4, 256,
                  lambda h, t: [qT[:, 2 * h + i, t * P:(t + 1) * P] for i in range(2)],
                  lambda h: [kT[:, 2 * h + i, :] for i in range(2)],
                  lambda h, s: xv[:, s, h * 256:(h + 1) * 256], xo, ar),
        Turn(k, xo, 8, k.hT),
        DveProduct(k, "xo", k.hT_operand, add_to_x(k)),
    ]

    ar.rest(base)
    u, xh3 = ar.take(FF2T, TOK), ar.take(TT, D)
    at_hi = ar.at
    swi = k.groups

    def a_act(act, st, i, bank):
        return act.activation(u[:, 2 * i:2 * i + 2, :], bank.rearrange("p (a b) -> p a b", a=2), ACT.Silu)

    def b_dve(dve, st, i, bank):
        dve.wait_ge(k.act_took, k.act_groups[swi + i + 1])
        dst = u[:, 2 * i:2 * i + 2, :]
        return dve.tensor_tensor(dst, dst, bank.rearrange("p (a b) -> p a b", a=2), ALU.mult)

    stages += [
        Norm(k, k.x, KD, k.hT, k.par("norm_ffn"), None, xh3, small),
        Product(k, "gate_up", k.hT_operand, a_act, b_dve),
        DveProduct(k, "swi_down", operand(k, base, FF2T, at_hi), add_to_x(k)),
    ]
    return stages


def all_stages(k, mem):
    ar = k.arena
    small, mods = ar.take(1, 72)[:, 0, :], [ar.take(6, KD) for _ in range(2)]
    base = ar.at
    stages = [Setup(k)]

    zs = ar.take(TT, D)
    at_b = ar.at
    xp, xc = ar.take(12, TOK + 4), ar.take(12, TOK)
    at_c = ar.at
    qT, kT, v = ar.take(8, TOK), ar.take(8, TOK), ar.take(TT, D)
    at_d = ar.at
    xf, xb = ar.take(TT, D), ar.take(TT, D)
    at_e = ar.at
    cbf, cbb = ar.take(2, 3 * P), ar.take(2, 3 * P)
    cs4, csn, dtc, tmp = ar.take(1, 512)[:, 0, :], ar.take(TT, 64), ar.take(TT, 64), ar.take(5, TOK)
    ar.rest(at_b)
    xt = ar.take(TT, D)
    ar.rest(at_b + 12 * (TOK + 4))
    e = ar.take(4, 3 * P)
    ar.rest(at_c)
    xh = ar.take(TT, D)
    ar.rest(at_d)
    yT = ar.take(16, TOK)
    ar.rest(at_b)
    table = ar.take(1, NH * 6 * GRID)[:, 0, :]
    ar.rest(at_b)
    y = ar.take(TT, D)
    junk = ar.take(TT, D)
    ar.rest(at_e)
    stages += [
        Product(k, "ada", None, None, None, guest=ada_take(k, mods, 0)),
        Inputs(k),
        Pads(k, xp),
        Norm(k, k.x, KD, k.hT, mods[0][:, 1, :], mods[0][:, 0, :], xh, small),
        Narrow(k, [(4, 64, 0)]),
        in0_stage(k, xp, xc, zs, qT, kT, v, ada_take(k, mods, 4)),
        SsdPrep(k, xc, xt, xf, xb, cbf, cbb, cs4, csn, dtc, tmp),
        Ssd(k, xt, xf, xb, cbf, cbb, cs4, csn, zs, e),
        Norm(k, zs, KD, yT[:, 0:8, :], k.par("ssd_norm"), None, xt, small),
        BiasTable(k, table),
        Attention(k, NH, HP,
                  lambda h, t: [qT[64 * (h % 2):64 * (h % 2) + 64, h // 2, t * P:(t + 1) * P]],
                  lambda h: [kT[64 * (h % 2):64 * (h % 2) + 64, h // 2, :]],
                  lambda h, s: v[:, s, h * HP:(h + 1) * HP], zs, ar,
                  table=lambda h, t: table.rearrange("p (h u c) -> p h (u c)", h=NH, u=6)
                  [:, h, GRID * (2 - 2 * t):GRID * (6 - 2 * t)]),
        Turn(k, zs, KD, yT[:, 8:16, :]),
        Product(k, "out0", operand(k, at_d, 16, at_c), *to_rows(y)),
        Post(k, y, mods[0][:, 2, :], junk, small),
    ]
    stages += mlp(k, 0, mods[0], base, small, ada_take(k, mods, 12))
    stages += layer1_stages(k, mods, base, small, ada_take(k, mods, 16))
    stages += block2_stages(k, 72, small, mem)
    return stages


def mlp(k, layer, mod, base, small, guest):
    ar = k.arena
    ar.rest(base)
    uo = operand(k, base, 32, base + 32 * TOK)
    ar.rest(base + 2 * 32 * TOK)
    y, xh = ar.take(TT, D), ar.take(TT, D)
    return [Norm(k, k.x, KD, k.hT, mod[:, 4, :], mod[:, 3, :], xh, small),
            *mlp_stages(k, layer, uo, y, guest),
            Post(k, y, mod[:, 5, :], xh, small)]


def program(nc, x, stream, params, consts, narrow, mem, out, where_p, where_c):
    with ExitStack() as ctx:
        k = Core(nc, ctx, params.shape[1], consts.shape[1], narrow.shape, where_p, where_c)
        stages = all_stages(k, mem)
        result = k.x[:, :, :]
        steps = {n: k.sem(f"{n}_steps") for n in ("act", "dve", "pool")}
        out_stored = k.sem("out_stored")
        block = ctx.enter_context(nc.Block())

        def meet(eng, n):
            eng.drain().then_inc(k.stage_done, 1)
            eng.wait_ge(k.stage_done, 3 * (n + 1))

        @block.sync
        def _(sp):
            sp.dma_start(k.par_all[:, :], params).then_inc(k.params_in, 16)

            def load(c, slot):
                sp.dma_start(k.ring[:, slot, :, :], stream[c]).then_inc(k.loaded[slot], 16)

            for c in range(min(RING, k.chunks)):
                load(c, c)
            for c in range(RING, AHEAD):
                sp.wait_ge(k.chunk_used, c - RING + 1)
                load(c, c % RING)
            sp.dma_start(k.x[:, :, :], x[0].rearrange("(t p) d -> p t d", p=P)).then_inc(k.inputs_in, 16)
            sp.dma_start(k.con_all[:, :], consts).then_inc(k.inputs_in, 16)
            sp.dma_start(k.narrow[:, :, :], narrow).then_inc(k.inputs_in, 16)
            done = AHEAD // RING
            rounds = k.chunks // RING
            if rounds > done:
                with sp.Fori(done, rounds) as r:
                    for slot in range(RING):
                        sp.wait_ge(k.chunk_used, r * RING + (slot - RING + 1))
                        load(r * RING + slot, slot)
            for c in range(RING * rounds, k.chunks):
                sp.wait_ge(k.chunk_used, c - RING + 1)
                load(c, c % RING)
            sp.wait_ge(k.stage_done, 3 * len(stages))
            sp.dma_start(out[0].rearrange("(t p) d -> p t d", p=P), result).then_inc(out_stored, 16)
            sp.wait_ge(out_stored, 16)

        @block.tensor
        def _(pe):
            for n, stage in enumerate(stages):
                stage.tensor(pe)
                meet(pe, n)

        @block.scalar
        def _(act):
            st = Steps(act, steps["act"])
            for n, stage in enumerate(stages):
                stage.scalar(act, st)
                meet(act, n)

        @block.vector
        def _(dve):
            st = Steps(dve, steps["dve"])
            for n, stage in enumerate(stages):
                stage.vector(dve, st)
                meet(dve, n)

        @block.gpsimd
        def _(pool):
            st = Steps(pool, steps["pool"])
            for n, stage in enumerate(stages):
                stage.gpsimd(pool, st)
                pool.wait_ge(k.stage_done, 3 * (n + 1))


def kernel(**inputs):
    import concourse.bacc as bacc
    from concourse.bass_utils import run_bass_kernel_spmd as run

    I = {n: np.asarray(a) for n, a in inputs.items()}
    params, where_p = pack_params(I)
    consts, where_c = constants()
    arrays = {"x": I["x"], "stream": pack_stream(I), "params": params, "consts": consts,
              "narrow": pack_narrow(I), "mem": I["mem_2"]}
    arrays = {n: np.ascontiguousarray(a) for n, a in arrays.items()}
    nc = bacc.Bacc("TRN2", target_bir_lowering=False, num_devices=1)
    args = [nc.dram_tensor(n, a.shape, mybir.dt.from_np(a.dtype), kind="ExternalInput").ap()
            for n, a in arrays.items()]
    out = nc.dram_tensor("out", (1, TOK, D), F32, kind="ExternalOutput").ap()
    program(nc, *args, out, where_p, where_c)
    return run(nc, [arrays], core_ids=[0]).results[0]["out"]
```
